# Optimizing a Trainium2 kernel written in Bass

```python
import math
import jax, jax.numpy as jnp
from jax import lax
import numpy as np

D_MODEL = 1024
BATCH = 1
SEQ = 512
DEPTH = 2
DEC_BATCH = 8
DEC_SEQ = 1
PAST_LEN = 4096
PAGE_SIZE = 128

N_EVEN = (DEPTH + 1) // 2
N_ODD = DEPTH // 2
CHUNK = 64
CONV_W = 4
EPS = 1e-6

DN_HEADS = 4
DN_DK = 128
DN_DV = 128
DN_QK = DN_HEADS * DN_DK
DN_V = DN_HEADS * DN_DV
DN_CONV_DIM = 2 * DN_QK + DN_V

SSM_HEADS = 8
SSM_P = 64
SSM_INNER = SSM_HEADS * SSM_P
SSM_GROUPS = 2
SSM_N = 128
SSM_CONV_DIM = SSM_INNER + 2 * SSM_GROUPS * SSM_N

MIX_EVEN = DN_V + SSM_INNER
IN_EVEN = DN_CONV_DIM + 2 * DN_HEADS + DN_V + SSM_INNER + SSM_CONV_DIM + SSM_HEADS

GLA_HEADS = 4
GLA_DK = 128
GLA_DV = 256
GLA_K = GLA_HEADS * GLA_DK
GLA_V = GLA_HEADS * GLA_DV
GLA_LR = 16
GLA_NORMALIZER = 16.0
IN_ODD = 2 * GLA_K + 2 * GLA_V + GLA_LR

PEER_HEADS = 8
PEER_DQ = 256
PEER_NKEYS = 128
PEER_TOPK = 16
PEER_N = PEER_NKEYS * PEER_NKEYS
PEER_BLOCK = 256

kernel_name = "hybrid_gdn_ssd_gla_peer_step"

def rmsnorm(x, w):
    xf = x.astype(jnp.float32)
    y = xf * lax.rsqrt(jnp.mean(xf * xf, axis=-1, keepdims=True) + EPS)
    return (y * w.astype(jnp.float32)).astype(x.dtype)

def l2norm(x):
    xf = x.astype(jnp.float32)
    return xf * lax.rsqrt(jnp.sum(xf * xf, axis=-1, keepdims=True) + EPS)

def causal_conv(x, buf, w):
    xc = jnp.concatenate([buf.astype(x.dtype), x], axis=1)
    y = lax.conv_general_dilated(xc, w[:, None, :].astype(x.dtype), (1,), 'VALID',
                                 dimension_numbers=('NWC', 'WIO', 'NWC'),
                                 feature_group_count=x.shape[-1])
    return y, xc[:, -(CONV_W - 1):]

def to_chunks(x, c):
    b, L = x.shape[:2]
    nc = -(-L // c)
    x = jnp.pad(x, [(0, 0), (0, nc * c - L)] + [(0, 0)] * (x.ndim - 2))
    x = x.reshape((b, nc, c) + x.shape[2:])
    return jnp.swapaxes(jnp.swapaxes(x, 2, 3), 0, 1)

def from_chunks(x, L):
    x = jnp.swapaxes(jnp.swapaxes(x, 0, 1), 2, 3)
    b, nc, c = x.shape[:3]
    return x.reshape((b, nc * c) + x.shape[3:])[:, :L]

def gated_delta_rule(q, k, v, beta, g, s0):
    L = q.shape[1]
    dv = v.shape[-1]
    c = min(CHUNK, L)
    q, k, v, beta, g = (to_chunks(t, c) for t in (q, k, v, beta, g))
    gc = jnp.cumsum(g, axis=-1)
    causal = jnp.tril(jnp.ones((c, c), bool))
    strict = jnp.tril(jnp.ones((c, c), bool), -1)
    decay = jnp.exp(jnp.where(causal, gc[..., :, None] - gc[..., None, :], -jnp.inf))
    kb = k * beta[..., None]
    m = jnp.where(strict, jnp.einsum('nbhik,nbhjk->nbhij', kb, k) * decay, 0.0)
    rhs = jnp.concatenate([v * beta[..., None], kb * jnp.exp(gc)[..., None]], axis=-1)
    sol = lax.linalg.triangular_solve(m + jnp.eye(c, dtype=m.dtype), rhs, left_side=True,
                                      lower=True, unit_diagonal=True)
    u, w = sol[..., :dv], sol[..., dv:]
    qk = jnp.where(causal, jnp.einsum('nbhik,nbhjk->nbhij', q, k) * decay, 0.0)
    q_in = q * jnp.exp(gc)[..., None]
    k_out = k * jnp.exp(gc[..., -1:] - gc)[..., None]
    g_last = jnp.exp(gc[..., -1])[..., None, None]

    def step(s, xs):
        u_n, w_n, qk_n, qi_n, ko_n, gl_n = xs
        v_new = u_n - jnp.einsum('bhik,bhkv->bhiv', w_n, s)
        o = jnp.einsum('bhik,bhkv->bhiv', qi_n, s) + jnp.einsum('bhij,bhjv->bhiv', qk_n, v_new)
        s = s * gl_n + jnp.einsum('bhik,bhiv->bhkv', ko_n, v_new)
        return s, o

    s, o = lax.scan(step, s0, (u, w, qk, q_in, k_out, g_last))
    return from_chunks(o, L), s

def ssd_scan(x, dt, a, bm, cm, s0):
    L = x.shape[1]
    c = min(CHUNK, L)
    rep = x.shape[2] // bm.shape[2]
    bh = jnp.repeat(bm, rep, axis=2)
    ch = jnp.repeat(cm, rep, axis=2)
    x, dt, bh, ch = (to_chunks(t, c) for t in (x, dt, bh, ch))
    ac = jnp.cumsum(dt * a[:, None], axis=-1)
    causal = jnp.tril(jnp.ones((c, c), bool))
    decay = jnp.exp(jnp.where(causal, ac[..., :, None] - ac[..., None, :], -jnp.inf))
    xdt = x * dt[..., None]
    scores = jnp.einsum('nbhis,nbhjs->nbhij', ch, bh) * decay
    y_diag = jnp.einsum('nbhij,nbhjp->nbhip', scores, xdt)
    c_in = ch * jnp.exp(ac)[..., None]
    b_out = bh * jnp.exp(ac[..., -1:] - ac)[..., None]
    a_last = jnp.exp(ac[..., -1])[..., None, None]

    def step(s, xs):
        yd, ci, bo, xd, al = xs
        y = yd + jnp.einsum('bhis,bhps->bhip', ci, s)
        s = s * al + jnp.einsum('bhip,bhis->bhps', xd, bo)
        return s, y

    s, y = lax.scan(step, s0, (y_diag, c_in, b_out, xdt, a_last))
    return from_chunks(y, L), s

def gla_scan(q, k, v, gk, s0):
    L = q.shape[1]
    c = min(CHUNK, L)
    q, k, v, gk = (to_chunks(t, c) for t in (q, k, v, gk))
    bc = jnp.cumsum(gk, axis=-2)
    causal = jnp.tril(jnp.ones((c, c), bool))[:, :, None]

    def step(s, xs):
        q_n, k_n, v_n, b_n = xs
        o = jnp.einsum('bhik,bhkv->bhiv', q_n * jnp.exp(b_n), s)
        dec = jnp.exp(jnp.where(causal, b_n[..., :, None, :] - b_n[..., None, :, :], -jnp.inf))
        att = jnp.einsum('bhik,bhjk,bhijk->bhij', q_n, k_n, dec)
        o = o + jnp.einsum('bhij,bhjv->bhiv', att, v_n)
        b_last = b_n[..., -1, :]
        s = s * jnp.exp(b_last)[..., None] + jnp.einsum(
            'bhik,bhiv->bhkv', k_n * jnp.exp(b_last[..., None, :] - b_n), v_n)
        return s, o

    s, o = lax.scan(step, s0, (q, k, v, bc))
    return from_chunks(o, L), s

def even_mixer(h, conv_dn, s_dn, conv_ssm, s_ssm, w_in, w_out, dn_conv_w, dn_a_log,
               dn_dt_bias, dn_norm_w, ssm_conv_w, ssm_conv_b, ssm_a_log, ssm_dt_bias,
               ssm_d, ssm_norm_w):
    f32 = jnp.float32
    bsz, L, _ = h.shape
    proj = h @ w_in
    sizes = [DN_CONV_DIM, DN_HEADS, DN_HEADS, DN_V, SSM_INNER, SSM_CONV_DIM]
    dn_qkv, dn_a, dn_b, dn_gate, ssm_z, ssm_xbc, ssm_dt = jnp.split(
        proj, [int(s) for s in np.cumsum(sizes)], axis=-1)

    qkv_pre, new_conv_dn = causal_conv(dn_qkv, conv_dn, dn_conv_w)
    qkv = jax.nn.silu(qkv_pre.astype(f32))
    q, k, v = jnp.split(qkv, [DN_QK, 2 * DN_QK], axis=-1)
    q = l2norm(q.reshape(bsz, L, DN_HEADS, DN_DK)) * (DN_DK ** -0.5)
    k = l2norm(k.reshape(bsz, L, DN_HEADS, DN_DK))
    v = v.reshape(bsz, L, DN_HEADS, DN_DV)
    beta = jax.nn.sigmoid(dn_b.astype(f32))
    g = -jnp.exp(dn_a_log.astype(f32)) * jax.nn.softplus(dn_a.astype(f32) + dn_dt_bias.astype(f32))
    o_dn, s_dn_new = gated_delta_rule(q, k, v, beta, g, s_dn.astype(f32))
    o_dn = rmsnorm(o_dn, dn_norm_w) * jax.nn.silu(
        dn_gate.astype(f32).reshape(bsz, L, DN_HEADS, DN_DV))

    xbc_pre, new_conv_ssm = causal_conv(ssm_xbc, conv_ssm, ssm_conv_w)
    xbc = jax.nn.silu(xbc_pre.astype(f32) + ssm_conv_b.astype(f32))
    xs, bm, cm = jnp.split(xbc, [SSM_INNER, SSM_INNER + SSM_GROUPS * SSM_N], axis=-1)
    xs = xs.reshape(bsz, L, SSM_HEADS, SSM_P)
    bm = bm.reshape(bsz, L, SSM_GROUPS, SSM_N)
    cm = cm.reshape(bsz, L, SSM_GROUPS, SSM_N)
    dt = jax.nn.softplus(ssm_dt.astype(f32) + ssm_dt_bias.astype(f32))
    a = -jnp.exp(ssm_a_log.astype(f32))
    y, s_ssm_new = ssd_scan(xs, dt, a, bm, cm, s_ssm.astype(f32))
    y = (y + ssm_d.astype(f32)[:, None] * xs).reshape(bsz, L, SSM_INNER)
    y = y * jax.nn.silu(ssm_z.astype(f32))
    y = rmsnorm(y.reshape(bsz, L, SSM_GROUPS, SSM_INNER // SSM_GROUPS),
                ssm_norm_w.reshape(SSM_GROUPS, SSM_INNER // SSM_GROUPS)).reshape(bsz, L, SSM_INNER)

    mixed = jnp.concatenate([o_dn.reshape(bsz, L, DN_V), y], axis=-1).astype(h.dtype)
    out = mixed @ w_out
    return (out, new_conv_dn.astype(conv_dn.dtype), s_dn_new.astype(s_dn.dtype),
            new_conv_ssm.astype(conv_ssm.dtype), s_ssm_new.astype(s_ssm.dtype))

def odd_mixer(h, s_gla, w_in, w_gate2, b_gate, norm_w, w_out):
    f32 = jnp.float32
    bsz, L, _ = h.shape
    proj = h @ w_in
    q, k, v, glr, og = jnp.split(
        proj, [GLA_K, 2 * GLA_K, 2 * GLA_K + GLA_V, 2 * GLA_K + GLA_V + GLA_LR], axis=-1)
    q = q.astype(f32).reshape(bsz, L, GLA_HEADS, GLA_DK) * (GLA_DK ** -0.5)
    k = k.astype(f32).reshape(bsz, L, GLA_HEADS, GLA_DK)
    v = v.astype(f32).reshape(bsz, L, GLA_HEADS, GLA_DV)
    gk = jax.nn.log_sigmoid((glr @ w_gate2).astype(f32) + b_gate.astype(f32)) / GLA_NORMALIZER
    gk = gk.reshape(bsz, L, GLA_HEADS, GLA_DK)
    o, s_new = gla_scan(q, k, v, gk, s_gla.astype(f32))
    o = rmsnorm(o, norm_w) * jax.nn.silu(og.astype(f32).reshape(bsz, L, GLA_HEADS, GLA_DV))
    out = o.reshape(bsz, L, GLA_V).astype(h.dtype) @ w_out
    return out, s_new.astype(s_gla.dtype)

def peer_ffn(h, w_q, keys1, keys2, u_tab, v_tab):
    f32 = jnp.float32
    bsz, L, d = h.shape
    t = h.reshape(bsz * L, d)
    n_tok = bsz * L
    blk = min(PEER_BLOCK, n_tok)
    nb = -(-n_tok // blk)
    t = jnp.pad(t, ((0, nb * blk - n_tok), (0, 0))).reshape(nb, blk, d)
    half = PEER_DQ // 2

    def block(tb):
        q = (tb @ w_q).astype(f32).reshape(blk, PEER_HEADS, 2, half)
        s1 = jnp.einsum('thd,hnd->thn', q[:, :, 0], keys1.astype(f32))
        s2 = jnp.einsum('thd,hnd->thn', q[:, :, 1], keys2.astype(f32))
        v1, i1 = lax.top_k(s1, PEER_TOPK)
        v2, i2 = lax.top_k(s2, PEER_TOPK)
        cand = (v1[..., :, None] + v2[..., None, :]).reshape(blk, PEER_HEADS, PEER_TOPK * PEER_TOPK)
        cand_idx = (i1[..., :, None] * PEER_NKEYS + i2[..., None, :]).reshape(
            blk, PEER_HEADS, PEER_TOPK * PEER_TOPK)
        top_s, top_j = lax.top_k(cand, PEER_TOPK)
        expert = jnp.take_along_axis(cand_idx, top_j, axis=-1)
        gate = jax.nn.softmax(top_s, axis=-1)
        pre = jnp.einsum('thkd,td->thk', u_tab[expert], tb).astype(f32)
        act = (jax.nn.gelu(pre) * gate).astype(tb.dtype)
        return jnp.einsum('thk,thkd->td', act, v_tab[expert])

    out = lax.map(block, t).reshape(nb * blk, d)[:n_tok]
    return out.reshape(bsz, L, d)

def setup_inputs(seed: int = 0) -> dict:
    key = jax.random.key(seed)
    ks = iter(jax.random.split(key, 64))

    def nrm(shape, scale):
        return jax.random.normal(next(ks), shape, jnp.float32) * scale

    def a_log(shape):
        return jnp.log(jax.random.uniform(next(ks), shape, jnp.float32, 1.0, 16.0))

    def dt_bias(shape):
        dt = jnp.exp(jax.random.uniform(next(ks), shape, jnp.float32,
                                        math.log(1e-3), math.log(1e-1)))
        return dt + jnp.log(-jnp.expm1(-dt))

    d = D_MODEL
    return {
        "x_prompt": nrm((BATCH, SEQ, d), 1.0),
        "x_sample": nrm((DEC_BATCH, DEC_SEQ, d), 1.0),
        "state_dn_conv": nrm((N_EVEN, DEC_BATCH, CONV_W - 1, DN_CONV_DIM), 1.0),
        "state_dn": nrm((N_EVEN, DEC_BATCH, DN_HEADS, DN_DK, DN_DV), 0.5),
        "state_ssm_conv": nrm((N_EVEN, DEC_BATCH, CONV_W - 1, SSM_CONV_DIM), 1.0),
        "state_ssm": nrm((N_EVEN, DEC_BATCH, SSM_HEADS, SSM_P, SSM_N), 0.5),
        "state_gla": nrm((N_ODD, DEC_BATCH, GLA_HEADS, GLA_DK, GLA_DV), 0.5),
        "ln_mix": 1.0 + nrm((DEPTH, d), 0.01),
        "ln_ffn": 1.0 + nrm((DEPTH, d), 0.01),
        "ln_final": 1.0 + nrm((d,), 0.01),
        "w_in_even": nrm((N_EVEN, d, IN_EVEN), d ** -0.5),
        "w_out_even": nrm((N_EVEN, MIX_EVEN, d), MIX_EVEN ** -0.5),
        "dn_conv_w": nrm((N_EVEN, CONV_W, DN_CONV_DIM), CONV_W ** -0.5),
        "dn_a_log": a_log((N_EVEN, DN_HEADS)),
        "dn_dt_bias": dt_bias((N_EVEN, DN_HEADS)),
        "dn_norm_w": 1.0 + nrm((N_EVEN, DN_DV), 0.01),
        "ssm_conv_w": nrm((N_EVEN, CONV_W, SSM_CONV_DIM), CONV_W ** -0.5),
        "ssm_conv_b": nrm((N_EVEN, SSM_CONV_DIM), 0.02),
        "ssm_a_log": a_log((N_EVEN, SSM_HEADS)),
        "ssm_dt_bias": dt_bias((N_EVEN, SSM_HEADS)),
        "ssm_d": 1.0 + nrm((N_EVEN, SSM_HEADS), 0.1),
        "ssm_norm_w": 1.0 + nrm((N_EVEN, SSM_INNER), 0.01),
        "w_in_odd": nrm((N_ODD, d, IN_ODD), d ** -0.5),
        "gla_w_gate2": nrm((N_ODD, GLA_LR, GLA_K), GLA_LR ** -0.5),
        "gla_b_gate": nrm((N_ODD, GLA_K), 0.1),
        "gla_norm_w": 1.0 + nrm((N_ODD, GLA_DV), 0.01),
        "w_out_odd": nrm((N_ODD, GLA_V, d), GLA_V ** -0.5),
        "peer_w_q": nrm((DEPTH, d, PEER_HEADS * PEER_DQ), d ** -0.5),
        "peer_keys1": nrm((DEPTH, PEER_HEADS, PEER_NKEYS, PEER_DQ // 2), (PEER_DQ // 2) ** -0.5),
        "peer_keys2": nrm((DEPTH, PEER_HEADS, PEER_NKEYS, PEER_DQ // 2), (PEER_DQ // 2) ** -0.5),
        "peer_u": nrm((DEPTH, PEER_N, d), d ** -0.5),
        "peer_v": nrm((DEPTH, PEER_N, d), PEER_HEADS ** -0.5),
    }

def reference(x_prompt, x_sample, state_dn_conv, state_dn, state_ssm_conv, state_ssm, state_gla,
              ln_mix, ln_ffn, ln_final, w_in_even, w_out_even, dn_conv_w, dn_a_log, dn_dt_bias,
              dn_norm_w, ssm_conv_w, ssm_conv_b, ssm_a_log, ssm_dt_bias, ssm_d, ssm_norm_w,
              w_in_odd, gla_w_gate2, gla_b_gate, gla_norm_w, w_out_odd, peer_w_q, peer_keys1,
              peer_keys2, peer_u, peer_v):

    def trunk(x, conv_dn0, s_dn0, conv_ssm0, s_ssm0, s_gla0):
        conv_dn_l, s_dn_l, conv_ssm_l, s_ssm_l, s_gla_l = [], [], [], [], []
        for i in range(DEPTH):
            j = i // 2
            h = rmsnorm(x, ln_mix[i])
            if i % 2 == 0:
                o, cd, sd, cs, ss = even_mixer(
                    h, conv_dn0[j], s_dn0[j], conv_ssm0[j], s_ssm0[j], w_in_even[j],
                    w_out_even[j], dn_conv_w[j], dn_a_log[j], dn_dt_bias[j], dn_norm_w[j],
                    ssm_conv_w[j], ssm_conv_b[j], ssm_a_log[j], ssm_dt_bias[j], ssm_d[j],
                    ssm_norm_w[j])
                conv_dn_l.append(cd)
                s_dn_l.append(sd)
                conv_ssm_l.append(cs)
                s_ssm_l.append(ss)
            else:
                o, sg = odd_mixer(h, s_gla0[j], w_in_odd[j], gla_w_gate2[j], gla_b_gate[j],
                                  gla_norm_w[j], w_out_odd[j])
                s_gla_l.append(sg)
            x = x + o
            x = x + peer_ffn(rmsnorm(x, ln_ffn[i]), peer_w_q[i], peer_keys1[i], peer_keys2[i],
                             peer_u[i], peer_v[i])
        return (rmsnorm(x, ln_final), jnp.stack(conv_dn_l), jnp.stack(s_dn_l),
                jnp.stack(conv_ssm_l), jnp.stack(s_ssm_l), jnp.stack(s_gla_l))

    zc_dn = jnp.zeros((N_EVEN, BATCH) + state_dn_conv.shape[2:], state_dn_conv.dtype)
    zs_dn = jnp.zeros((N_EVEN, BATCH) + state_dn.shape[2:], state_dn.dtype)
    zc_ssm = jnp.zeros((N_EVEN, BATCH) + state_ssm_conv.shape[2:], state_ssm_conv.dtype)
    zs_ssm = jnp.zeros((N_EVEN, BATCH) + state_ssm.shape[2:], state_ssm.dtype)
    zs_gla = jnp.zeros((N_ODD, BATCH) + state_gla.shape[2:], state_gla.dtype)
    y_prompt, p_dn_conv, p_dn, p_ssm_conv, p_ssm, p_gla = trunk(
        x_prompt, zc_dn, zs_dn, zc_ssm, zs_ssm, zs_gla)

    y_sample, s_dn_conv, s_dn, s_ssm_conv, s_ssm, s_gla = trunk(
        x_sample, state_dn_conv, state_dn, state_ssm_conv, state_ssm, state_gla)

    return (y_prompt, y_sample, p_dn_conv, p_dn, p_ssm_conv, p_ssm, p_gla,
            s_dn_conv, s_dn, s_ssm_conv, s_ssm, s_gla)


_drawn_inputs = setup_inputs


def setup_inputs(seed=0):
    import zlib

    import numpy as np

    out = dict(_drawn_inputs(seed))
    spreads = {}
    factors = {}
    for name, (base, spread) in spreads.items():
        noise = np.random.default_rng([zlib.crc32(name.encode()), seed]).standard_normal(out[name].shape)
        drawn = base * np.exp(spread * noise) if base else spread * noise
        out[name] = __import__('jax').numpy.asarray(drawn.astype(out[name].dtype))
    for name, factor in factors.items():
        out[name] = (out[name] * factor).astype(out[name].dtype)
    return out
```

```python
import concourse.bass as bass
from concourse import mybir
from contextlib import ExitStack

P = 128
D = 1024
KD = D // P
NP_TOK = 512
NS_TOK = 8
T = NP_TOK + NS_TOK
TH = T // 2
GROUPS = NP_TOK // P
EPS = 1e-6
NKEY = 128
TOPK = 16
PH = 8
TILE = 104
NT = T // TILE
JG = 4
JQ = 32
QUARTERS = NKEY // JQ
GQ = JQ // JG
GT = 13
GSTEPS = T // GT
WSLOTS = 4
GEMMS = [("even_in", 28), ("even_out", 8), ("query0", 16), ("odd_in", 24), ("odd_out", 8), ("query1", 16)]
BLOCKS = dict(GEMMS)
BASE = {name: sum(b for _, b in GEMMS[:k]) for k, (name, _) in enumerate(GEMMS)}
NBLOCKS = sum(BLOCKS.values())
IDENT, ONES, CAUSAL, STRICT, LEVEL0 = 0, 1, 2, 3, 4
LEVELS = 7
GLAMASK = LEVEL0 + LEVELS
NMASK = GLAMASK + 1
GC = 32
BIG = 1e30
ARENA = 38224
NLOADS = 11


def build_program(nc, io):
    f32, f16, u32 = mybir.dt.float32, mybir.dt.float16, mybir.dt.uint32
    ALU = mybir.AluOpType
    ACT = mybir.ActivationFunctionType
    X = mybir.AxisListType.X
    ds = bass.ds

    with ExitStack() as ctx:
        def sb(name, shape, dt=f32):
            return ctx.enter_context(nc.sbuf_tensor(name, shape, dt))

        sems = {}

        def sem(name):
            if name not in sems:
                sems[name] = ctx.enter_context(nc.semaphore(name))
            return sems[name]

        xT = sb("xT", [P, KD, T])
        hT = sb("hT", [P, KD, T])
        wring = sb("wring", [P, WSLOTS, KD, P])
        masks = sb("masks", [P, NMASK, P])
        ln = sb("ln", [P, 5, KD])
        iota = sb("iota", [P, NKEY], f16)
        eps = sb("eps", [P, 4])
        conv_w = sb("conv_w", [P, 20, 4])
        conv_b = sb("conv_b", [P, 20])
        small_w = sb("small_w", [P, KD, 16])
        glr_w = sb("glr_w", [P, KD, 16])
        small_b = sb("small_b", [P, 16])
        a_log = sb("a_log", [P, 12])
        head_w = sb("head_w", [P, 16])
        gate2 = sb("gate2", [16, 512])
        arena = sb("arena", [P, ARENA])
        ps = ctx.enter_context(nc.psum_tensor("ps", [P, 8, 512], f32))
        ident = masks[:, IDENT, :]
        ones = masks[:, ONES, :]
        causal = masks[:, CAUSAL, :]

        def mask4(k):
            return masks[:, k:k + 1, :].to_broadcast([P, 4, P])

        class Region:

            def __init__(self, at, end=ARENA):
                self.at, self.end = at, end

            def take(self, *shape, dt=f32):
                n = 1
                for x in shape:
                    n *= x
                words = n // 2 if dt == f16 else n
                v = arena[:, self.at:self.at + words]
                self.at += words
                assert self.at <= self.end, (self.at, self.end)
                if dt != f32:
                    v = v.bitcast(dt)
                if len(shape) == 2:
                    v = v.rearrange("p (a b) -> p a b", a=shape[0])
                if len(shape) == 3:
                    v = v.rearrange("p (a b c) -> p a b c", a=shape[0], b=shape[1])
                return v

        def both(bank, rows=P):
            return ps[0:rows, bank:bank + 2, 0:TH]

        def split(v):
            return v.rearrange("p (b t) -> p b t", b=2)

        def bank4(bank):
            return ps[:, bank, :].rearrange("p (h i) -> p h i", h=4)

        ev = Region(0)
        proj = ev.take(28, T)
        conv = ev.take(20, T)
        sq4 = ev.take(4, T)
        g_raw = ev.take(5, 16)
        g_abs = ev.take(5, 16)
        g_sp = ev.take(5, 16)
        g12 = ev.take(5, 12)
        beta = ev.take(5, 4)
        neg_a = ev.take(12)
        s_dn = ev.take(4, P)
        s_ssm = ev.take(512)
        buf_c = ev.take(3, 20, NS_TOK)
        new_c = ev.take(3, 20, NS_TOK)
        acc_c = ev.take(20, NS_TOK)
        tmp_c = ev.take(20, NS_TOK)
        tail_c = ev.take(3, 20)
        (kb, nmat, qkt, kbt, kout, vb, pmat, xmat, vt, wt, vn, qi, xd, xo) = [ev.take(4, P) for _ in range(14)]
        ci = ev.take(8, P)
        xd8, xo8 = [v.rearrange("p b (a c) -> p (b a) c", a=2) for v in (xd, xo)]
        sc = Region(0, 20 * T)
        w_sl = sc.take(20, P)
        g_sl = sc.take(12)
        b_sl = sc.take(4)
        d_sl = sc.take(8)
        gct = sc.take(12)
        egc = sc.take(12)
        dec = sc.take(12, P)
        erow = sc.take(12, P)
        nl = sc.take(6, 512)
        btk = sc.take(2, P)
        att = sc.take(8, P)
        b_e = sc.take(4)
        sm = Region(0, 20 * T)
        sm_dn = sm.take(32, P)
        sm_ssm = sm.take(NS_TOK, 512)
        sm_r = sm.take(4, NS_TOK)
        sm_xd = sm.take(4, NS_TOK)
        sm_val = sm.take(24)
        sm_diag = sm.take(NS_TOK, 24)
        sm_bc = sm.take(NS_TOK, 24)

        od = Region(0)
        oproj = od.take(24, T)
        glrT = od.take(T)
        gk = od.take(GROUPS, 512)
        gk2 = od.take(GROUPS, 512)
        gbias = od.take(512)
        s_gla = od.take(4, 256)
        o_sl = od.take(16, P)
        gk_sl = od.take(512)
        (bt, dm, dl, e_q, e_k, e_b, kc, ko, gatt) = [od.take(4, P) for _ in range(9)]
        (qt, kt, qb) = [od.take(4, P) for _ in range(3)]
        vtok = od.take(8, P)
        sm_gla = od.take(32, 256)
        sm_a = od.take(4, NS_TOK)
        sm_a2 = od.take(4, NS_TOK)
        sm_q = od.take(4, NS_TOK)
        osq = Region(0, 16 * T)
        o_sq = osq.take(8, T)
        o_r = osq.take(4, T)

        nm = Region(0)
        nsq = nm.take(KD, T)
        nrt = nm.take(T)

        pr = Region(0)
        uring = pr.take(2, JG * KD, P)
        vring = pr.take(2, JG, D)
        g0 = pr.at
        gates = pr.take(JQ, T)
        a0 = pr.at
        aring = pr.take(2, JG, T)
        a1 = pr.at
        idx1T = pr.take(T, dt=f16)
        idx2T = pr.take(T, dt=f16)
        ghiT = pr.take(T, dt=f16)
        gloT = pr.take(T, dt=f16)
        hot = Region(a0, a1)
        hot_i = hot.take(4, GT * NKEY, dt=f16).rearrange("p s (t i) -> p s t i", t=GT)
        hot_j = hot.take(4, GT * JQ, dt=f16).rearrange("p s (t j) -> p s t j", t=GT)
        tk = Region(g0, a0)
        query = tk.take(2 * PH, T)
        score = tk.take(2 * PH, NKEY)
        cand = tk.take(PH, TOPK * TOPK)
        eq = tk.take(PH * TOPK, TOPK)
        work = tk.take(256)
        topv = tk.take(2 * PH, TOPK)
        topi = tk.take(2 * PH, TOPK, dt=u32)
        topf = tk.take(2 * PH, TOPK)
        tk2 = Region(a0, a1)
        keys = tk2.take(2 * PH, NKEY)
        bests = tk2.take(PH, TOPK)
        bestj = tk2.take(PH, TOPK, dt=u32)
        posu = tk2.take(PH, TOPK, dt=u32)
        posf = tk2.take(PH, TOPK)
        res = tk2.take(3, P)
        ssum = tk2.take(PH)
        gfull = tk2.take(TILE)
        iota16 = tk2.take(TOPK)

        block = ctx.enter_context(nc.Block())

        @block.sync
        def _(sp):
            n = 0
            for dst, src in ((masks[:, :, :], io["masks"]), (xT[:, :, :], io["xT"]), (ln[:, :, :], io["ln"]),
                             (conv_w[:, :, :], io["conv_w"]), (conv_b[:, :], io["conv_b"]),
                             (small_w[:, :, :], io["small_w"]), (glr_w[:, :, :], io["glr_w"]),
                             (head_w[:, :], io["head_w"]), (gate2[:, :], io["gate2"]),
                             (small_b[:, :], io["small_b"].to_broadcast([P, 16])),
                             (a_log[:, :], io["a_log"].to_broadcast([P, 12]))):
                sp.dma_start(dst, src).then_inc(sem("params"), 16)
                n += 1
            assert n == NLOADS

            def load_block(i, u, base):
                sp.dma_start(wring[:, u, :, :].rearrange("p k c -> p (k c)"),
                             io["weights"][ds(WSLOTS * i + (base + u), 1)].rearrange("a p c -> (a p) c"))\
                    .then_inc(sem(f"w_loaded{u}"), 16)

            def stream(name):
                base = BASE[name]
                if base == 0:
                    for u in range(WSLOTS):
                        load_block(0, u, 0)
                with sp.Fori(int(base == 0), BLOCKS[name] // WSLOTS) as i:
                    for u in range(WSLOTS):
                        sp.wait_ge(sem("gemm_done"), WSLOTS * i + (base + u - WSLOTS + 1))
                        load_block(i, u, base)

            def experts(L):
                def load(what, ring, slot, g):
                    sp.dma_start(ring[:, slot].rearrange("p a b -> p (a b)"),
                                 io[what][L][ds(g, 1)].rearrange("a p c -> (a p) c"))\
                        .then_inc(sem(f"{what}_loaded{slot}"), 16)
                sp.wait_ge(sem("h_ready"), 2 * L + 2)
                for slot in range(2):
                    load("u", uring, slot, slot)
                    load("v", vring, slot, slot)
                with sp.Fori(1, QUARTERS * GQ // 2) as m:
                    for slot in range(2):
                        sp.wait_ge(sem("pre_done"), m * (2 * JG) + (JG * (slot - 1) + L * NKEY))
                        load("u", uring, slot, 2 * m + slot)
                        sp.wait_ge(sem("y_done"), m * (2 * KD) + (KD * (slot - 1) + L * KD * QUARTERS * GQ))
                        load("v", vring, slot, 2 * m + slot)

            stream("even_in")
            stream("even_out")
            stream("query0")
            experts(0)
            stream("odd_in")
            stream("odd_out")
            stream("query1")
            experts(1)

        @block.gpsimd
        def _(pool):
            pool.iota(iota[:, :], pattern=[[1, NKEY]], base=0, channel_multiplier=0,
                      allow_small_or_imprecise_dtypes=True).then_inc(sem("iota_ready"), 1)
            pool.dma_start(buf_c, io["conv_buf"]).then_inc(sem("buf_loaded"), 16)
            pool.wait_ge(sem("conv_done"), 21)
            pool.dma_start(io["o_conv_s"], new_c).then_inc(sem("stored"), 16)
            pool.dma_start(io["o_conv_p"], tail_c).then_inc(sem("stored"), 16)
            with pool.Fori(0, GROUPS) as g:
                pool.wait_ge(sem("n_ready"), g + 1)
                for l in range(1, LEVELS):
                    pool.tensor_tensor(nl[:, l - 1, :].rearrange("p (h i) -> p h i", h=4), nmat, mask4(LEVEL0 + l),
                                       ALU.mult).then_inc(sem("nl_ready"), 1)
            pool.wait_ge(sem("even_group"), GROUPS + 1)
            pool.dma_start(io["o_dn"][:, 0, :], s_dn.rearrange("p h d -> p (h d)")).then_inc(sem("stored"), 16)
            pool.dma_start(io["o_ssm"][:, 0, :], s_ssm).then_inc(sem("stored"), 16)
            pool.dma_start(sm_dn.rearrange("p a d -> p (a d)"), io["s_dn"]).then_inc(sem("even_states"), 16)
            pool.dma_start(sm_ssm.rearrange("p a d -> p (a d)"), io["s_ssm"]).then_inc(sem("even_states"), 16)
            pool.wait_ge(sem("even_sample"), 1)
            pool.dma_start(io["o_dn"][:, 1:9, :], sm_dn.rearrange("p (b h) d -> p b (h d)", b=NS_TOK))\
                .then_inc(sem("even_stored"), 16)
            pool.dma_start(io["o_ssm"][:, 1:9, :], sm_ssm).then_inc(sem("even_stored"), 16)

            def peer(L):
                pool.wait_ge(sem("h_ready"), 2 * L + 2)
                pool.dma_start(keys, io["keys"][L]).then_inc(sem("keys_loaded"), 16)
                with pool.Fori(0, QUARTERS) as q:
                    with pool.Fori(0, GSTEPS // 2) as i:
                        for s in range(2):
                            pool.wait_ge(sem("hot_eq_ready"), q * GSTEPS + 2 * i + (L * QUARTERS * GSTEPS + s + 1))
                            at = ds(2 * GT * i + GT * s, GT)
                            hi, lo = hot_j[:, 2 * s], hot_j[:, 2 * s + 1]

                            def col(v):
                                return v[:, at].rearrange("p (t a) -> p t a", a=1).to_broadcast([P, GT, JQ])
                            pool.tensor_tensor(hi, lo, col(ghiT), ALU.mult)
                            pool.drain()
                            pool.tensor_tensor(lo, lo, col(gloT), ALU.mult).then_inc(sem("hot_j_ready"), 1)

            peer(0)
            pool.wait_ge(sem("h_ready"), 3)
            pool.dma_start(gbias, io["gbias"].to_broadcast([P, 512])).then_inc(sem("odd_loads"), 16)
            pool.dma_start(sm_gla.rearrange("p a d -> p (a d)"), io["s_gla"]).then_inc(sem("odd_states"), 16)
            pool.wait_ge(sem("odd_group"), GROUPS + 1)
            pool.dma_start(io["o_gla"][:, 0, :], s_gla.rearrange("p h d -> p (h d)")).then_inc(sem("odd_stored"), 16)
            pool.wait_ge(sem("odd_sample"), 1)
            pool.dma_start(io["o_gla"][:, 1:9, :], sm_gla.rearrange("p (b h) d -> p b (h d)", b=NS_TOK))\
                .then_inc(sem("odd_stored"), 16)
            peer(1)
            pool.wait_ge(sem("h_ready"), 5)
            pool.dma_start(io["o_y"], hT[:, :, :]).then_inc(sem("stored"), 16)
            pool.wait_ge(sem("stored"), 16 * 5)
            pool.wait_ge(sem("even_stored"), 32)
            pool.wait_ge(sem("odd_stored"), 32)

        @block.tensor
        def _(pe):
            def mm(out, lhsT, rhs, start=True, stop=True):
                return pe.matmul(out, lhsT, rhs, start=start, stop=stop)

            def norm(k):
                pe.wait_ge(sem("squares_ready"), k + 1)
                for h in range(2):
                    for c in range(KD):
                        last = mm(ps[:, h, 0:TH], ones, nsq[:, c, h * TH:(h + 1) * TH], c == 0, c == KD - 1)
                last.then_inc(sem("ssq_ready"), 1)

            def gemm(name):
                base = BASE[name]
                with pe.Fori(0, BLOCKS[name] // WSLOTS) as i:
                    for u in range(WSLOTS):
                        pe.wait_ge(sem(f"w_loaded{u}"), i * 16 + 16 * (base // WSLOTS + 1))
                        pe.wait_ge(sem("gemm_free"), WSLOTS * i + (base + u + 1))
                        for h in range(2):
                            for c in range(KD):
                                last = mm(ps[:, 2 * (u % 2) + h, 0:TH], wring[:, u, c, :],
                                          hT[:, c, h * TH:(h + 1) * TH], c == 0, c == KD - 1)
                        last.then_inc(sem("gemm_done"), 1)

            def root_sums(count, nblocks, per):
                pe.wait_ge(sem("sq4_ready"), count)
                for b in range(nblocks // per):
                    for h in range(2):
                        for k in range(per):
                            last = mm(ps[:, 2 * b + h, 0:TH], ones, sq_src[0][:, b * per + k, h * TH:(h + 1) * TH],
                                      k == 0, k == per - 1)
                last.then_inc(sem("sums4_ready"), 1)

            sq_src = [sq4]

            pe.wait_ge(sem("params"), 16 * NLOADS)
            norm(0)
            pe.wait_ge(sem("h_ready"), 1)
            gemm("even_in")

            pe.wait_ge(sem("gemm_free"), BASE["even_out"] + 2)
            for n in range(5):
                rows = P if n < 4 else NS_TOK
                for c in range(KD):
                    last = mm(ps[0:rows, 0, 16 * n:16 * n + 16], hT[:, c, n * P:n * P + rows], small_w[:, c, :],
                              c == 0, c == KD - 1)
            last.then_inc(sem("gates_mm"), 1)

            pe.wait_ge(sem("gates_read"), 1)
            root_sums(1, 4, 1)
            root_sums(2, 4, 1)

            with pe.Fori(0, GROUPS) as g:
                def at(name, per=1, k=1):
                    pe.wait_ge(sem(name), g * per + k)
                at("gates_cut")
                for h in range(12):
                    mm(ps[:, h // 4, (h % 4) * P:(h % 4 + 1) * P], g_sl[:, h:h + 1].to_broadcast([P, P]), causal)
                mm(ps[:, 3, 0:12], causal, g_sl)
                for h in range(4):
                    last = mm(ps[:, 4, h * P:(h + 1) * P], b_sl[:, h:h + 1].to_broadcast([P, P]), ident)
                last.then_inc(sem("rows_ready"), 1)
                at("kb_ready")
                for h in range(4):
                    mm(ps[:, 5, h * P:(h + 1) * P], w_sl[:, 4 + h, :], kb[:, h, :])
                for h in range(4):
                    mm(ps[:, 6, h * P:(h + 1) * P], w_sl[:, 4 + h, :], w_sl[:, h, :])
                for h in range(4):
                    pe.transpose(ps[:, 7, h * P:(h + 1) * P], w_sl[:, 4 + h, :], ident)
                for h in range(4):
                    last = pe.transpose(ps[:, 0, h * P:(h + 1) * P], w_sl[:, 8 + h, :], ident)
                last.then_inc(sem("kk_ready"), 1)
                for j in range(2):
                    mm(ps[:, 1, j * P:(j + 1) * P], w_sl[:, 16 + j, :], w_sl[:, 18 + j, :])
                for b in range(4):
                    pe.transpose(ps[:, 2, b * P:(b + 1) * P], w_sl[:, 12 + b, :], ident)
                for j in range(2):
                    last = pe.transpose(ps[:, 3, j * P:(j + 1) * P], w_sl[:, 16 + j, :], ident)
                last.then_inc(sem("ssm_mm"), 1)
                at("p0_ready")
                for h in range(4):
                    last = pe.transpose(ps[:, 5, h * P:(h + 1) * P], pmat[:, h, :], ident)
                last.then_inc(sem("x0_ready"), 1)
                for l in range(1, LEVELS):
                    at("px_ready", LEVELS, l)
                    at("nl_ready", LEVELS - 1, l)
                    for h in range(4):
                        last = mm(ps[:, 6, h * P:(h + 1) * P], nl[:, l - 1, h * P:(h + 1) * P], xmat[:, h, :])
                    last.then_inc(sem("vt_mm"), 1)
                    at("vt_ready", LEVELS - 1, l)
                    for h in range(4):
                        last = mm(ps[:, 7, h * P:(h + 1) * P], vt[:, h, :], pmat[:, h, :])
                    if l < LEVELS - 1:
                        for h in range(4):
                            last = mm(ps[:, 0, h * P:(h + 1) * P], pmat[:, h, :], vt[:, h, :])
                    last.then_inc(sem("z_mm"), 1)
                at("px_ready", LEVELS, LEVELS)
                for h in range(4):
                    last = mm(ps[:, 5, h * P:(h + 1) * P], kbt[:, h, :], pmat[:, h, :])
                last.then_inc(sem("wt_mm"), 1)
                at("wt_ready")
                for h in range(4):
                    mm(ps[:, 6, h * P:(h + 1) * P], pmat[:, h, :], vb[:, h, :], True, False)
                    last = mm(ps[:, 6, h * P:(h + 1) * P], wt[:, h, :], s_dn[:, h, :], False, True)
                last.then_inc(sem("vn_mm"), 1)
                at("vn_ready")
                for h in range(4):
                    mm(ps[:, 7, h * P:(h + 1) * P], s_dn[:, h, :], qi[:, h, :], True, False)
                    mm(ps[:, 7, h * P:(h + 1) * P], vn[:, h, :], qkt[:, h, :], False, True)
                for h in range(4):
                    last = mm(ps[:, 0, h * P:(h + 1) * P], kout[:, h, :], vn[:, h, :])
                last.then_inc(sem("o_mm"), 1)
                at("att_ready")
                for h in range(8):
                    out = ps[64 * (h % 2):64 * (h % 2) + 64, 4, (h // 2) * P:(h // 2 + 1) * P]
                    mm(out, xd[:, h // 2, 64 * (h % 2):64 * (h % 2) + 64], att[:, h, :], True, False)
                    mm(out, s_ssm[:, 64 * h:64 * h + 64], ci[:, h, :], False, True)
                for j in range(2):
                    last = mm(ps[:, 5, j * 256:(j + 1) * 256], btk[:, j, :],
                              xo[:, 2 * j:2 * j + 2, :].rearrange("p a b -> p (a b)"))
                last.then_inc(sem("ssm_out_mm"), 1)

            pe.wait_ge(sem("even_group"), GROUPS + 1)
            pe.wait_ge(sem("diag_ready"), 1)
            mm(ps[:, 0, 0:192], ones[0:NS_TOK, :], sm_diag[0:NS_TOK, :, :].rearrange("p b c -> p (b c)"))\
                .then_inc(sem("bc_mm"), 1)
            pe.wait_ge(sem("even_states"), 32)
            for h in range(4):
                for b in range(NS_TOK):
                    last = mm(ps[:, 1, h * 8 + b:h * 8 + b + 1], sm_dn[:, b * 4 + h, :],
                              conv[:, 4 + h, NP_TOK + b:NP_TOK + b + 1])
            last.then_inc(sem("r_mm"), 1)
            pe.wait_ge(sem("delta_ready"), 1)
            for b in range(NS_TOK):
                for h in range(4):
                    last = mm(ps[:, b, h * P:(h + 1) * P], sm_r[:, h, b:b + 1].to_broadcast([P, P]), ident)
                last.then_inc(sem("delta_rows"), 1)
            pe.wait_ge(sem("dn_states_new"), 1)
            for h in range(4):
                for b in range(NS_TOK):
                    last = mm(ps[:, 0, h * 8 + b:h * 8 + b + 1], sm_dn[:, b * 4 + h, :],
                              conv[:, h, NP_TOK + b:NP_TOK + b + 1])
            last.then_inc(sem("sm_o_mm"), 1)
            pe.wait_ge(sem("sm_o_read"), 1)
            for b in range(NS_TOK):
                for k in range(4):
                    last = mm(ps[:, b, k * P:(k + 1) * P], sm_xd[:, k, b:b + 1].to_broadcast([P, P]), ident)
                last.then_inc(sem("x_rows"), 1)
            pe.wait_ge(sem("ssm_states_new"), 1)
            for k in range(4):
                for b in range(NS_TOK):
                    last = mm(ps[:, 0, k * 8 + b:k * 8 + b + 1], sm_ssm[:, b, k * P:(k + 1) * P],
                              conv[:, 18 + k // 2, NP_TOK + b:NP_TOK + b + 1])
            last.then_inc(sem("sm_y_mm"), 1)

            root_sums(3, 4, 1)
            root_sums(4, 4, 2)
            pe.wait_ge(sem("mix_ready"), 1)
            gemm("even_out")

            def retrieval(L):
                pe.wait_ge(sem("gemm_free"), BASE[f"query{L}"] + BLOCKS[f"query{L}"] + 2)
                pe.wait_ge(sem("keys_loaded"), 16 * (L + 1))
                for n in range(NT):
                    pe.wait_ge(sem("score_free"), L * NT + n + 1)
                    for k in range(2 * PH):
                        last = mm(ps[0:TILE, k // 4, (k % 4) * P:(k % 4 + 1) * P],
                                  query[:, k, n * TILE:(n + 1) * TILE], keys[:, k, :])
                    last.then_inc(sem("score_mm"), 1)
                    if n:
                        chosen(L, n - 1)
                chosen(L, NT - 1)

            def chosen(L, n):
                pe.wait_ge(sem("chosen"), L * NT + n + 1)
                for k in range(3):
                    last = pe.transpose(ps[:, 4, k * TILE:(k + 1) * TILE], res[0:TILE, k, :], ident[0:TILE, 0:TILE])
                last.then_inc(sem("chosen_mm"), 1)

            def experts(L):
                def pre(slot, g, q):
                    pe.wait_ge(sem(f"u_loaded{slot}"), q * (16 * GQ // 2) + g * 16 + (16 * (L * QUARTERS * GQ // 2 + 1)))
                    for j in range(JG):
                        pe.wait_ge(sem("pre_free"), q * JQ + g * (2 * JG) + (slot * JG + L * NKEY + j + 1))
                        for h in range(2):
                            for c in range(KD):
                                last = mm(ps[:, 2 * (j % 2) + h, 0:TH], uring[:, slot, j * KD + c, :],
                                          hT[:, c, h * TH:(h + 1) * TH], c == 0, c == KD - 1)
                        last.then_inc(sem("pre_done"), 1)

                def out(slot, g, q):
                    pe.wait_ge(sem(f"v_loaded{slot}"), q * (16 * GQ // 2) + g * 16 + (16 * (L * QUARTERS * GQ // 2 + 1)))
                    pe.wait_ge(sem("act_ready"), q * JQ + g * (2 * JG) + (slot * JG + L * NKEY + JG))
                    for c in range(KD):
                        pe.wait_ge(sem("y_free"), q * (KD * GQ) + g * (2 * KD) + (slot * KD + L * KD * QUARTERS * GQ + c + 1))
                        for h in range(2):
                            for j in range(JG):
                                last = mm(ps[:, 4 + 2 * (c % 2) + h, 0:TH], vring[:, slot, j, c * P:(c + 1) * P],
                                          aring[:, slot, j, h * TH:(h + 1) * TH], j == 0, j == JG - 1)
                        last.then_inc(sem("y_done"), 1)

                with pe.Fori(0, QUARTERS) as q:
                    with pe.Fori(0, GSTEPS // 4) as i:
                        for s in range(4):
                            n = q * GSTEPS + 4 * i + (L * QUARTERS * GSTEPS + s + 1)
                            pe.wait_ge(sem("hot_i_ready"), n)
                            pe.wait_ge(sem("hot_j_ready"), n)
                            pe.wait_ge(sem("gate_free"), n)
                            for t in range(GT):
                                o = ps[:, s, t * JQ:(t + 1) * JQ]
                                mm(o, hot_i[:, s, t, :], hot_j[:, 2 * (s % 2), t, :], True, False)
                                last = mm(o, hot_i[:, s, t, :], hot_j[:, 2 * (s % 2) + 1, t, :], False, True)
                            last.then_inc(sem("gate_mm"), 1)
                    pe.wait_ge(sem("gate_free"), q * GSTEPS + (L * QUARTERS * GSTEPS + GSTEPS + 4))
                    pre(0, 0, q)
                    with pe.Fori(0, GQ // 2 - 1) as m:
                        pre(1, m, q)
                        out(0, m, q)
                        pre(0, m + 1, q)
                        out(1, m, q)
                    pre(1, GQ // 2 - 1, q)
                    out(0, GQ // 2 - 1, q)
                    out(1, GQ // 2 - 1, q)

            def peer(L):
                norm(2 * L + 1)
                pe.wait_ge(sem("h_ready"), 2 * L + 2)
                gemm(f"query{L}")
                retrieval(L)
                experts(L)

            pe.sem_inc(sem("gate_mm"), 4)
            peer(0)
            norm(2)
            pe.wait_ge(sem("h_ready"), 3)
            gemm("odd_in")

            pe.wait_ge(sem("gemm_free"), BASE["odd_out"] + 2)
            for h in range(2):
                for c in range(KD):
                    last = mm(ps[0:16, h, 0:TH], glr_w[:, c, :], hT[:, c, h * TH:(h + 1) * TH], c == 0, c == KD - 1)
            last.then_inc(sem("glr_mm"), 1)
            pe.wait_ge(sem("glr_ready"), 1)
            for n in range(GROUPS):
                last = mm(ps[:, 4 + n, :], glrT[0:16, n * P:(n + 1) * P], gate2[:, :])
            last.then_inc(sem("gk_mm"), 1)
            for h in range(4):
                last = mm(ps[:, 2, h * 8:(h + 1) * 8], gate2[:, h * P:(h + 1) * P], glrT[0:16, NP_TOK:T])
            last.then_inc(sem("gk_sample_mm"), 1)

            with pe.Fori(0, GROUPS) as g:
                def at(name, per=1, k=1):
                    pe.wait_ge(sem(name), g * per + k)
                at("odd_cut")
                for h in range(4):
                    last = mm(ps[:, 0, h * P:(h + 1) * P], gk_sl[:, h * P:(h + 1) * P], masks[:, GLAMASK, :])
                last.then_inc(sem("bt_mm"), 1)
                for b in range(8):
                    last = pe.transpose(ps[:, 2 + b // 4, (b % 4) * P:(b % 4 + 1) * P], o_sl[:, 8 + b, :], ident)
                last.then_inc(sem("v_mm"), 1)
                at("qk_ready")
                for h in range(4):
                    mm(ps[:, 1, h * P:(h + 1) * P], kt[:, h, :], qt[:, h, :])
                for h in range(4):
                    last = pe.transpose(ps[:, 4, h * P:(h + 1) * P], kc[:, h, :], ident)
                last.then_inc(sem("gatt_mm"), 1)
                at("gatt_ready")
                at("vtok_ready")
                for b in range(8):
                    last = mm(ps[:, 5 + b // 4, (b % 4) * P:(b % 4 + 1) * P], vtok[:, b, :], gatt[:, b // 2, :])
                last.then_inc(sem("intra_mm"), 1)
                at("intra_read")
                for c in range(P // GC):
                    at("s_ready", P // GC, c + 1)
                    for h in range(4):
                        mm(ps[:, 2 + 2 * (c % 2) + h // 2, (h % 2) * 256:(h % 2) * 256 + 256],
                           ko[c * GC:(c + 1) * GC, h, :],
                           vtok[c * GC:(c + 1) * GC, 2 * h:2 * h + 2, :].rearrange("p a b -> p (a b)"))
                    for b in range(8):
                        last = mm(ps[:, 6 + b // 4, (b % 4) * P + c * GC:(b % 4) * P + (c + 1) * GC],
                                  s_gla[:, b // 2, (b % 2) * P:(b % 2 + 1) * P],
                                  qb[:, b // 2, c * GC:(c + 1) * GC])
                    last.then_inc(sem("inter_mm"), 1)

            pe.wait_ge(sem("odd_group"), GROUPS + 1)
            for r in range(2):
                pe.wait_ge(sem("gla_rows_read"), r + 1)
                for b in range(4):
                    for h in range(4):
                        for k in range(2):
                            o = (h * 2 + k) * P
                            last = mm(ps[:, 2 * b + o // 512, o % 512:o % 512 + P],
                                      oproj[:, 8 + 2 * h + k, NP_TOK + 4 * r + b:NP_TOK + 4 * r + b + 1].to_broadcast([P, P]),
                                      ident)
                last.then_inc(sem("gla_rows"), 1)
            pe.wait_ge(sem("gla_states_new"), 1)
            for b in range(NS_TOK):
                for k in range(8):
                    last = mm(ps[:, 0, k * 8 + b:k * 8 + b + 1],
                              sm_gla[:, b * 4 + k // 2, (k % 2) * P:(k % 2 + 1) * P], sm_q[:, k // 2, b:b + 1])
            last.then_inc(sem("gla_o_mm"), 1)
            sq_src[0] = o_sq
            root_sums(5, 8, 2)
            pe.wait_ge(sem("mix_ready"), 2)
            gemm("odd_out")
            peer(1)
            norm(4)

        @block.scalar
        def _(act):
            def f(out, in_, func, **k):
                return act.activation(out, in_, func, **k)

            def norm(k):
                if k:
                    act.wait_ge(sem("x_ready"), k)
                f(nsq, xT[:, :, :], ACT.Square).then_inc(sem("squares_ready"), 1)
                act.wait_ge(sem("ssq_ready"), k + 1)
                f(split(nrt), both(0), ACT.Sqrt, scale=1.0 / D, bias=eps[:, 0:1]).then_inc(sem("root_ready"), 1)

            def copies(name, dst):
                base = BASE[name]
                with act.Fori(0, BLOCKS[name] // WSLOTS) as i:
                    for u in range(WSLOTS):
                        act.wait_ge(sem("gemm_done"), WSLOTS * i + (base + u + 1))
                        f(dst[:, ds(WSLOTS * i + u, 1), :].rearrange("p a (b t) -> p (a b) t", b=2),
                          both(2 * (u % 2)), ACT.Copy).then_inc(sem("gemm_free"), 1)

            act.wait_ge(sem("params"), 16 * NLOADS)
            act.wait_ge(sem("eps_ready"), 1)
            act.sem_inc(sem("gemm_free"), 2)
            act.sem_inc(sem("gate_free"), 4)
            act.sem_inc(sem("pre_free"), 2)
            act.sem_inc(sem("score_free"), 1)
            norm(0)
            copies("even_in", proj)
            act.wait_ge(sem("gates_abs"), 1)
            f(g_abs, g_abs, ACT.Exp, scale=-1.0).then_inc(sem("act_gates"), 1)
            act.wait_ge(sem("act_gates"), 1)
            f(g_abs, g_abs, ACT.Ln, bias=eps[:, 2:3]).then_inc(sem("act_gates"), 1)
            f(neg_a, a_log[:, :], ACT.Exp).then_inc(sem("act_gates"), 1)
            f(beta, g_raw[:, :, 12:16], ACT.Sigmoid).then_inc(sem("act_gates"), 1)
            f(proj[:, 20:28, :], proj[:, 20:28, :], ACT.Silu).then_inc(sem("gates_silu"), 1)
            act.wait_ge(sem("conv_done"), 21)
            f(conv, conv, ACT.Silu).then_inc(sem("conv_silu"), 1)
            act.wait_ge(sem("conv_silu"), 1)
            for r in range(2):
                if r:
                    act.wait_ge(sem("l2_done"), r)
                f(sq4, conv[:, 4 * r:4 * r + 4, :], ACT.Square).then_inc(sem("sq4_ready"), 1)
                act.wait_ge(sem("sums4_ready"), r + 1)
                f(sq4.rearrange("p a (b t) -> p (a b) t", b=2), ps[:, :, 0:TH], ACT.Sqrt,
                  scale=(float(P), 1.0)[r], bias=eps[:, 1 - r:2 - r]).then_inc(sem("roots4_ready"), 1)

            with act.Fori(0, GROUPS) as g:
                def at(name, per=1, k=1):
                    act.wait_ge(sem(name), g * per + k)
                at("even_group")
                f(w_sl, conv[:, :, ds(g * P, P)], ACT.Copy).then_inc(sem("w_cut"), 1)
                at("dec_ready")
                f(dec, dec, ACT.Exp).then_inc(sem("dec_exp"), 1)
                f(egc, gct, ACT.Exp)
                f(erow, ps[:, 0:3, :].rearrange("p b (h i) -> p (b h) i", h=4), ACT.Exp).then_inc(sem("erow_ready"), 1)
                for l in range(1, LEVELS):
                    at("vt_mm", LEVELS - 1, l)
                    f(vt, bank4(6), ACT.Copy).then_inc(sem("vt_ready"), 1)
                at("wt_mm")
                f(wt, bank4(5), ACT.Copy, scale=-1.0).then_inc(sem("wt_ready"), 1)
                at("vn_mm")
                f(vn, bank4(6), ACT.Copy).then_inc(sem("vn_ready"), 1)

            act.wait_ge(sem("even_group"), GROUPS + 1)
            f(sm_val[0:NS_TOK, 0:12], g12[0:NS_TOK, 4, :], ACT.Exp).then_inc(sem("sm_exp"), 1)

            act.wait_ge(sem("even_sample"), 1)
            f(sq4, hT[:, 0:4, :], ACT.Square).then_inc(sem("sq4_ready"), 1)
            act.wait_ge(sem("sums4_ready"), 3)
            f(sq4.rearrange("p a (b t) -> p (a b) t", b=2), ps[:, :, 0:TH], ACT.Sqrt,
              scale=1.0 / P, bias=eps[:, 0:1]).then_inc(sem("roots4_ready"), 1)
            act.wait_ge(sem("ssm_gated"), 1)
            f(sq4, hT[:, 4:8, :], ACT.Square).then_inc(sem("sq4_ready"), 1)
            act.wait_ge(sem("sums4_ready"), 4)
            f(sq4[:, 0:2, :].rearrange("p a (b t) -> p (a b) t", b=2), ps[:, 0:4, 0:TH], ACT.Sqrt,
              scale=1.0 / 256, bias=eps[:, 0:1]).then_inc(sem("roots4_ready"), 1)

            def peer(L):
                norm(2 * L + 1)
                copies(f"query{L}", query)
                with act.Fori(0, NT) as n:
                    act.wait_ge(sem("score_mm"), n + (L * NT + 1))
                    act.wait_ge(sem("topk_free"), n + (L * NT + 1))
                    f(score[0:TILE].rearrange("p (b k) i -> p b (k i)", b=4), ps[0:TILE, 0:4, :], ACT.Copy)\
                        .then_inc(sem("score_ready"), 1)
                    act.wait_ge(sem("score_ready"), n + (L * NT + 1))
                    act.sem_inc(sem("score_free"), 1)
                    act.wait_ge(sem("best_diff"), n + (L * NT + 1))
                    f(bests[0:TILE], posf[0:TILE], ACT.Exp).then_inc(sem("best_exp"), 1)
                with act.Fori(0, QUARTERS) as q:
                    act.wait_ge(sem("quarter_free"), q + (L * (QUARTERS + 1) + 1))
                    with act.Fori(0, GSTEPS // 4) as i:
                        for s in range(4):
                            act.wait_ge(sem("gate_mm"), q * GSTEPS + 4 * i + (L * QUARTERS * GSTEPS + s + 5))
                            f(gates[:, :, ds(4 * GT * i + GT * s, GT)],
                              ps[:, s, 0:GT * JQ].rearrange("p (t j) -> p j t", t=GT), ACT.Copy)\
                                .then_inc(sem("gate_free"), 1)

                    def gelu(slot, m):
                        for j in range(JG):
                            act.wait_ge(sem("pre_done"), q * JQ + m * (2 * JG) + (slot * JG + L * NKEY + j + 1))
                            if j == 0:
                                act.wait_ge(sem("a_free"), q * GQ + 2 * m + (slot + L * QUARTERS * GQ + 1))
                            f(split(aring[:, slot, j, :]), both(2 * (j % 2)), ACT.Gelu_apprx_tanh)\
                                .then_inc(sem("pre_free"), 1)
                    with act.Fori(0, GQ // 2) as m:
                        gelu(0, m)
                        gelu(1, m)

            act.wait_ge(sem("even_stored"), 32)
            act.wait_ge(sem("stored"), 64)
            peer(0)
            norm(2)
            copies("odd_in", oproj)
            act.wait_ge(sem("glr_mm"), 1)
            f(split(glrT[0:16]), both(0, 16), ACT.Copy).then_inc(sem("glr_ready"), 1)
            act.wait_ge(sem("gk_abs"), 1)
            f(gk2, gk2, ACT.Exp, scale=-1.0).then_inc(sem("act_gk"), 1)
            f(sm_a2, sm_a2, ACT.Exp, scale=-1.0).then_inc(sem("act_gk"), 1)
            act.wait_ge(sem("act_gk"), 2)
            f(gk2, gk2, ACT.Ln, bias=eps[:, 2:3]).then_inc(sem("act_gk"), 1)
            f(sm_a2, sm_a2, ACT.Ln, bias=eps[:, 2:3]).then_inc(sem("act_gk"), 1)
            act.wait_ge(sem("sm_gk"), 1)
            f(sm_a, sm_a, ACT.Exp, scale=1.0 / 16).then_inc(sem("sm_alpha"), 1)
            f(oproj[:, 16:24, :], oproj[:, 16:24, :], ACT.Silu).then_inc(sem("gates_silu"), 1)
            with act.Fori(0, GROUPS) as g:
                def at(name, per=1, k=1):
                    act.wait_ge(sem(name), g * per + k)
                at("odd_group")
                f(gk_sl, gk[:, ds(g, 1), :].rearrange("p a b -> p (a b)"), ACT.Copy)
                f(o_sl, oproj[:, 0:16, ds(g * P, P)], ACT.Copy).then_inc(sem("odd_cut"), 1)
                at("v_mm")
                f(vtok, ps[:, 2:4, :].rearrange("p b (v i) -> p (b v) i", v=4), ACT.Copy).then_inc(sem("vtok_ready"), 1)
                at("dm_ready")
                f(e_q, dm, ACT.Exp)
                f(e_k, dm, ACT.Exp, scale=-1.0)
                f(e_b, bt, ACT.Exp)
                f(dl, dl, ACT.Exp).then_inc(sem("exps_ready"), 1)
            act.wait_ge(sem("odd_sample"), 1)
            f(o_sq, hT[:, :, :], ACT.Square).then_inc(sem("sq4_ready"), 1)
            act.wait_ge(sem("sums4_ready"), 5)
            f(o_r.rearrange("p a (b t) -> p (a b) t", b=2), ps[:, :, 0:TH], ACT.Sqrt,
              scale=1.0 / 256, bias=eps[:, 0:1]).then_inc(sem("roots4_ready"), 1)
            act.wait_ge(sem("odd_stored"), 32)
            peer(1)
            norm(4)

        @block.vector
        def _(dve):
            tt, stt, tsc, cp = dve.tensor_tensor, dve.scalar_tensor_tensor, dve.tensor_scalar, dve.tensor_copy
            SUB, ADD, MUL = ALU.subtract, ALU.add, ALU.mult

            def signal(name):
                dve.drain()
                dve.sem_inc(sem(name), 1)

            def norm(k):
                dve.wait_ge(sem("root_ready"), k + 1)
                dve.reciprocal(nrt, nrt)
                dve.drain()
                for c in range(KD):
                    last = stt(hT[:, c, :], xT[:, c, :], ln[:, k, c:c + 1], nrt, MUL, MUL)
                last.then_inc(sem("h_ready"), 1)

            def residual(name):
                base = BASE[name]
                with dve.Fori(0, BLOCKS[name] // WSLOTS) as i:
                    for u in range(WSLOTS):
                        dve.wait_ge(sem("gemm_done"), WSLOTS * i + (base + u + 1))
                        x = xT[:, ds(WSLOTS * i + u, 1), :].rearrange("p a (b t) -> p (a b) t", b=2)
                        tt(x, both(2 * (u % 2)), x, ADD).then_inc(sem("gemm_free"), 1)
                signal("x_ready")

            for c, v in enumerate((EPS, P * EPS, 1.0)):
                dve.memset(eps[:, c:c + 1], v)
            dve.memset(g_raw, 0.0)
            signal("eps_ready")
            dve.wait_ge(sem("params"), 16 * NLOADS)
            norm(0)

            with dve.Fori(0, 20) as n:
                dve.wait_ge(sem("gemm_free"), n + 3)

                def blk(v, a, b):
                    return v[:, ds(n, 1), a:b].rearrange("p a t -> p (a t)")
                w = conv_w[:, ds(n, 1), :].rearrange("p a w -> p (a w)")
                tsc(blk(conv, 0, NP_TOK), blk(proj, 0, NP_TOK), w[:, 3:4],
                    conv_b[:, ds(n, 1)], MUL, ADD)
                for s in range(1, 4):
                    dve.drain()
                    stt(blk(conv, s, NP_TOK), blk(proj, 0, NP_TOK - s), w[:, 3 - s:4 - s],
                        blk(conv, s, NP_TOK), MUL, ADD)
                dve.drain()
                dve.sem_inc(sem("conv_done"), 1)
            dve.wait_ge(sem("buf_loaded"), 16)
            x_new = proj[:, 0:20, NP_TOK:T]

            def wcol(k):
                return conv_w[:, :, k:k + 1].to_broadcast([P, 20, NS_TOK])
            tt(acc_c, x_new, wcol(3), MUL)
            for k in range(3):
                tt(tmp_c, buf_c[:, k], wcol(k), MUL)
                dve.drain()
                tt(acc_c, acc_c, tmp_c, ADD)
                dve.drain()
                cp(new_c[:, k], x_new if k == 2 else buf_c[:, k + 1])
                cp(tail_c[:, k, :], proj[:, 0:20, NP_TOK - 3 + k:NP_TOK - 2 + k].rearrange("p n a -> p (n a)"))
            tt(conv[:, :, NP_TOK:T], acc_c, conv_b[:, :].rearrange("p (n a) -> p n a", a=1).to_broadcast([P, 20, NS_TOK]), ADD)
            signal("conv_done")

            dve.wait_ge(sem("gates_mm"), 1)
            cp(g_raw[:, 0:4, :], ps[:, 0, 0:64].rearrange("p (n c) -> p n c", n=4))
            cp(g_raw[0:NS_TOK, 4, :], ps[0:NS_TOK, 0, 64:80])
            signal("gates_read")
            bias = small_b[:, :].rearrange("p (a c) -> p a c", a=1).to_broadcast([P, 5, 16])
            tt(g_raw, g_raw, bias, ADD)
            dve.drain()
            stt(g_abs, g_raw, -1.0, g_raw, MUL, ALU.max)
            tsc(g_sp, g_raw, 0.0, None, ALU.max)
            signal("gates_abs")
            dve.wait_ge(sem("act_gates"), 4)
            tt(g_sp, g_sp, g_abs, ADD)
            tsc(neg_a, neg_a, -1.0, None, MUL)
            dve.drain()
            tt(g12, g_sp[:, :, 0:12], neg_a.rearrange("p (a c) -> p a c", a=1).to_broadcast([P, 5, 12]), MUL)
            for r in range(2):
                dve.wait_ge(sem("roots4_ready"), r + 1)
                dve.reciprocal(sq4, sq4)
                dve.drain()
                tt(conv[:, 4 * r:4 * r + 4, :], conv[:, 4 * r:4 * r + 4, :], sq4, MUL)
                signal("l2_done")
            dve.memset(s_dn, 0.0)
            dve.memset(s_ssm, 0.0)
            signal("even_group")

            def bc(v, n):
                return v.rearrange("p (k a) -> p k a", a=1).to_broadcast([P, v.shape[1], n])

            def at_end(v):
                return v[:, :, P - 1:P]

            with dve.Fori(0, GROUPS) as g:
                def at(name, per=1, k=1):
                    dve.wait_ge(sem(name), g * per + k)

                def cut(v, a, b):
                    return v[:, ds(g, 1), a:b].rearrange("p a c -> p (a c)")
                cp(g_sl, cut(g12, 0, 12))
                cp(b_sl, cut(beta, 0, 4))
                cp(d_sl, cut(g_sp, 4, 12)).then_inc(sem("gates_cut"), 1)
                at("rows_ready")
                cp(gct, ps[:, 3, 0:12])
                dve.drain()
                tt(dec, ps[:, 0:3, :].rearrange("p b (h i) -> p (b h) i", h=4), bc(gct, P), SUB)
                dve.drain()
                tsc(dec, dec, 0.0, None, ALU.min).then_inc(sem("dec_ready"), 1)
                at("erow_ready")
                tt(dec, dec, masks[:, CAUSAL:CAUSAL + 1, :].to_broadcast([P, 12, P]), MUL)
                tt(b_e, b_sl, egc[:, 0:4], MUL)
                at("w_cut")
                tt(kb, w_sl[:, 4:8, :], bank4(4), MUL).then_inc(sem("kb_ready"), 1)
                tt(qi, w_sl[:, 0:4, :], erow[:, 0:4, :], MUL)
                at("kk_ready")
                tt(nmat, bank4(5), dec[:, 0:4, :], MUL)
                dve.drain()
                tt(nmat, nmat, mask4(STRICT), MUL).then_inc(sem("n_ready"), 1)
                tt(qkt, bank4(6), dec[:, 0:4, :], MUL)
                dve.drain()
                tt(pmat, nmat, mask4(LEVEL0), MUL)
                tt(kbt, bank4(7), bc(b_e, P), MUL)
                tt(kout, bank4(7), at_end(dec[:, 0:4, :]).to_broadcast([P, 4, P]), MUL)
                tt(vb, bank4(0), bc(b_sl, P), MUL)
                dve.drain()
                tt(pmat, mask4(IDENT), pmat, SUB).then_inc(sem("p0_ready"), 1)
                at("x0_ready")
                cp(xmat, bank4(5)).then_inc(sem("px_ready"), 1)
                at("ssm_mm")

                def ssm_work(l):
                    if l == 1:
                        cp(btk, ps[:, 3, 0:256].rearrange("p (a b) -> p a b", a=2))
                    if l == 2:
                        tt(xd8, ps[:, 2, :].rearrange("p (h c) -> p h c", h=8), bc(d_sl, 64), MUL)
                    if l == 3:
                        dve.drain()
                        tt(xo8, xd8, at_end(dec[:, 4:12, :]).to_broadcast([P, 8, 64]), MUL)
                    if l == 4:
                        for j in range(2):
                            tt(att[:, 4 * j:4 * j + 4, :], dec[:, 4 + 4 * j:8 + 4 * j, :],
                               ps[:, 1, j * P:(j + 1) * P].rearrange("p (a i) -> p a i", a=1).to_broadcast([P, 4, P]), MUL)
                    if l == 5:
                        for j in range(2):
                            last = tt(ci[:, 4 * j:4 * j + 4, :], erow[:, 4 + 4 * j:8 + 4 * j, :],
                                      w_sl[:, 18 + j:19 + j, :].to_broadcast([P, 4, P]), MUL)
                        last.then_inc(sem("att_ready"), 1)
                for l in range(1, LEVELS):
                    ssm_work(l)
                    at("z_mm", LEVELS - 1, l)
                    last = tt(pmat, pmat, bank4(7), SUB)
                    if l < LEVELS - 1:
                        last = tt(xmat, xmat, bank4(0), SUB)
                    last.then_inc(sem("px_ready"), 1)
                at("o_mm")
                cp(hT[:, 0:4, ds(g * P, P)], bank4(7))
                for h in range(4):
                    stt(s_dn[:, h, :], s_dn[:, h, :], erow[:, h, P - 1:P], ps[:, 0, h * P:(h + 1) * P], MUL, ADD)
                at("ssm_out_mm")
                cp(hT[:, 4:8, ds(g * P, P)], bank4(4))
                s8 = s_ssm.rearrange("p (h c) -> p h c", h=8)
                tt(s8, s8, at_end(erow[:, 4:12, :]).to_broadcast([P, 8, 64]), MUL)
                dve.drain()
                tt(s_ssm, s_ssm, ps[:, 5, :], ADD)
                dve.drain()
                dve.sem_inc(sem("even_group"), 1)

            dve.wait_ge(sem("sm_exp"), 1)
            cp(sm_val[0:NS_TOK, 12:16], beta[0:NS_TOK, 4, :])
            cp(sm_val[0:NS_TOK, 16:24], g_sp[0:NS_TOK, 4, 4:12])
            dve.drain()
            tt(sm_diag[0:NS_TOK], sm_val[0:NS_TOK].rearrange("p (a c) -> p a c", a=1).to_broadcast([NS_TOK, NS_TOK, 24]),
               ident[0:NS_TOK, 0:NS_TOK].rearrange("p (b a) -> p b a", a=1).to_broadcast([NS_TOK, NS_TOK, 24]), MUL)\
                .then_inc(sem("diag_ready"), 1)
            dve.wait_ge(sem("bc_mm"), 1)
            cp(sm_bc, ps[:, 0, 0:192].rearrange("p (b c) -> p b c", b=NS_TOK))
            dve.drain()
            dve.wait_ge(sem("r_mm"), 1)
            tt(sm_r, ps[:, 1, 0:32].rearrange("p (h b) -> p h b", h=4), sm_bc[:, :, 0:4].rearrange("p b h -> p h b"), MUL)
            dve.drain()
            tt(sm_r, conv[:, 8:12, NP_TOK:T], sm_r, SUB)
            dve.drain()
            tt(sm_r, sm_r, sm_bc[:, :, 12:16].rearrange("p b h -> p h b"), MUL).then_inc(sem("delta_ready"), 1)
            for h in range(4):
                v = sm_dn.rearrange("p (b h) d -> p h b d", h=4)[:, h]
                tt(v, v, sm_bc[:, :, h:h + 1].to_broadcast([P, NS_TOK, P]), MUL)
            dve.drain()
            for b in range(NS_TOK):
                dve.wait_ge(sem("delta_rows"), b + 1)
                for h in range(4):
                    s = sm_dn[:, b * 4 + h, :]
                    stt(s, ps[:, b, h * P:(h + 1) * P], conv[:, 4 + h, NP_TOK + b:NP_TOK + b + 1], s, MUL, ADD)
            signal("dn_states_new")
            for half in range(2):
                r = slice(64 * half, 64 * half + 64)
                tt(sm_xd[r], conv[r, 12:16, NP_TOK:T], sm_bc[r, :, 16 + half:24:2].rearrange("p b k -> p k b"), MUL)
            for h in range(8):
                v = sm_ssm[:, :, 64 * h:64 * h + 64]
                tt(v, v, sm_bc[:, :, 4 + h:5 + h].to_broadcast([P, NS_TOK, 64]), MUL)
            dve.wait_ge(sem("sm_o_mm"), 1)
            cp(hT[:, 0:4, NP_TOK:T], ps[:, 0, 0:32].rearrange("p (h b) -> p h b", h=4))
            signal("sm_o_read")
            for b in range(NS_TOK):
                dve.wait_ge(sem("x_rows"), b + 1)
                for j in range(2):
                    s = sm_ssm[:, b, 256 * j:256 * j + 256]
                    stt(s, ps[:, b, 256 * j:256 * j + 256], conv[:, 16 + j, NP_TOK + b:NP_TOK + b + 1], s, MUL, ADD)
            signal("ssm_states_new")
            dve.wait_ge(sem("sm_y_mm"), 1)
            cp(hT[:, 4:8, NP_TOK:T], ps[:, 0, 0:32].rearrange("p (h b) -> p h b", h=4))
            signal("even_sample")

            for k in range(4):
                stt(hT[:, 4 + k, :], conv[:, 12 + k, :], head_w[:, 5 + k:6 + k], hT[:, 4 + k, :], MUL, ADD)
            dve.drain()
            dve.wait_ge(sem("gates_silu"), 1)
            tt(hT[:, 4:8, :], hT[:, 4:8, :], proj[:, 24:28, :], MUL)
            dve.wait_ge(sem("roots4_ready"), 3)
            dve.reciprocal(sq4, sq4)
            dve.drain()
            tt(hT[:, 0:4, :], hT[:, 0:4, :], sq4, MUL)
            signal("ssm_gated")
            stt(hT[:, 0:4, :], hT[:, 0:4, :], head_w[:, 0:1], proj[:, 20:24, :], MUL, MUL)
            dve.wait_ge(sem("roots4_ready"), 4)
            dve.reciprocal(sq4[:, 0:2, :], sq4[:, 0:2, :])
            dve.drain()
            for k in range(4):
                stt(hT[:, 4 + k, :], hT[:, 4 + k, :], head_w[:, 1 + k:2 + k], sq4[:, k // 2, :], MUL, MUL)
            signal("mix_ready")
            residual("even_out")

            def top16(L, n, src, vals, idx, count):
                for k in range(count):
                    dve.max(vals(k)[:, 0:8], src(k))
                dve.drain()
                for k in range(count):
                    dve.max_index(idx(k)[:, 0:8], vals(k)[:, 0:8], src(k))
                dve.drain()
                for k in range(count):
                    dve.match_replace(out=src(k), in_to_replace=vals(k)[:, 0:8], in_values=src(k), imm_value=-3e38)
                dve.drain()
                for k in range(count):
                    dve.max(vals(k)[:, 8:16], src(k))
                dve.drain()
                for k in range(count):
                    dve.max_index(idx(k)[:, 8:16], vals(k)[:, 8:16], src(k))
                dve.drain()

            def peer(L):
                norm(2 * L + 1)
                R = slice(0, TILE)
                dve.wait_ge(sem("iota_ready"), 1)
                dve.wait_ge(sem("keys_loaded"), 16 * (L + 1))
                signal("topk_free")
                with dve.Fori(0, NT) as n:
                    dve.wait_ge(sem("score_ready"), n + (L * NT + 1))
                    cp(iota16, iota[:, 0:TOPK])
                    top16(L, n, lambda k: score[R, k, :], lambda k: topv[R, k, :], lambda k: topi[R, k, :], 2 * PH)
                    dve.sem_inc(sem("topk_free"), 1)
                    cp(topf[R], topi[R])
                    for h in range(PH):
                        tt(cand[R, h, :].rearrange("p (a b) -> p a b", a=TOPK),
                           topv[R, 2 * h, :].rearrange("p (a b) -> p a b", b=1).to_broadcast([TILE, TOPK, TOPK]),
                           topv[R, 2 * h + 1, :].rearrange("p (a b) -> p a b", a=1).to_broadcast([TILE, TOPK, TOPK]), ADD)
                    dve.drain()
                    top16(L, n, lambda k: cand[R, k, :], lambda k: bests[R, k, :], lambda k: bestj[R, k, :], PH)
                    tt(posf[R], bests[R], bests[R, :, 0:1].to_broadcast([TILE, PH, TOPK]), SUB)\
                        .then_inc(sem("best_diff"), 1)
                    dve.wait_ge(sem("best_exp"), n + (L * NT + 1))
                    dve.reduce_sum(ssum[R], bests[R], axis=X)
                    dve.drain()
                    dve.reciprocal(ssum[R], ssum[R])
                    dve.drain()
                    tt(res[R, 2, :].rearrange("p (h k) -> p h k", h=PH), bests[R],
                       ssum[R].rearrange("p (h a) -> p h a", a=1).to_broadcast([TILE, PH, TOPK]), MUL)
                    for side, (op, by) in enumerate(((ALU.logical_shift_right, 4), (ALU.bitwise_and, 15))):
                        tsc(posu[R], bestj[R], by, None, op)
                        dve.drain()
                        cp(posf[R], posu[R])
                        dve.drain()
                        tt(eq[R], posf[R].rearrange("p h (k a) -> p (h k) a", a=1).to_broadcast([TILE, PH * TOPK, TOPK]),
                           iota16[R].rearrange("p (k a) -> p k a", k=1).to_broadcast([TILE, PH * TOPK, TOPK]), ALU.is_equal)
                        dve.drain()
                        for h in range(PH):
                            e = eq[R, h * TOPK:(h + 1) * TOPK, :]
                            tt(e, e, topf[R, 2 * h + side:2 * h + side + 1, :].to_broadcast([TILE, TOPK, TOPK]), MUL)
                        dve.drain()
                        dve.reduce_sum(res[R, side, :], eq[R], axis=X)
                        dve.drain()
                    dve.sem_inc(sem("chosen"), 1)
                    dve.wait_ge(sem("chosen_mm"), n + (L * NT + 1))
                    cols = ds(n * TILE, TILE)
                    cp(idx1T[:, cols], ps[:, 4, 0:TILE])
                    cp(idx2T[:, cols], ps[:, 4, TILE:2 * TILE])
                    cp(gfull, ps[:, 4, 2 * TILE:3 * TILE])
                    dve.drain()
                    cp(ghiT[:, cols], gfull)
                    dve.drain()
                    tt(gloT[:, cols], gfull, ghiT[:, cols], SUB)
                signal("quarter_free")
                with dve.Fori(0, QUARTERS) as q:
                    with dve.Fori(0, GSTEPS // 4) as i:
                        for s in range(4):
                            dve.wait_ge(sem("gate_mm"), q * GSTEPS + 4 * i + (L * QUARTERS * GSTEPS + s + 1))
                            tt(hot_i[:, s], iota[:, :].rearrange("p (a i) -> p a i", a=1).to_broadcast([P, GT, NKEY]),
                               idx1T[:, ds(4 * GT * i + GT * s, GT)].rearrange("p (t a) -> p t a", a=1)
                               .to_broadcast([P, GT, NKEY]), ALU.is_equal).then_inc(sem("hot_i_ready"), 1)
                            dve.wait_ge(sem("gate_mm"), q * GSTEPS + 4 * i + (L * QUARTERS * GSTEPS + s + 3))
                            tt(hot_j[:, 2 * (s % 2) + 1],
                               iota[:, ds(q * JQ, JQ)].rearrange("p (a j) -> p a j", a=1).to_broadcast([P, GT, JQ]),
                               idx2T[:, ds(4 * GT * i + GT * s, GT)].rearrange("p (t a) -> p t a", a=1)
                               .to_broadcast([P, GT, JQ]), ALU.is_equal).then_inc(sem("hot_eq_ready"), 1)
                    dve.wait_ge(sem("gate_free"), q * GSTEPS + (L * QUARTERS * GSTEPS + GSTEPS + 4))

                    def gate(slot, m):
                        for j in range(JG):
                            dve.wait_ge(sem("pre_free"), q * JQ + m * (2 * JG) + (slot * JG + L * NKEY + j + 3))
                            a = aring[:, slot, j, :]
                            tt(a, a, gates[:, ds(m * (2 * JG) + (slot * JG + j), 1), :].rearrange("p a t -> p (a t)"),
                               MUL).then_inc(sem("act_ready"), 1)

                    def add(slot, m):
                        for c in range(KD):
                            dve.wait_ge(sem("y_done"), q * (KD * GQ) + m * (2 * KD) + (slot * KD + L * KD * QUARTERS * GQ + c + 1))
                            last = tt(split(xT[:, c, :]), both(4 + 2 * (c % 2)), split(xT[:, c, :]), ADD)
                            last.then_inc(sem("y_free"), 1)
                        dve.drain()
                        dve.sem_inc(sem("a_free"), 1)
                    gate(0, 0)
                    with dve.Fori(0, GQ // 2 - 1) as m:
                        gate(1, m)
                        add(0, m)
                        gate(0, m + 1)
                        add(1, m)
                    gate(1, GQ // 2 - 1)
                    add(0, GQ // 2 - 1)
                    add(1, GQ // 2 - 1)
                    dve.sem_inc(sem("quarter_free"), 1)
                signal("x_ready")

            dve.sem_inc(sem("a_free"), 2)
            dve.sem_inc(sem("y_free"), 2)
            peer(0)
            norm(2)

            dve.wait_ge(sem("odd_loads"), 16)
            dve.wait_ge(sem("gk_sample_mm"), 1)
            tt(gk, ps[:, 4:8, :], gbias.rearrange("p (a c) -> p a c", a=1).to_broadcast([P, GROUPS, 512]), ADD)
            tt(sm_a, ps[:, 2, 0:32].rearrange("p (h b) -> p h b", h=4),
               head_w[:, 11:15].rearrange("p (h b) -> p h b", b=1).to_broadcast([P, 4, NS_TOK]), ADD)
            dve.drain()
            stt(gk2, gk, -1.0, gk, MUL, ALU.max)
            stt(sm_a2, sm_a, -1.0, sm_a, MUL, ALU.max)
            tsc(gk, gk, 0.0, None, ALU.min)
            tsc(sm_a, sm_a, 0.0, None, ALU.min)
            signal("gk_abs")
            dve.wait_ge(sem("act_gk"), 4)
            tt(sm_a, sm_a, sm_a2, SUB).then_inc(sem("sm_gk"), 1)
            tt(gk, gk, gk2, SUB)
            dve.drain()
            tsc(gk, gk, 1.0 / 16, None, MUL)
            dve.memset(s_gla, 0.0)
            signal("odd_group")
            dve.sem_inc(sem("s_ready"), 1)
            scale = float(P) ** -0.5

            def chunks(v):
                return v.rearrange("p h (c i) -> p (h c) i", i=GC)
            with dve.Fori(0, GROUPS) as g:
                def at(name, per=1, k=1):
                    dve.wait_ge(sem(name), g * per + k)
                at("bt_mm")
                cp(bt, bank4(0))
                dve.drain()
                b16 = chunks(bt)
                tt(chunks(dm), b16, b16[:, :, GC // 2 - 1:GC // 2].to_broadcast([P, 16, GC]), SUB)
                tt(chunks(dl), b16[:, :, GC - 1:GC].to_broadcast([P, 16, GC]), b16, SUB).then_inc(sem("dm_ready"), 1)
                at("odd_cut")
                at("exps_ready")
                stt(qt, o_sl[:, 0:4, :], scale, e_q, MUL, MUL)
                tt(kt, o_sl[:, 4:8, :], e_k, MUL)
                tt(kc, o_sl[:, 4:8, :], dl, MUL).then_inc(sem("qk_ready"), 1)
                stt(qb, o_sl[:, 0:4, :], scale, e_b, MUL, MUL)
                at("gatt_mm")
                tsc(gatt, bank4(1), BIG, -BIG, ALU.min, ALU.max)
                cp(ko, bank4(4))
                dve.drain()
                tt(gatt, gatt, mask4(GLAMASK), MUL).then_inc(sem("gatt_ready"), 1)
                at("intra_mm")
                o = hT[:, :, ds(g * P, P)]
                cp(o, ps[:, 5:7, :].rearrange("p b (v i) -> p (b v) i", v=4)).then_inc(sem("intra_read"), 1)
                for c in range(P // GC):
                    at("inter_mm", P // GC, c + 1)
                    for h in range(4):
                        last = stt(s_gla[:, h, :], s_gla[:, h, :], e_b[:, h, (c + 1) * GC - 1:(c + 1) * GC],
                                   ps[:, 2 + 2 * (c % 2) + h // 2, (h % 2) * 256:(h % 2) * 256 + 256], MUL, ADD)
                    last.then_inc(sem("s_ready"), 1)
                tt(o, o, ps[:, 6:8, :].rearrange("p b (v i) -> p (b v) i", v=4), ADD)
                dve.drain()
                dve.sem_inc(sem("odd_group"), 1)

            tsc(sm_q, oproj[:, 0:4, NP_TOK:T], scale, None, MUL)
            signal("gla_rows_read")
            dve.wait_ge(sem("sm_alpha"), 1)
            dve.wait_ge(sem("odd_states"), 16)
            for h in range(4):
                v = sm_gla.rearrange("p (b h) d -> p h b d", h=4)[:, h]
                tt(v, v, sm_a[:, h, :].rearrange("p (b a) -> p b a", a=1).to_broadcast([P, NS_TOK, 256]), MUL)
            dve.drain()
            for r in range(2):
                dve.wait_ge(sem("gla_rows"), r + 1)
                for b in range(4):
                    for h in range(4):
                        s = sm_gla[:, (4 * r + b) * 4 + h, :]
                        stt(s, ps[:, 2 * b + h // 2, (h % 2) * 256:(h % 2) * 256 + 256],
                            oproj[:, 4 + h, NP_TOK + 4 * r + b:NP_TOK + 4 * r + b + 1], s, MUL, ADD)
                signal("gla_rows_read")
            dve.sem_inc(sem("gla_states_new"), 1)
            dve.wait_ge(sem("gla_o_mm"), 1)
            cp(hT[:, :, NP_TOK:T], ps[:, 0, 0:64].rearrange("p (k b) -> p k b", k=8))
            signal("odd_sample")
            dve.wait_ge(sem("roots4_ready"), 5)
            dve.wait_ge(sem("gates_silu"), 2)
            dve.reciprocal(o_r, o_r)
            dve.drain()
            for k in range(8):
                stt(hT[:, k, :], hT[:, k, :], head_w[:, 9 + k % 2:10 + k % 2], o_r[:, k // 2, :], MUL, MUL)
            dve.drain()
            tt(hT[:, :, :], hT[:, :, :], oproj[:, 16:24, :], MUL)
            signal("mix_ready")
            residual("odd_out")
            peer(1)
            norm(4)


INPUTS = dict(
    masks=(P, NMASK, P), xT=(P, KD, T), ln=(P, 5, KD), conv_w=(P, 20, 4), conv_b=(P, 20), small_w=(P, KD, 16),
    glr_w=(P, KD, 16), head_w=(P, 16), gate2=(16, 512), small_b=(1, 16), a_log=(1, 12), gbias=(1, 512),
    conv_buf=(P, 3, 20, NS_TOK), s_dn=(P, 32 * P), s_ssm=(P, NS_TOK * 512), s_gla=(P, 32 * 256),
    keys0=(P, 16, NKEY), keys1=(P, 16, NKEY), weights=(NBLOCKS, P, D),
    u0=(32, P, JG * D), u1=(32, P, JG * D), v0=(32, P, JG * D), v1=(32, P, JG * D))
OUTPUTS = dict(
    o_y=(P, KD, T), o_conv_p=(P, 3, 20), o_conv_s=(P, 3, 20, NS_TOK), o_dn=(P, 9, 512), o_ssm=(P, 9, 512),
    o_gla=(P, 9, 1024))


def constant_masks():
    import numpy as np
    r, c = np.arange(P)[:, None], np.arange(P)[None, :]
    m = [r == c, r == r + 0 * c, c >= r, c > r]
    for l in range(LEVELS):
        s = 1 << l
        m.append((r // (2 * s) == c // (2 * s)) & (r // s < c // s))
    m.append((r // GC == c // GC) & (c >= r))
    return np.ascontiguousarray(np.stack(m, axis=1).astype(np.float32))


def kernel(**inp):
    import numpy as np
    import concourse.bacc as bacc
    from concourse.bass_utils import run_bass_kernel_spmd

    A = {k: np.asarray(v) for k, v in inp.items()}
    f = np.ascontiguousarray

    def rows(w):
        return w.reshape(KD, P, -1).transpose(1, 0, 2)

    def blocks(w):
        return w.reshape(KD, P, -1, P).transpose(2, 1, 0, 3).reshape(-1, P, D)

    def cols(v):
        return v.reshape(-1, P).T

    we, wo = A["w_in_even"][0], A["w_in_odd"][0]
    qkv, a_in, b_in, gate, z, xbc, dt_in = np.split(we, [1536, 1540, 1544, 2056, 2568, 3592], axis=1)
    qk, v_in, glr, og = np.split(wo, [1024, 2048, 2064], axis=1)
    x = np.concatenate([A["x_prompt"][0], A["x_sample"][:, 0]], axis=0)
    zero = np.zeros
    keys = [np.stack([A["peer_keys1"][l], A["peer_keys2"][l]], axis=1).reshape(16, NKEY, P).transpose(2, 0, 1)
            for l in range(2)]
    conv_buf = np.concatenate([A["state_dn_conv"][0], A["state_ssm_conv"][0]], axis=2)
    ins = dict(
        masks=constant_masks(),
        xT=x.T.reshape(KD, P, T).transpose(1, 0, 2),
        ln=np.stack([A["ln_mix"][0], A["ln_ffn"][0], A["ln_mix"][1], A["ln_ffn"][1], A["ln_final"]])
        .reshape(5, KD, P).transpose(2, 0, 1),
        conv_w=np.concatenate([A["dn_conv_w"][0], A["ssm_conv_w"][0]], axis=1).reshape(4, 20, P).transpose(2, 1, 0),
        conv_b=np.concatenate([zero((12, P), np.float32), A["ssm_conv_b"][0].reshape(8, P)], axis=0).T,
        small_w=rows(np.concatenate([a_in, dt_in, b_in], axis=1)),
        glr_w=rows(glr),
        head_w=np.concatenate([cols(A["dn_norm_w"][0]), cols(A["ssm_norm_w"][0]),
                               cols(np.repeat(A["ssm_d"][0], 64)), cols(A["gla_norm_w"][0]),
                               cols(A["gla_b_gate"][0]), zero((P, 1), np.float32)], axis=1),
        gate2=A["gla_w_gate2"][0],
        small_b=np.concatenate([A["dn_dt_bias"][0], A["ssm_dt_bias"][0], zero(4, np.float32)])[None],
        a_log=np.concatenate([A["dn_a_log"][0], A["ssm_a_log"][0]])[None],
        gbias=A["gla_b_gate"][0][None],
        conv_buf=conv_buf.reshape(NS_TOK, 3, 20, P).transpose(3, 1, 2, 0),
        s_dn=A["state_dn"][0].transpose(2, 0, 1, 3).reshape(P, -1),
        s_ssm=A["state_ssm"][0].transpose(3, 0, 1, 2).reshape(P, -1),
        s_gla=A["state_gla"][0].transpose(2, 0, 1, 3).reshape(P, -1),
        keys0=keys[0], keys1=keys[1],
        weights=np.concatenate([blocks(np.concatenate([qkv, xbc, gate, z], axis=1)), blocks(A["w_out_even"][0]),
                                blocks(A["peer_w_q"][0]), blocks(np.concatenate([qk, v_in, og], axis=1)),
                                blocks(A["w_out_odd"][0]), blocks(A["peer_w_q"][1])], axis=0),
    )
    for l in range(2):
        u = A["peer_u"][l].reshape(NKEY, 32, JG, KD, P)
        ins[f"u{l}"] = u.transpose(1, 4, 2, 3, 0).reshape(32, P, JG * D)
        v = A["peer_v"][l].reshape(NKEY, 32, JG, D)
        ins[f"v{l}"] = v.transpose(1, 0, 2, 3).reshape(32, P, JG * D)
    ins = {k: f(v) for k, v in ins.items()}

    nc = bacc.Bacc("TRN2", target_bir_lowering=False, num_devices=1)
    f32 = mybir.dt.float32
    io = {k: nc.dram_tensor("in_" + k, s, f32, kind="ExternalInput").ap() for k, s in INPUTS.items()}
    for k, s in INPUTS.items():
        assert ins[k].shape == s and ins[k].dtype == np.float32, (k, ins[k].shape, s)
    io.update({k: nc.dram_tensor("out_" + k, s, f32, kind="ExternalOutput").ap() for k, s in OUTPUTS.items()})
    for k in ("keys", "u", "v"):
        io[k] = [io[f"{k}0"], io[f"{k}1"]]
    build_program(nc, io)
    r = run_bass_kernel_spmd(nc, [{"in_" + k: v for k, v in ins.items()}], core_ids=[0]).results[0]

    y = r["out_o_y"].transpose(2, 1, 0).reshape(T, D)
    tail = r["out_o_conv_p"].transpose(1, 2, 0).reshape(1, 1, 3, 2560)
    new = r["out_o_conv_s"].transpose(3, 1, 2, 0).reshape(1, NS_TOK, 3, 2560)
    dn = r["out_o_dn"].reshape(P, 9, 4, P).transpose(1, 2, 0, 3)[None]
    ssm = r["out_o_ssm"].reshape(P, 9, 8, 64).transpose(1, 2, 3, 0)[None]
    gla = r["out_o_gla"].reshape(P, 9, 4, 256).transpose(1, 2, 0, 3)[None]
    return (f(y[None, :NP_TOK]), f(y[NP_TOK:, None]), f(tail[..., :1536]), f(dn[:, :1]), f(tail[..., 1536:]),
            f(ssm[:, :1]), f(gla[:, :1]), f(new[..., :1536]), f(dn[:, 1:]), f(new[..., 1536:]), f(ssm[:, 1:]),
            f(gla[:, 1:]))
```

```python
import concourse.bass as bass
from concourse import mybir
from contextlib import ExitStack

P = 128
D = 1024
KD = D // P
NP_TOK = 512
NS_TOK = 8
T = NP_TOK + NS_TOK
TH = T // 2
GROUPS = NP_TOK // P
EPS = 1e-6
NKEY = 128
TOPK = 16
PH = 8
TILE = 104
NT = T // TILE
JG = 2
NG = NKEY // JG
GT = 8
GS = TILE // GT
GTURN = 6
WSLOTS = 4
GEMMS = [("even_in", 28), ("even_out", 8), ("query0", 16), ("odd_in", 24), ("odd_out", 8), ("query1", 16)]
BLOCKS = dict(GEMMS)
BASE = {name: sum(b for _, b in GEMMS[:k]) for k, (name, _) in enumerate(GEMMS)}
NBLOCKS = sum(BLOCKS.values())
IDENT, ONES, CAUSAL, STRICT, LEVEL0 = 0, 1, 2, 3, 4
LEVELS = 7
GLAMASK = LEVEL0 + LEVELS
NMASK = GLAMASK + 1
GC = 32
BIG = 1e30
ARENA = 38224
NLOADS = 11


def build_program(nc, io):
    f32, f16, u32 = mybir.dt.float32, mybir.dt.float16, mybir.dt.uint32
    f32r = mybir.dt.float32r
    ALU = mybir.AluOpType
    ACT = mybir.ActivationFunctionType
    X = mybir.AxisListType.X
    ds = bass.ds

    with ExitStack() as ctx:
        def sb(name, shape, dt=f32):
            return ctx.enter_context(nc.sbuf_tensor(name, shape, dt))

        sems = {}

        def sem(name):
            if name not in sems:
                sems[name] = ctx.enter_context(nc.semaphore(name))
            return sems[name]

        xT = sb("xT", [P, KD, T])
        h_at = nc.sbuf_base
        hT = sb("hT", [P, KD, T])
        assert nc.sbuf_base == h_at + 4 * KD * T
        wring = sb("wring", [P, WSLOTS, KD, P])
        masks = sb("masks", [P, NMASK, P])
        ln = sb("ln", [P, 5, KD])
        iota = sb("iota", [P, NKEY], f16)
        eps = sb("eps", [P, 4])
        conv_w = sb("conv_w", [P, 20, 4])
        conv_b = sb("conv_b", [P, 20])
        small_w = sb("small_w", [P, KD, 16])
        glr_w = sb("glr_w", [P, KD, 16])
        small_b = sb("small_b", [P, 16])
        a_log = sb("a_log", [P, 12])
        head_w = sb("head_w", [P, 16])
        gate2 = sb("gate2", [16, 512])
        arena_at = nc.sbuf_base
        arena = sb("arena", [P, ARENA])
        assert nc.sbuf_base == arena_at + 4 * ARENA
        ps = ctx.enter_context(nc.psum_tensor("ps", [P, 8, 512], f32))
        ident = masks[:, IDENT, :]
        ones = masks[:, ONES, :]
        causal = masks[:, CAUSAL, :]

        def mask4(k):
            return masks[:, k:k + 1, :].to_broadcast([P, 4, P])

        class Region:

            def __init__(self, at, end=ARENA):
                self.at, self.end = at, end

            def take_r(self, name, *shape):
                at = arena_at + 4 * self.at
                self.take(*shape)
                return at_byte(name, at, *shape)

            def take(self, *shape, dt=f32):
                n = 1
                for x in shape:
                    n *= x
                words = n // 2 if dt == f16 else n
                v = arena[:, self.at:self.at + words]
                self.at += words
                assert self.at <= self.end, (self.at, self.end)
                if dt != f32:
                    v = v.bitcast(dt)
                if len(shape) == 2:
                    v = v.rearrange("p (a b) -> p a b", a=shape[0])
                if len(shape) == 3:
                    v = v.rearrange("p (a b c) -> p a b c", a=shape[0], b=shape[1])
                return v

        def at_byte(name, at, *shape):
            return nc.alloc_sbuf_tensor_at(name, [P, *shape], f32r, offset=at)

        def both(bank, rows=P):
            return ps[0:rows, bank:bank + 2, 0:TH]

        def split(v):
            return v.rearrange("p (b t) -> p b t", b=2)

        def bank4(bank):
            return ps[:, bank, :].rearrange("p (h i) -> p h i", h=4)

        ev = Region(0)
        proj = ev.take(28, T)
        conv = ev.take(20, T)
        sq4 = ev.take(4, T)
        g_raw = ev.take(5, 16)
        g_abs = ev.take(5, 16)
        g_sp = ev.take(5, 16)
        g12 = ev.take(5, 12)
        beta = ev.take(5, 4)
        neg_a = ev.take(12)
        s_dn = ev.take(4, P)
        s_ssm = ev.take(512)
        buf_c = ev.take(3, 20, NS_TOK)
        new_c = ev.take(3, 20, NS_TOK)
        acc_c = ev.take(20, NS_TOK)
        tmp_c = ev.take(20, NS_TOK)
        tail_c = ev.take(3, 20)
        (kb, nmat, qkt, kbt, kout, vb, pmat, xmat, vt, wt, vn, qi, xd, xo) = [ev.take(4, P) for _ in range(14)]
        ci = ev.take(8, P)
        xd8, xo8 = [v.rearrange("p b (a c) -> p (b a) c", a=2) for v in (xd, xo)]
        sc = Region(0, 20 * T)
        w_sl = sc.take(20, P)
        g_sl = sc.take(12)
        b_sl = sc.take(4)
        d_sl = sc.take(8)
        gct = sc.take(12)
        egc = sc.take(12)
        dec = sc.take(12, P)
        erow = sc.take(12, P)
        nl = sc.take(6, 512)
        btk = sc.take(2, P)
        att = sc.take(8, P)
        b_e = sc.take(4)
        sm = Region(0, 20 * T)
        sm_dn = sm.take(32, P)
        sm_ssm = sm.take(NS_TOK, 512)
        sm_r = sm.take(4, NS_TOK)
        sm_xd = sm.take(4, NS_TOK)
        sm_val = sm.take(24)
        sm_diag = sm.take(NS_TOK, 24)
        sm_bc = sm.take(NS_TOK, 24)

        od = Region(0)
        oproj = od.take(24, T)
        glrT = od.take(T)
        gk = od.take(GROUPS, 512)
        gk2 = od.take(GROUPS, 512)
        gbias = od.take(512)
        s_gla = od.take(4, 256)
        o_sl = od.take(16, P)
        gk_sl = od.take(512)
        (bt, dm, dl, e_q, e_k, e_b, kc, ko, gatt) = [od.take(4, P) for _ in range(9)]
        (qt, kt, qb) = [od.take(4, P) for _ in range(3)]
        vtok = od.take(8, P)
        sm_gla = od.take(32, 256)
        sm_a = od.take(4, NS_TOK)
        sm_a2 = od.take(4, NS_TOK)
        sm_q = od.take(4, NS_TOK)
        osq = Region(0, 16 * T)
        o_sq = osq.take(8, T)
        o_r = osq.take(4, T)

        nm = Region(0)
        nsq = nm.take(KD, T)
        nrt = nm.take(T)

        pr = Region(0)
        ulo = Region(pr.at).take_r("u_lo", 2, JG * KD, P)
        uring = pr.take(2, JG * KD, P)
        idx1T = pr.take(T, dt=f16)
        idx2T = pr.take(T, dt=f16)
        gT = pr.take(T)
        r0 = pr.at
        stage = [pr.take(NKEY, TILE) for _ in range(2)]
        h0 = pr.at
        hot_i = pr.take(3, GT, NKEY)
        hot_j = pr.take(3, GT, NKEY)

        def hot_slot(s):
            return s % 2 if s < GTURN else 2

        def pair(s):
            return s % 3 if s < GTURN else 3
        ex = Region(r0 + NKEY * TILE, h0)
        hhi = ex.take_r("h_hi", KD, T)
        uhi = ex.take_r("u_hi", 2, JG * KD, P)
        vlo = Region(ex.at).take_r("v_lo", 2, JG, D)
        vring = ex.take(2, JG, D)
        ex = Region(r0, r0 + NKEY * TILE)
        vhi = ex.take_r("v_hi", 2, JG, D)
        gring = ex.take(2, NT * JG, TILE).rearrange("p s (n j) t -> p s n j t", j=JG)
        ex = Region(h0)
        alo = Region(ex.at).take_r("a_lo", 2, JG, T)
        hlo = at_byte("h_lo", h_at, KD, T)
        aring = ex.take(2, JG, T)
        ahi = ex.take_r("a_hi", 2, JG, T)
        tk = Region(r0)
        query = tk.take(2 * PH, T)
        score = tk.take(2 * PH, NKEY)
        cand = tk.take(PH, TOPK * TOPK)
        eq = tk.take(PH * TOPK, TOPK)
        topv = tk.take(2 * PH, TOPK)
        topi = tk.take(2 * PH, TOPK, dt=u32)
        topf = tk.take(2 * PH, TOPK)
        keys = tk.take(2 * PH, NKEY)
        bests = tk.take(PH, TOPK)
        bestj = tk.take(PH, TOPK, dt=u32)
        posu = tk.take(PH, TOPK, dt=u32)
        posf = tk.take(PH, TOPK)
        res = tk.take(3, P)
        ssum = tk.take(PH)
        iota16 = tk.take(TOPK)

        block = ctx.enter_context(nc.Block())

        @block.sync
        def _(sp):
            n = 0
            for dst, src in ((masks[:, :, :], io["masks"]), (xT[:, :, :], io["xT"]), (ln[:, :, :], io["ln"]),
                             (conv_w[:, :, :], io["conv_w"]), (conv_b[:, :], io["conv_b"]),
                             (small_w[:, :, :], io["small_w"]), (glr_w[:, :, :], io["glr_w"]),
                             (head_w[:, :], io["head_w"]), (gate2[:, :], io["gate2"]),
                             (small_b[:, :], io["small_b"].to_broadcast([P, 16])),
                             (a_log[:, :], io["a_log"].to_broadcast([P, 12]))):
                sp.dma_start(dst, src).then_inc(sem("params"), 16)
                n += 1
            assert n == NLOADS

            def load_block(i, u, base):
                sp.dma_start(wring[:, u, :, :].rearrange("p k c -> p (k c)"),
                             io["weights"][ds(WSLOTS * i + (base + u), 1)].rearrange("a p c -> (a p) c"))\
                    .then_inc(sem(f"w_loaded{u}"), 16)

            def stream(name):
                base = BASE[name]
                if base == 0:
                    for u in range(WSLOTS):
                        load_block(0, u, 0)
                with sp.Fori(int(base == 0), BLOCKS[name] // WSLOTS) as i:
                    for u in range(WSLOTS):
                        sp.wait_ge(sem("gemm_done"), WSLOTS * i + (base + u - WSLOTS + 1))
                        load_block(i, u, base)

            def experts(L):
                def load(what, ring, slot, g):
                    sp.dma_start(ring[:, slot].rearrange("p a b -> p (a b)"),
                                 io[what][L][ds(g, 1)].rearrange("a p c -> (a p) c"))\
                        .then_inc(sem(f"{what}_loaded{slot}"), 16)

                def load_gates(slot, g):
                    sp.dma_start(gring[:, slot],
                                 io["gates"][:, :, ds(g * JG, JG), :]).then_inc(sem(f"g_loaded{slot}"), 16)

                def store_gates(n, slot):
                    sp.wait_ge(sem("gate_free"), n * GS + (L * NT * GS + GS + 3))
                    sp.dma_start(io["gates"][:, ds(n, 1)].rearrange("p a j t -> p (a j t)"),
                                 stage[slot].rearrange("p j t -> p (j t)")).then_inc(sem(f"stored{slot}"), 16)

                sp.wait_ge(sem("h_ready"), 2 * L + 2)
                for slot in range(2):
                    load("u", uring, slot, slot)
                with sp.Fori(0, NT // 2) as i:
                    store_gates(2 * i, 0)
                    store_gates(2 * i + 1, 1)
                store_gates(NT - 1, 0)
                sp.wait_ge(sem("stored1"), 16 * (NT // 2) * (L + 1) + 16)
                for slot in range(2):
                    load("v", vring, slot, slot)
                sp.wait_ge(sem("stored0"), 16 * (NT // 2 + 1) * (L + 1) + 16)
                for slot in range(2):
                    load_gates(slot, slot)
                with sp.Fori(1, NG // 2) as m:
                    for slot in range(2):
                        sp.wait_ge(sem("pre_done"), m * (2 * JG) + (JG * (slot - 1) + L * NKEY))
                        load("u", uring, slot, 2 * m + slot)
                        sp.wait_ge(sem("gated"), m * (2 * JG) + (JG * (slot - 1) + L * NKEY))
                        load_gates(slot, 2 * m + slot)
                        sp.wait_ge(sem("y_done"), m * (2 * KD) + (KD * (slot - 1) + L * KD * NG))
                        load("v", vring, slot, 2 * m + slot)

            for slot in range(2):
                sp.sem_inc(sem(f"stored{slot}"), 16)
            stream("even_in")
            stream("even_out")
            stream("query0")
            experts(0)
            stream("odd_in")
            stream("odd_out")
            stream("query1")
            experts(1)

        @block.gpsimd
        def _(pool):
            pool.iota(iota[:, :], pattern=[[1, NKEY]], base=0, channel_multiplier=0,
                      allow_small_or_imprecise_dtypes=True).then_inc(sem("iota_ready"), 1)
            pool.dma_start(buf_c, io["conv_buf"]).then_inc(sem("buf_loaded"), 16)
            pool.wait_ge(sem("conv_done"), 21)
            pool.dma_start(io["o_conv_s"], new_c).then_inc(sem("stored"), 16)
            pool.dma_start(io["o_conv_p"], tail_c).then_inc(sem("stored"), 16)
            with pool.Fori(0, GROUPS) as g:
                pool.wait_ge(sem("n_ready"), g + 1)
                for l in range(1, LEVELS):
                    pool.tensor_tensor(nl[:, l - 1, :].rearrange("p (h i) -> p h i", h=4), nmat, mask4(LEVEL0 + l),
                                       ALU.mult).then_inc(sem("nl_ready"), 1)
            pool.wait_ge(sem("even_group"), GROUPS + 1)
            pool.dma_start(io["o_dn"][:, 0, :], s_dn.rearrange("p h d -> p (h d)")).then_inc(sem("stored"), 16)
            pool.dma_start(io["o_ssm"][:, 0, :], s_ssm).then_inc(sem("stored"), 16)
            pool.dma_start(sm_dn.rearrange("p a d -> p (a d)"), io["s_dn"]).then_inc(sem("even_states"), 16)
            pool.dma_start(sm_ssm.rearrange("p a d -> p (a d)"), io["s_ssm"]).then_inc(sem("even_states"), 16)
            pool.wait_ge(sem("even_sample"), 1)
            pool.dma_start(io["o_dn"][:, 1:9, :], sm_dn.rearrange("p (b h) d -> p b (h d)", b=NS_TOK))\
                .then_inc(sem("even_stored"), 16)
            pool.dma_start(io["o_ssm"][:, 1:9, :], sm_ssm).then_inc(sem("even_stored"), 16)

            def peer(L):
                pool.wait_ge(sem("h_ready"), 2 * L + 2)
                pool.dma_start(keys, io["keys"][L]).then_inc(sem("keys_loaded"), 16)

                def step(n, s):
                    pool.wait_ge(sem("hot_eq_ready"), n + (L * NT * GS + 1))
                    hot = hot_j[:, hot_slot(s)]
                    pool.tensor_tensor(hot, hot, gT[:, ds(n * GT, GT)].rearrange("p (t a) -> p t a", a=1)
                                       .to_broadcast([P, GT, NKEY]), ALU.mult).then_inc(sem("hot_j_ready"), 1)
                with pool.Fori(0, NT) as n:
                    with pool.Fori(0, GS // GTURN) as i:
                        for s in range(GTURN):
                            step(n * GS + i * GTURN + s, s)
                    step(n * GS + (GS - 1), GTURN)
                with pool.Fori(0, NG // 2) as m:
                    for slot in range(2):
                        pool.wait_ge(sem("vhi_ready"), 2 * m + (L * NG + slot + 1))
                        pool.tensor_tensor(vlo[:, slot], vring[:, slot], vhi[:, slot].bitcast(f32),
                                           ALU.subtract).then_inc(sem("v_ready"), 1)

            peer(0)
            pool.wait_ge(sem("h_ready"), 3)
            pool.dma_start(gbias, io["gbias"].to_broadcast([P, 512])).then_inc(sem("odd_loads"), 16)
            pool.dma_start(sm_gla.rearrange("p a d -> p (a d)"), io["s_gla"]).then_inc(sem("odd_states"), 16)
            pool.wait_ge(sem("odd_group"), GROUPS + 1)
            pool.dma_start(io["o_gla"][:, 0, :], s_gla.rearrange("p h d -> p (h d)")).then_inc(sem("odd_stored"), 16)
            pool.wait_ge(sem("odd_sample"), 1)
            pool.dma_start(io["o_gla"][:, 1:9, :], sm_gla.rearrange("p (b h) d -> p b (h d)", b=NS_TOK))\
                .then_inc(sem("odd_stored"), 16)
            peer(1)
            pool.wait_ge(sem("h_ready"), 5)
            pool.dma_start(io["o_y"], hT[:, :, :]).then_inc(sem("stored"), 16)
            pool.wait_ge(sem("stored"), 16 * 5)
            pool.wait_ge(sem("even_stored"), 32)
            pool.wait_ge(sem("odd_stored"), 32)

        @block.tensor
        def _(pe):
            def mm(out, lhsT, rhs, start=True, stop=True):
                return pe.matmul(out, lhsT, rhs, start=start, stop=stop)

            def norm(k):
                pe.wait_ge(sem("squares_ready"), k + 1)
                for h in range(2):
                    for c in range(KD):
                        last = mm(ps[:, h, 0:TH], ones, nsq[:, c, h * TH:(h + 1) * TH], c == 0, c == KD - 1)
                last.then_inc(sem("ssq_ready"), 1)

            def gemm(name):
                base = BASE[name]
                with pe.Fori(0, BLOCKS[name] // WSLOTS) as i:
                    for u in range(WSLOTS):
                        pe.wait_ge(sem(f"w_loaded{u}"), i * 16 + 16 * (base // WSLOTS + 1))
                        pe.wait_ge(sem("gemm_free"), WSLOTS * i + (base + u + 1))
                        for h in range(2):
                            for c in range(KD):
                                last = mm(ps[:, 2 * (u % 2) + h, 0:TH], wring[:, u, c, :],
                                          hT[:, c, h * TH:(h + 1) * TH], c == 0, c == KD - 1)
                        last.then_inc(sem("gemm_done"), 1)

            def root_sums(count, nblocks, per):
                pe.wait_ge(sem("sq4_ready"), count)
                for b in range(nblocks // per):
                    for h in range(2):
                        for k in range(per):
                            last = mm(ps[:, 2 * b + h, 0:TH], ones, sq_src[0][:, b * per + k, h * TH:(h + 1) * TH],
                                      k == 0, k == per - 1)
                last.then_inc(sem("sums4_ready"), 1)

            sq_src = [sq4]

            pe.wait_ge(sem("params"), 16 * NLOADS)
            norm(0)
            pe.wait_ge(sem("h_ready"), 1)
            gemm("even_in")

            pe.wait_ge(sem("gemm_free"), BASE["even_out"] + 2)
            for n in range(5):
                rows = P if n < 4 else NS_TOK
                for c in range(KD):
                    last = mm(ps[0:rows, 0, 16 * n:16 * n + 16], hT[:, c, n * P:n * P + rows], small_w[:, c, :],
                              c == 0, c == KD - 1)
            last.then_inc(sem("gates_mm"), 1)

            pe.wait_ge(sem("gates_read"), 1)
            root_sums(1, 4, 1)
            root_sums(2, 4, 1)

            with pe.Fori(0, GROUPS) as g:
                def at(name, per=1, k=1):
                    pe.wait_ge(sem(name), g * per + k)
                at("gates_cut")
                for h in range(12):
                    mm(ps[:, h // 4, (h % 4) * P:(h % 4 + 1) * P], g_sl[:, h:h + 1].to_broadcast([P, P]), causal)
                mm(ps[:, 3, 0:12], causal, g_sl)
                for h in range(4):
                    last = mm(ps[:, 4, h * P:(h + 1) * P], b_sl[:, h:h + 1].to_broadcast([P, P]), ident)
                last.then_inc(sem("rows_ready"), 1)
                at("kb_ready")
                for h in range(4):
                    mm(ps[:, 5, h * P:(h + 1) * P], w_sl[:, 4 + h, :], kb[:, h, :])
                for h in range(4):
                    mm(ps[:, 6, h * P:(h + 1) * P], w_sl[:, 4 + h, :], w_sl[:, h, :])
                for h in range(4):
                    pe.transpose(ps[:, 7, h * P:(h + 1) * P], w_sl[:, 4 + h, :], ident)
                for h in range(4):
                    last = pe.transpose(ps[:, 0, h * P:(h + 1) * P], w_sl[:, 8 + h, :], ident)
                last.then_inc(sem("kk_ready"), 1)
                for j in range(2):
                    mm(ps[:, 1, j * P:(j + 1) * P], w_sl[:, 16 + j, :], w_sl[:, 18 + j, :])
                for b in range(4):
                    pe.transpose(ps[:, 2, b * P:(b + 1) * P], w_sl[:, 12 + b, :], ident)
                for j in range(2):
                    last = pe.transpose(ps[:, 3, j * P:(j + 1) * P], w_sl[:, 16 + j, :], ident)
                last.then_inc(sem("ssm_mm"), 1)
                at("p0_ready")
                for h in range(4):
                    last = pe.transpose(ps[:, 5, h * P:(h + 1) * P], pmat[:, h, :], ident)
                last.then_inc(sem("x0_ready"), 1)
                for l in range(1, LEVELS):
                    at("px_ready", LEVELS, l)
                    at("nl_ready", LEVELS - 1, l)
                    for h in range(4):
                        last = mm(ps[:, 6, h * P:(h + 1) * P], nl[:, l - 1, h * P:(h + 1) * P], xmat[:, h, :])
                    last.then_inc(sem("vt_mm"), 1)
                    at("vt_ready", LEVELS - 1, l)
                    for h in range(4):
                        last = mm(ps[:, 7, h * P:(h + 1) * P], vt[:, h, :], pmat[:, h, :])
                    if l < LEVELS - 1:
                        for h in range(4):
                            last = mm(ps[:, 0, h * P:(h + 1) * P], pmat[:, h, :], vt[:, h, :])
                    last.then_inc(sem("z_mm"), 1)
                at("px_ready", LEVELS, LEVELS)
                for h in range(4):
                    last = mm(ps[:, 5, h * P:(h + 1) * P], kbt[:, h, :], pmat[:, h, :])
                last.then_inc(sem("wt_mm"), 1)
                at("wt_ready")
                for h in range(4):
                    mm(ps[:, 6, h * P:(h + 1) * P], pmat[:, h, :], vb[:, h, :], True, False)
                    last = mm(ps[:, 6, h * P:(h + 1) * P], wt[:, h, :], s_dn[:, h, :], False, True)
                last.then_inc(sem("vn_mm"), 1)
                at("vn_ready")
                for h in range(4):
                    mm(ps[:, 7, h * P:(h + 1) * P], s_dn[:, h, :], qi[:, h, :], True, False)
                    mm(ps[:, 7, h * P:(h + 1) * P], vn[:, h, :], qkt[:, h, :], False, True)
                for h in range(4):
                    last = mm(ps[:, 0, h * P:(h + 1) * P], kout[:, h, :], vn[:, h, :])
                last.then_inc(sem("o_mm"), 1)
                at("att_ready")
                for h in range(8):
                    out = ps[64 * (h % 2):64 * (h % 2) + 64, 4, (h // 2) * P:(h // 2 + 1) * P]
                    mm(out, xd[:, h // 2, 64 * (h % 2):64 * (h % 2) + 64], att[:, h, :], True, False)
                    mm(out, s_ssm[:, 64 * h:64 * h + 64], ci[:, h, :], False, True)
                for j in range(2):
                    last = mm(ps[:, 5, j * 256:(j + 1) * 256], btk[:, j, :],
                              xo[:, 2 * j:2 * j + 2, :].rearrange("p a b -> p (a b)"))
                last.then_inc(sem("ssm_out_mm"), 1)

            pe.wait_ge(sem("even_group"), GROUPS + 1)
            pe.wait_ge(sem("diag_ready"), 1)
            mm(ps[:, 0, 0:192], ones[0:NS_TOK, :], sm_diag[0:NS_TOK, :, :].rearrange("p b c -> p (b c)"))\
                .then_inc(sem("bc_mm"), 1)
            pe.wait_ge(sem("even_states"), 32)
            for h in range(4):
                for b in range(NS_TOK):
                    last = mm(ps[:, 1, h * 8 + b:h * 8 + b + 1], sm_dn[:, b * 4 + h, :],
                              conv[:, 4 + h, NP_TOK + b:NP_TOK + b + 1])
            last.then_inc(sem("r_mm"), 1)
            pe.wait_ge(sem("delta_ready"), 1)
            for b in range(NS_TOK):
                for h in range(4):
                    last = mm(ps[:, b, h * P:(h + 1) * P], sm_r[:, h, b:b + 1].to_broadcast([P, P]), ident)
                last.then_inc(sem("delta_rows"), 1)
            pe.wait_ge(sem("dn_states_new"), 1)
            for h in range(4):
                for b in range(NS_TOK):
                    last = mm(ps[:, 0, h * 8 + b:h * 8 + b + 1], sm_dn[:, b * 4 + h, :],
                              conv[:, h, NP_TOK + b:NP_TOK + b + 1])
            last.then_inc(sem("sm_o_mm"), 1)
            pe.wait_ge(sem("sm_o_read"), 1)
            for b in range(NS_TOK):
                for k in range(4):
                    last = mm(ps[:, b, k * P:(k + 1) * P], sm_xd[:, k, b:b + 1].to_broadcast([P, P]), ident)
                last.then_inc(sem("x_rows"), 1)
            pe.wait_ge(sem("ssm_states_new"), 1)
            for k in range(4):
                for b in range(NS_TOK):
                    last = mm(ps[:, 0, k * 8 + b:k * 8 + b + 1], sm_ssm[:, b, k * P:(k + 1) * P],
                              conv[:, 18 + k // 2, NP_TOK + b:NP_TOK + b + 1])
            last.then_inc(sem("sm_y_mm"), 1)

            root_sums(3, 4, 1)
            root_sums(4, 4, 2)
            pe.wait_ge(sem("mix_ready"), 1)
            gemm("even_out")

            def retrieval(L):
                pe.wait_ge(sem("gemm_free"), BASE[f"query{L}"] + BLOCKS[f"query{L}"] + 2)
                pe.wait_ge(sem("keys_loaded"), 16 * (L + 1))
                for n in range(NT):
                    pe.wait_ge(sem("score_free"), L * NT + n + 1)
                    for k in range(2 * PH):
                        last = mm(ps[0:TILE, k // 4, (k % 4) * P:(k % 4 + 1) * P],
                                  query[:, k, n * TILE:(n + 1) * TILE], keys[:, k, :])
                    last.then_inc(sem("score_mm"), 1)
                    if n:
                        chosen(L, n - 1)
                chosen(L, NT - 1)

            def chosen(L, n):
                pe.wait_ge(sem("chosen"), L * NT + n + 1)
                for k in range(3):
                    last = pe.transpose(ps[:, 4, k * TILE:(k + 1) * TILE], res[0:TILE, k, :], ident[0:TILE, 0:TILE])
                last.then_inc(sem("chosen_mm"), 1)

            def step(n, s, L):
                k = n + (L * NT * GS + 1)
                pe.wait_ge(sem("hot_i_ready"), k)
                pe.wait_ge(sem("hot_j_ready"), k)
                pe.wait_ge(sem("gate_free"), k)
                for t in range(GT):
                    last = mm(ps[:, 2 * pair(s) + t // 4, (t % 4) * P:(t % 4 + 1) * P],
                              hot_i[:, hot_slot(s), t, :], hot_j[:, hot_slot(s), t, :])
                last.then_inc(sem("gate_mm"), 1)

            def experts(L):
                with pe.Fori(0, NT) as n:
                    with pe.Fori(0, GS // GTURN) as i:
                        for s in range(GTURN):
                            step(n * GS + i * GTURN + s, s, L)
                    step(n * GS + (GS - 1), GTURN, L)

                def product(bank, w, w_hi, x, x_hi, first, final):
                    for h in range(2):
                        cols = slice(h * TH, (h + 1) * TH)
                        mm(ps[:, bank + h, 0:TH], w_hi, x[:, cols], first, False)
                        mm(ps[:, bank + h, 0:TH], w_hi, x_hi[:, cols], False, False)
                    for h in range(2):
                        cols = slice(h * TH, (h + 1) * TH)
                        last = mm(ps[:, bank + h, 0:TH], w, x_hi[:, cols], False, final)
                    return last

                def pre(slot, m):
                    pe.wait_ge(sem("u_ready"), 2 * m + (L * NG + slot + 1))
                    for j in range(JG):
                        pe.wait_ge(sem("pre_free"), m * (2 * JG) + (slot * JG + L * NKEY + j + 1))
                        for c in range(KD):
                            last = product(2 * j, ulo[:, slot, j * KD + c, :], uhi[:, slot, j * KD + c, :],
                                           hlo[:, c, :], hhi[:, c, :], c == 0, c == KD - 1)
                        last.then_inc(sem("pre_done"), 1)

                def out(slot, m):
                    pe.wait_ge(sem("v_ready"), 2 * m + (L * NG + slot + 1))
                    pe.wait_ge(sem("act_ready"), m * (2 * JG) + (slot * JG + L * NKEY + JG))
                    for c in range(KD):
                        pe.wait_ge(sem("y_free"), m * (2 * KD) + (slot * KD + L * KD * NG + c + 1))
                        cols = slice(c * P, (c + 1) * P)
                        for j in range(JG):
                            last = product(4 + 2 * (c % 2), vlo[:, slot, j, cols], vhi[:, slot, j, cols],
                                           alo[:, slot, j, :], ahi[:, slot, j, :], j == 0, j == JG - 1)
                        last.then_inc(sem("y_done"), 1)

                pe.wait_ge(sem("gate_free"), (L + 1) * NT * GS + 3)
                pe.wait_ge(sem("h_split"), L + 1)
                pre(0, 0)
                with pe.Fori(0, NG // 2 - 1) as m:
                    pre(1, m)
                    out(0, m)
                    pre(0, m + 1)
                    out(1, m)
                pre(1, NG // 2 - 1)
                out(0, NG // 2 - 1)
                out(1, NG // 2 - 1)

            def peer(L):
                norm(2 * L + 1)
                pe.wait_ge(sem("h_ready"), 2 * L + 2)
                gemm(f"query{L}")
                retrieval(L)
                experts(L)

            pe.sem_inc(sem("gate_mm"), 2)
            peer(0)
            norm(2)
            pe.wait_ge(sem("h_ready"), 3)
            gemm("odd_in")

            pe.wait_ge(sem("gemm_free"), BASE["odd_out"] + 2)
            for h in range(2):
                for c in range(KD):
                    last = mm(ps[0:16, h, 0:TH], glr_w[:, c, :], hT[:, c, h * TH:(h + 1) * TH], c == 0, c == KD - 1)
            last.then_inc(sem("glr_mm"), 1)
            pe.wait_ge(sem("glr_ready"), 1)
            for n in range(GROUPS):
                last = mm(ps[:, 4 + n, :], glrT[0:16, n * P:(n + 1) * P], gate2[:, :])
            last.then_inc(sem("gk_mm"), 1)
            for h in range(4):
                last = mm(ps[:, 2, h * 8:(h + 1) * 8], gate2[:, h * P:(h + 1) * P], glrT[0:16, NP_TOK:T])
            last.then_inc(sem("gk_sample_mm"), 1)

            with pe.Fori(0, GROUPS) as g:
                def at(name, per=1, k=1):
                    pe.wait_ge(sem(name), g * per + k)
                at("odd_cut")
                for h in range(4):
                    last = mm(ps[:, 0, h * P:(h + 1) * P], gk_sl[:, h * P:(h + 1) * P], masks[:, GLAMASK, :])
                last.then_inc(sem("bt_mm"), 1)
                for b in range(8):
                    last = pe.transpose(ps[:, 2 + b // 4, (b % 4) * P:(b % 4 + 1) * P], o_sl[:, 8 + b, :], ident)
                last.then_inc(sem("v_mm"), 1)
                at("qk_ready")
                for h in range(4):
                    mm(ps[:, 1, h * P:(h + 1) * P], kt[:, h, :], qt[:, h, :])
                for h in range(4):
                    last = pe.transpose(ps[:, 4, h * P:(h + 1) * P], kc[:, h, :], ident)
                last.then_inc(sem("gatt_mm"), 1)
                at("gatt_ready")
                at("vtok_ready")
                for b in range(8):
                    last = mm(ps[:, 5 + b // 4, (b % 4) * P:(b % 4 + 1) * P], vtok[:, b, :], gatt[:, b // 2, :])
                last.then_inc(sem("intra_mm"), 1)
                at("intra_read")
                for c in range(P // GC):
                    at("s_ready", P // GC, c + 1)
                    for h in range(4):
                        mm(ps[:, 2 + 2 * (c % 2) + h // 2, (h % 2) * 256:(h % 2) * 256 + 256],
                           ko[c * GC:(c + 1) * GC, h, :],
                           vtok[c * GC:(c + 1) * GC, 2 * h:2 * h + 2, :].rearrange("p a b -> p (a b)"))
                    for b in range(8):
                        last = mm(ps[:, 6 + b // 4, (b % 4) * P + c * GC:(b % 4) * P + (c + 1) * GC],
                                  s_gla[:, b // 2, (b % 2) * P:(b % 2 + 1) * P],
                                  qb[:, b // 2, c * GC:(c + 1) * GC])
                    last.then_inc(sem("inter_mm"), 1)

            pe.wait_ge(sem("odd_group"), GROUPS + 1)
            for r in range(2):
                pe.wait_ge(sem("gla_rows_read"), r + 1)
                for b in range(4):
                    for h in range(4):
                        for k in range(2):
                            o = (h * 2 + k) * P
                            last = mm(ps[:, 2 * b + o // 512, o % 512:o % 512 + P],
                                      oproj[:, 8 + 2 * h + k, NP_TOK + 4 * r + b:NP_TOK + 4 * r + b + 1].to_broadcast([P, P]),
                                      ident)
                last.then_inc(sem("gla_rows"), 1)
            pe.wait_ge(sem("gla_states_new"), 1)
            for b in range(NS_TOK):
                for k in range(8):
                    last = mm(ps[:, 0, k * 8 + b:k * 8 + b + 1],
                              sm_gla[:, b * 4 + k // 2, (k % 2) * P:(k % 2 + 1) * P], sm_q[:, k // 2, b:b + 1])
            last.then_inc(sem("gla_o_mm"), 1)
            sq_src[0] = o_sq
            root_sums(5, 8, 2)
            pe.wait_ge(sem("mix_ready"), 2)
            gemm("odd_out")
            peer(1)
            norm(4)

        @block.scalar
        def _(act):
            def f(out, in_, func, **k):
                return act.activation(out, in_, func, **k)

            def norm(k):
                if k:
                    act.wait_ge(sem("x_ready"), k)
                f(nsq, xT[:, :, :], ACT.Square).then_inc(sem("squares_ready"), 1)
                act.wait_ge(sem("ssq_ready"), k + 1)
                f(split(nrt), both(0), ACT.Sqrt, scale=1.0 / D, bias=eps[:, 0:1]).then_inc(sem("root_ready"), 1)

            def copies(name, dst):
                base = BASE[name]
                with act.Fori(0, BLOCKS[name] // WSLOTS) as i:
                    for u in range(WSLOTS):
                        act.wait_ge(sem("gemm_done"), WSLOTS * i + (base + u + 1))
                        f(dst[:, ds(WSLOTS * i + u, 1), :].rearrange("p a (b t) -> p (a b) t", b=2),
                          both(2 * (u % 2)), ACT.Copy).then_inc(sem("gemm_free"), 1)

            act.wait_ge(sem("params"), 16 * NLOADS)
            act.wait_ge(sem("eps_ready"), 1)
            act.sem_inc(sem("gemm_free"), 2)
            act.sem_inc(sem("gate_free"), 3)
            act.sem_inc(sem("pre_free"), 2)
            act.sem_inc(sem("score_free"), 1)
            norm(0)
            copies("even_in", proj)
            act.wait_ge(sem("gates_abs"), 1)
            f(g_abs, g_abs, ACT.Exp, scale=-1.0).then_inc(sem("act_gates"), 1)
            act.wait_ge(sem("act_gates"), 1)
            f(g_abs, g_abs, ACT.Ln, bias=eps[:, 2:3]).then_inc(sem("act_gates"), 1)
            f(neg_a, a_log[:, :], ACT.Exp).then_inc(sem("act_gates"), 1)
            f(beta, g_raw[:, :, 12:16], ACT.Sigmoid).then_inc(sem("act_gates"), 1)
            f(proj[:, 20:28, :], proj[:, 20:28, :], ACT.Silu).then_inc(sem("gates_silu"), 1)
            act.wait_ge(sem("conv_done"), 21)
            f(conv, conv, ACT.Silu).then_inc(sem("conv_silu"), 1)
            act.wait_ge(sem("conv_silu"), 1)
            for r in range(2):
                if r:
                    act.wait_ge(sem("l2_done"), r)
                f(sq4, conv[:, 4 * r:4 * r + 4, :], ACT.Square).then_inc(sem("sq4_ready"), 1)
                act.wait_ge(sem("sums4_ready"), r + 1)
                f(sq4.rearrange("p a (b t) -> p (a b) t", b=2), ps[:, :, 0:TH], ACT.Sqrt,
                  scale=(float(P), 1.0)[r], bias=eps[:, 1 - r:2 - r]).then_inc(sem("roots4_ready"), 1)

            with act.Fori(0, GROUPS) as g:
                def at(name, per=1, k=1):
                    act.wait_ge(sem(name), g * per + k)
                at("even_group")
                f(w_sl, conv[:, :, ds(g * P, P)], ACT.Copy).then_inc(sem("w_cut"), 1)
                at("dec_ready")
                f(dec, dec, ACT.Exp).then_inc(sem("dec_exp"), 1)
                f(egc, gct, ACT.Exp)
                f(erow, ps[:, 0:3, :].rearrange("p b (h i) -> p (b h) i", h=4), ACT.Exp).then_inc(sem("erow_ready"), 1)
                for l in range(1, LEVELS):
                    at("vt_mm", LEVELS - 1, l)
                    f(vt, bank4(6), ACT.Copy).then_inc(sem("vt_ready"), 1)
                at("wt_mm")
                f(wt, bank4(5), ACT.Copy, scale=-1.0).then_inc(sem("wt_ready"), 1)
                at("vn_mm")
                f(vn, bank4(6), ACT.Copy).then_inc(sem("vn_ready"), 1)

            act.wait_ge(sem("even_group"), GROUPS + 1)
            f(sm_val[0:NS_TOK, 0:12], g12[0:NS_TOK, 4, :], ACT.Exp).then_inc(sem("sm_exp"), 1)

            act.wait_ge(sem("even_sample"), 1)
            f(sq4, hT[:, 0:4, :], ACT.Square).then_inc(sem("sq4_ready"), 1)
            act.wait_ge(sem("sums4_ready"), 3)
            f(sq4.rearrange("p a (b t) -> p (a b) t", b=2), ps[:, :, 0:TH], ACT.Sqrt,
              scale=1.0 / P, bias=eps[:, 0:1]).then_inc(sem("roots4_ready"), 1)
            act.wait_ge(sem("ssm_gated"), 1)
            f(sq4, hT[:, 4:8, :], ACT.Square).then_inc(sem("sq4_ready"), 1)
            act.wait_ge(sem("sums4_ready"), 4)
            f(sq4[:, 0:2, :].rearrange("p a (b t) -> p (a b) t", b=2), ps[:, 0:4, 0:TH], ACT.Sqrt,
              scale=1.0 / 256, bias=eps[:, 0:1]).then_inc(sem("roots4_ready"), 1)

            def peer(L):
                norm(2 * L + 1)
                copies(f"query{L}", query)
                with act.Fori(0, NT) as n:
                    act.wait_ge(sem("score_mm"), n + (L * NT + 1))
                    act.wait_ge(sem("topk_free"), n + (L * NT + 1))
                    f(score[0:TILE].rearrange("p (b k) i -> p b (k i)", b=4), ps[0:TILE, 0:4, :], ACT.Copy)\
                        .then_inc(sem("score_ready"), 1)
                    act.wait_ge(sem("score_ready"), n + (L * NT + 1))
                    act.sem_inc(sem("score_free"), 1)
                    act.wait_ge(sem("best_diff"), n + (L * NT + 1))
                    f(bests[0:TILE], posf[0:TILE], ACT.Exp).then_inc(sem("best_exp"), 1)

                def step(tile, slot, k, s):
                    act.wait_ge(sem("gate_mm"), tile * GS + k + (L * NT * GS + 3))
                    f(stage[slot][:, :, ds(k * GT, GT)].rearrange("p j (b t) -> p j b t", b=2),
                      ps[:, 2 * pair(s):2 * pair(s) + 2, :].rearrange("p b (t j) -> p j b t", j=NKEY), ACT.Copy)\
                        .then_inc(sem("gate_free"), 1)

                def tile(n, slot, stored):
                    act.wait_ge(sem(f"stored{slot}"), stored)
                    with act.Fori(0, GS // GTURN) as i:
                        for s in range(GTURN):
                            step(n, slot, GTURN * i + s, s)
                    step(n, slot, GS - 1, GTURN)
                with act.Fori(0, NT // 2) as i:
                    tile(2 * i, 0, 16 * i + 16 * (L * (NT // 2 + 1) + 1))
                    tile(2 * i + 1, 1, 16 * i + 16 * (L * (NT // 2) + 1))
                tile(NT - 1, 0, 16 * (NT // 2) + 16 * (L * (NT // 2 + 1) + 1))

                def cut_u(slot, m):
                    act.wait_ge(sem(f"u_loaded{slot}"), 16 * m + 16 * (L * NG // 2 + 1))
                    f(uhi[:, slot], uring[:, slot], ACT.Copy).then_inc(sem("uhi_ready"), 1)

                def cut_v(slot, m):
                    act.wait_ge(sem(f"v_loaded{slot}"), 16 * m + 16 * (L * NG // 2 + 1))
                    f(vhi[:, slot], vring[:, slot], ACT.Copy).then_inc(sem("vhi_ready"), 1)

                def gelu(slot, m):
                    for j in range(JG):
                        act.wait_ge(sem("pre_done"), m * (2 * JG) + (slot * JG + L * NKEY + j + 1))
                        f(split(aring[:, slot, j, :]), both(2 * j), ACT.Gelu_apprx_tanh).then_inc(sem("pre_free"), 1)

                def cut_a(slot, m):
                    for j in range(JG):
                        act.wait_ge(sem("gated"), m * (2 * JG) + (slot * JG + L * NKEY + j + 1))
                        f(ahi[:, slot, j, :], aring[:, slot, j, :], ACT.Copy).then_inc(sem("ahi_ready"), 1)

                def group(slot, m):
                    act.wait_ge(sem("y_free"), m * (2 * KD) + (slot * KD + (L * NG - 1) * KD + 2))
                    gelu(slot, m)
                    cut_a(slot, m)
                    cut_v(slot, m)

                act.wait_ge(sem("stored1"), 16 * (NT // 2) * (L + 1) + 16)
                f(hhi[:, :, :], hT[:, :, :], ACT.Copy).then_inc(sem("hhi_ready"), 1)
                cut_u(0, 0)
                cut_u(1, 0)
                gelu(0, 0)
                act.wait_ge(sem("stored0"), 16 * (NT // 2 + 1) * (L + 1) + 16)
                cut_a(0, 0)
                cut_v(0, 0)
                with act.Fori(0, NG // 2 - 1) as m:
                    group(1, m)
                    cut_u(0, m + 1)
                    group(0, m + 1)
                    cut_u(1, m + 1)
                group(1, NG // 2 - 1)

            act.wait_ge(sem("even_stored"), 32)
            act.wait_ge(sem("stored"), 64)
            peer(0)
            norm(2)
            copies("odd_in", oproj)
            act.wait_ge(sem("glr_mm"), 1)
            f(split(glrT[0:16]), both(0, 16), ACT.Copy).then_inc(sem("glr_ready"), 1)
            act.wait_ge(sem("gk_abs"), 1)
            f(gk2, gk2, ACT.Exp, scale=-1.0).then_inc(sem("act_gk"), 1)
            f(sm_a2, sm_a2, ACT.Exp, scale=-1.0).then_inc(sem("act_gk"), 1)
            act.wait_ge(sem("act_gk"), 2)
            f(gk2, gk2, ACT.Ln, bias=eps[:, 2:3]).then_inc(sem("act_gk"), 1)
            f(sm_a2, sm_a2, ACT.Ln, bias=eps[:, 2:3]).then_inc(sem("act_gk"), 1)
            act.wait_ge(sem("sm_gk"), 1)
            f(sm_a, sm_a, ACT.Exp, scale=1.0 / 16).then_inc(sem("sm_alpha"), 1)
            f(oproj[:, 16:24, :], oproj[:, 16:24, :], ACT.Silu).then_inc(sem("gates_silu"), 1)
            with act.Fori(0, GROUPS) as g:
                def at(name, per=1, k=1):
                    act.wait_ge(sem(name), g * per + k)
                at("odd_group")
                f(gk_sl, gk[:, ds(g, 1), :].rearrange("p a b -> p (a b)"), ACT.Copy)
                f(o_sl, oproj[:, 0:16, ds(g * P, P)], ACT.Copy).then_inc(sem("odd_cut"), 1)
                at("v_mm")
                f(vtok, ps[:, 2:4, :].rearrange("p b (v i) -> p (b v) i", v=4), ACT.Copy).then_inc(sem("vtok_ready"), 1)
                at("dm_ready")
                f(e_q, dm, ACT.Exp)
                f(e_k, dm, ACT.Exp, scale=-1.0)
                f(e_b, bt, ACT.Exp)
                f(dl, dl, ACT.Exp).then_inc(sem("exps_ready"), 1)
            act.wait_ge(sem("odd_sample"), 1)
            f(o_sq, hT[:, :, :], ACT.Square).then_inc(sem("sq4_ready"), 1)
            act.wait_ge(sem("sums4_ready"), 5)
            f(o_r.rearrange("p a (b t) -> p (a b) t", b=2), ps[:, :, 0:TH], ACT.Sqrt,
              scale=1.0 / 256, bias=eps[:, 0:1]).then_inc(sem("roots4_ready"), 1)
            act.wait_ge(sem("odd_stored"), 32)
            peer(1)
            norm(4)

        @block.vector
        def _(dve):
            tt, stt, tsc, cp = dve.tensor_tensor, dve.scalar_tensor_tensor, dve.tensor_scalar, dve.tensor_copy
            SUB, ADD, MUL = ALU.subtract, ALU.add, ALU.mult

            def signal(name):
                dve.drain()
                dve.sem_inc(sem(name), 1)

            def norm(k):
                dve.wait_ge(sem("root_ready"), k + 1)
                dve.reciprocal(nrt, nrt)
                dve.drain()
                for c in range(KD):
                    last = stt(hT[:, c, :], xT[:, c, :], ln[:, k, c:c + 1], nrt, MUL, MUL)
                last.then_inc(sem("h_ready"), 1)

            def residual(name):
                base = BASE[name]
                with dve.Fori(0, BLOCKS[name] // WSLOTS) as i:
                    for u in range(WSLOTS):
                        dve.wait_ge(sem("gemm_done"), WSLOTS * i + (base + u + 1))
                        x = xT[:, ds(WSLOTS * i + u, 1), :].rearrange("p a (b t) -> p (a b) t", b=2)
                        tt(x, both(2 * (u % 2)), x, ADD).then_inc(sem("gemm_free"), 1)
                signal("x_ready")

            for c, v in enumerate((EPS, P * EPS, 1.0)):
                dve.memset(eps[:, c:c + 1], v)
            dve.memset(g_raw, 0.0)
            signal("eps_ready")
            dve.wait_ge(sem("params"), 16 * NLOADS)
            norm(0)

            with dve.Fori(0, 20) as n:
                dve.wait_ge(sem("gemm_free"), n + 3)

                def blk(v, a, b):
                    return v[:, ds(n, 1), a:b].rearrange("p a t -> p (a t)")
                w = conv_w[:, ds(n, 1), :].rearrange("p a w -> p (a w)")
                tsc(blk(conv, 0, NP_TOK), blk(proj, 0, NP_TOK), w[:, 3:4],
                    conv_b[:, ds(n, 1)], MUL, ADD)
                for s in range(1, 4):
                    dve.drain()
                    stt(blk(conv, s, NP_TOK), blk(proj, 0, NP_TOK - s), w[:, 3 - s:4 - s],
                        blk(conv, s, NP_TOK), MUL, ADD)
                dve.drain()
                dve.sem_inc(sem("conv_done"), 1)
            dve.wait_ge(sem("buf_loaded"), 16)
            x_new = proj[:, 0:20, NP_TOK:T]

            def wcol(k):
                return conv_w[:, :, k:k + 1].to_broadcast([P, 20, NS_TOK])
            tt(acc_c, x_new, wcol(3), MUL)
            for k in range(3):
                tt(tmp_c, buf_c[:, k], wcol(k), MUL)
                dve.drain()
                tt(acc_c, acc_c, tmp_c, ADD)
                dve.drain()
                cp(new_c[:, k], x_new if k == 2 else buf_c[:, k + 1])
                cp(tail_c[:, k, :], proj[:, 0:20, NP_TOK - 3 + k:NP_TOK - 2 + k].rearrange("p n a -> p (n a)"))
            tt(conv[:, :, NP_TOK:T], acc_c, conv_b[:, :].rearrange("p (n a) -> p n a", a=1).to_broadcast([P, 20, NS_TOK]), ADD)
            signal("conv_done")

            dve.wait_ge(sem("gates_mm"), 1)
            cp(g_raw[:, 0:4, :], ps[:, 0, 0:64].rearrange("p (n c) -> p n c", n=4))
            cp(g_raw[0:NS_TOK, 4, :], ps[0:NS_TOK, 0, 64:80])
            signal("gates_read")
            bias = small_b[:, :].rearrange("p (a c) -> p a c", a=1).to_broadcast([P, 5, 16])
            tt(g_raw, g_raw, bias, ADD)
            dve.drain()
            stt(g_abs, g_raw, -1.0, g_raw, MUL, ALU.max)
            tsc(g_sp, g_raw, 0.0, None, ALU.max)
            signal("gates_abs")
            dve.wait_ge(sem("act_gates"), 4)
            tt(g_sp, g_sp, g_abs, ADD)
            tsc(neg_a, neg_a, -1.0, None, MUL)
            dve.drain()
            tt(g12, g_sp[:, :, 0:12], neg_a.rearrange("p (a c) -> p a c", a=1).to_broadcast([P, 5, 12]), MUL)
            for r in range(2):
                dve.wait_ge(sem("roots4_ready"), r + 1)
                dve.reciprocal(sq4, sq4)
                dve.drain()
                tt(conv[:, 4 * r:4 * r + 4, :], conv[:, 4 * r:4 * r + 4, :], sq4, MUL)
                signal("l2_done")
            dve.memset(s_dn, 0.0)
            dve.memset(s_ssm, 0.0)
            signal("even_group")

            def bc(v, n):
                return v.rearrange("p (k a) -> p k a", a=1).to_broadcast([P, v.shape[1], n])

            def at_end(v):
                return v[:, :, P - 1:P]

            with dve.Fori(0, GROUPS) as g:
                def at(name, per=1, k=1):
                    dve.wait_ge(sem(name), g * per + k)

                def cut(v, a, b):
                    return v[:, ds(g, 1), a:b].rearrange("p a c -> p (a c)")
                cp(g_sl, cut(g12, 0, 12))
                cp(b_sl, cut(beta, 0, 4))
                cp(d_sl, cut(g_sp, 4, 12)).then_inc(sem("gates_cut"), 1)
                at("rows_ready")
                cp(gct, ps[:, 3, 0:12])
                dve.drain()
                tt(dec, ps[:, 0:3, :].rearrange("p b (h i) -> p (b h) i", h=4), bc(gct, P), SUB)
                dve.drain()
                tsc(dec, dec, 0.0, None, ALU.min).then_inc(sem("dec_ready"), 1)
                at("erow_ready")
                tt(dec, dec, masks[:, CAUSAL:CAUSAL + 1, :].to_broadcast([P, 12, P]), MUL)
                tt(b_e, b_sl, egc[:, 0:4], MUL)
                at("w_cut")
                tt(kb, w_sl[:, 4:8, :], bank4(4), MUL).then_inc(sem("kb_ready"), 1)
                tt(qi, w_sl[:, 0:4, :], erow[:, 0:4, :], MUL)
                at("kk_ready")
                tt(nmat, bank4(5), dec[:, 0:4, :], MUL)
                dve.drain()
                tt(nmat, nmat, mask4(STRICT), MUL).then_inc(sem("n_ready"), 1)
                tt(qkt, bank4(6), dec[:, 0:4, :], MUL)
                dve.drain()
                tt(pmat, nmat, mask4(LEVEL0), MUL)
                tt(kbt, bank4(7), bc(b_e, P), MUL)
                tt(kout, bank4(7), at_end(dec[:, 0:4, :]).to_broadcast([P, 4, P]), MUL)
                tt(vb, bank4(0), bc(b_sl, P), MUL)
                dve.drain()
                tt(pmat, mask4(IDENT), pmat, SUB).then_inc(sem("p0_ready"), 1)
                at("x0_ready")
                cp(xmat, bank4(5)).then_inc(sem("px_ready"), 1)
                at("ssm_mm")

                def ssm_work(l):
                    if l == 1:
                        cp(btk, ps[:, 3, 0:256].rearrange("p (a b) -> p a b", a=2))
                    if l == 2:
                        tt(xd8, ps[:, 2, :].rearrange("p (h c) -> p h c", h=8), bc(d_sl, 64), MUL)
                    if l == 3:
                        dve.drain()
                        tt(xo8, xd8, at_end(dec[:, 4:12, :]).to_broadcast([P, 8, 64]), MUL)
                    if l == 4:
                        for j in range(2):
                            tt(att[:, 4 * j:4 * j + 4, :], dec[:, 4 + 4 * j:8 + 4 * j, :],
                               ps[:, 1, j * P:(j + 1) * P].rearrange("p (a i) -> p a i", a=1).to_broadcast([P, 4, P]), MUL)
                    if l == 5:
                        for j in range(2):
                            last = tt(ci[:, 4 * j:4 * j + 4, :], erow[:, 4 + 4 * j:8 + 4 * j, :],
                                      w_sl[:, 18 + j:19 + j, :].to_broadcast([P, 4, P]), MUL)
                        last.then_inc(sem("att_ready"), 1)
                for l in range(1, LEVELS):
                    ssm_work(l)
                    at("z_mm", LEVELS - 1, l)
                    last = tt(pmat, pmat, bank4(7), SUB)
                    if l < LEVELS - 1:
                        last = tt(xmat, xmat, bank4(0), SUB)
                    last.then_inc(sem("px_ready"), 1)
                at("o_mm")
                cp(hT[:, 0:4, ds(g * P, P)], bank4(7))
                for h in range(4):
                    stt(s_dn[:, h, :], s_dn[:, h, :], erow[:, h, P - 1:P], ps[:, 0, h * P:(h + 1) * P], MUL, ADD)
                at("ssm_out_mm")
                cp(hT[:, 4:8, ds(g * P, P)], bank4(4))
                s8 = s_ssm.rearrange("p (h c) -> p h c", h=8)
                tt(s8, s8, at_end(erow[:, 4:12, :]).to_broadcast([P, 8, 64]), MUL)
                dve.drain()
                tt(s_ssm, s_ssm, ps[:, 5, :], ADD)
                dve.drain()
                dve.sem_inc(sem("even_group"), 1)

            dve.wait_ge(sem("sm_exp"), 1)
            cp(sm_val[0:NS_TOK, 12:16], beta[0:NS_TOK, 4, :])
            cp(sm_val[0:NS_TOK, 16:24], g_sp[0:NS_TOK, 4, 4:12])
            dve.drain()
            tt(sm_diag[0:NS_TOK], sm_val[0:NS_TOK].rearrange("p (a c) -> p a c", a=1).to_broadcast([NS_TOK, NS_TOK, 24]),
               ident[0:NS_TOK, 0:NS_TOK].rearrange("p (b a) -> p b a", a=1).to_broadcast([NS_TOK, NS_TOK, 24]), MUL)\
                .then_inc(sem("diag_ready"), 1)
            dve.wait_ge(sem("bc_mm"), 1)
            cp(sm_bc, ps[:, 0, 0:192].rearrange("p (b c) -> p b c", b=NS_TOK))
            dve.drain()
            dve.wait_ge(sem("r_mm"), 1)
            tt(sm_r, ps[:, 1, 0:32].rearrange("p (h b) -> p h b", h=4), sm_bc[:, :, 0:4].rearrange("p b h -> p h b"), MUL)
            dve.drain()
            tt(sm_r, conv[:, 8:12, NP_TOK:T], sm_r, SUB)
            dve.drain()
            tt(sm_r, sm_r, sm_bc[:, :, 12:16].rearrange("p b h -> p h b"), MUL).then_inc(sem("delta_ready"), 1)
            for h in range(4):
                v = sm_dn.rearrange("p (b h) d -> p h b d", h=4)[:, h]
                tt(v, v, sm_bc[:, :, h:h + 1].to_broadcast([P, NS_TOK, P]), MUL)
            dve.drain()
            for b in range(NS_TOK):
                dve.wait_ge(sem("delta_rows"), b + 1)
                for h in range(4):
                    s = sm_dn[:, b * 4 + h, :]
                    stt(s, ps[:, b, h * P:(h + 1) * P], conv[:, 4 + h, NP_TOK + b:NP_TOK + b + 1], s, MUL, ADD)
            signal("dn_states_new")
            for half in range(2):
                r = slice(64 * half, 64 * half + 64)
                tt(sm_xd[r], conv[r, 12:16, NP_TOK:T], sm_bc[r, :, 16 + half:24:2].rearrange("p b k -> p k b"), MUL)
            for h in range(8):
                v = sm_ssm[:, :, 64 * h:64 * h + 64]
                tt(v, v, sm_bc[:, :, 4 + h:5 + h].to_broadcast([P, NS_TOK, 64]), MUL)
            dve.wait_ge(sem("sm_o_mm"), 1)
            cp(hT[:, 0:4, NP_TOK:T], ps[:, 0, 0:32].rearrange("p (h b) -> p h b", h=4))
            signal("sm_o_read")
            for b in range(NS_TOK):
                dve.wait_ge(sem("x_rows"), b + 1)
                for j in range(2):
                    s = sm_ssm[:, b, 256 * j:256 * j + 256]
                    stt(s, ps[:, b, 256 * j:256 * j + 256], conv[:, 16 + j, NP_TOK + b:NP_TOK + b + 1], s, MUL, ADD)
            signal("ssm_states_new")
            dve.wait_ge(sem("sm_y_mm"), 1)
            cp(hT[:, 4:8, NP_TOK:T], ps[:, 0, 0:32].rearrange("p (h b) -> p h b", h=4))
            signal("even_sample")

            for k in range(4):
                stt(hT[:, 4 + k, :], conv[:, 12 + k, :], head_w[:, 5 + k:6 + k], hT[:, 4 + k, :], MUL, ADD)
            dve.drain()
            dve.wait_ge(sem("gates_silu"), 1)
            tt(hT[:, 4:8, :], hT[:, 4:8, :], proj[:, 24:28, :], MUL)
            dve.wait_ge(sem("roots4_ready"), 3)
            dve.reciprocal(sq4, sq4)
            dve.drain()
            tt(hT[:, 0:4, :], hT[:, 0:4, :], sq4, MUL)
            signal("ssm_gated")
            stt(hT[:, 0:4, :], hT[:, 0:4, :], head_w[:, 0:1], proj[:, 20:24, :], MUL, MUL)
            dve.wait_ge(sem("roots4_ready"), 4)
            dve.reciprocal(sq4[:, 0:2, :], sq4[:, 0:2, :])
            dve.drain()
            for k in range(4):
                stt(hT[:, 4 + k, :], hT[:, 4 + k, :], head_w[:, 1 + k:2 + k], sq4[:, k // 2, :], MUL, MUL)
            signal("mix_ready")
            residual("even_out")

            def top16(L, n, src, vals, idx, count):
                for k in range(count):
                    dve.max(vals(k)[:, 0:8], src(k))
                dve.drain()
                for k in range(count):
                    dve.max_index(idx(k)[:, 0:8], vals(k)[:, 0:8], src(k))
                dve.drain()
                for k in range(count):
                    dve.match_replace(out=src(k), in_to_replace=vals(k)[:, 0:8], in_values=src(k), imm_value=-3e38)
                dve.drain()
                for k in range(count):
                    dve.max(vals(k)[:, 8:16], src(k))
                dve.drain()
                for k in range(count):
                    dve.max_index(idx(k)[:, 8:16], vals(k)[:, 8:16], src(k))
                dve.drain()

            def peer(L):
                norm(2 * L + 1)
                R = slice(0, TILE)
                dve.wait_ge(sem("iota_ready"), 1)
                dve.wait_ge(sem("keys_loaded"), 16 * (L + 1))
                signal("topk_free")
                with dve.Fori(0, NT) as n:
                    dve.wait_ge(sem("score_ready"), n + (L * NT + 1))
                    cp(iota16, iota[:, 0:TOPK])
                    top16(L, n, lambda k: score[R, k, :], lambda k: topv[R, k, :], lambda k: topi[R, k, :], 2 * PH)
                    dve.sem_inc(sem("topk_free"), 1)
                    cp(topf[R], topi[R])
                    for h in range(PH):
                        tt(cand[R, h, :].rearrange("p (a b) -> p a b", a=TOPK),
                           topv[R, 2 * h, :].rearrange("p (a b) -> p a b", b=1).to_broadcast([TILE, TOPK, TOPK]),
                           topv[R, 2 * h + 1, :].rearrange("p (a b) -> p a b", a=1).to_broadcast([TILE, TOPK, TOPK]), ADD)
                    dve.drain()
                    top16(L, n, lambda k: cand[R, k, :], lambda k: bests[R, k, :], lambda k: bestj[R, k, :], PH)
                    tt(posf[R], bests[R], bests[R, :, 0:1].to_broadcast([TILE, PH, TOPK]), SUB)\
                        .then_inc(sem("best_diff"), 1)
                    dve.wait_ge(sem("best_exp"), n + (L * NT + 1))
                    dve.reduce_sum(ssum[R], bests[R], axis=X)
                    dve.drain()
                    dve.reciprocal(ssum[R], ssum[R])
                    dve.drain()
                    tt(res[R, 2, :].rearrange("p (h k) -> p h k", h=PH), bests[R],
                       ssum[R].rearrange("p (h a) -> p h a", a=1).to_broadcast([TILE, PH, TOPK]), MUL)
                    for side, (op, by) in enumerate(((ALU.logical_shift_right, 4), (ALU.bitwise_and, 15))):
                        tsc(posu[R], bestj[R], by, None, op)
                        dve.drain()
                        cp(posf[R], posu[R])
                        dve.drain()
                        tt(eq[R], posf[R].rearrange("p h (k a) -> p (h k) a", a=1).to_broadcast([TILE, PH * TOPK, TOPK]),
                           iota16[R].rearrange("p (k a) -> p k a", k=1).to_broadcast([TILE, PH * TOPK, TOPK]), ALU.is_equal)
                        dve.drain()
                        for h in range(PH):
                            e = eq[R, h * TOPK:(h + 1) * TOPK, :]
                            tt(e, e, topf[R, 2 * h + side:2 * h + side + 1, :].to_broadcast([TILE, TOPK, TOPK]), MUL)
                        dve.drain()
                        dve.reduce_sum(res[R, side, :], eq[R], axis=X)
                        dve.drain()
                    dve.sem_inc(sem("chosen"), 1)
                    dve.wait_ge(sem("chosen_mm"), n + (L * NT + 1))
                    cols = ds(n * TILE, TILE)
                    cp(idx1T[:, cols], ps[:, 4, 0:TILE])
                    cp(idx2T[:, cols], ps[:, 4, TILE:2 * TILE])
                    cp(gT[:, cols], ps[:, 4, 2 * TILE:3 * TILE])
                    dve.drain()

                def step(n, s):
                    dve.wait_ge(sem("gate_mm"), n + (L * NT * GS + 1))
                    at = ds(n * GT, GT)

                    def hot(idx):
                        return (iota[:, :].rearrange("p (a i) -> p a i", a=1).to_broadcast([P, GT, NKEY]),
                                idx[:, at].rearrange("p (t a) -> p t a", a=1).to_broadcast([P, GT, NKEY]), ALU.is_equal)
                    tt(hot_j[:, hot_slot(s)], *hot(idx2T)).then_inc(sem("hot_eq_ready"), 1)
                    tt(hot_i[:, hot_slot(s)], *hot(idx1T)).then_inc(sem("hot_i_ready"), 1)
                with dve.Fori(0, NT) as n:
                    with dve.Fori(0, GS // GTURN) as i:
                        for s in range(GTURN):
                            step(n * GS + i * GTURN + s, s)
                    step(n * GS + (GS - 1), GTURN)

                def gate(slot, m):
                    dve.wait_ge(sem(f"g_loaded{slot}"), 16 * m + 16 * (L * NG // 2 + 1))
                    for j in range(JG):
                        dve.wait_ge(sem("pre_free"), m * (2 * JG) + (slot * JG + L * NKEY + j + 3))
                        a = aring[:, slot, j, :].rearrange("p (n t) -> p n t", n=NT)
                        tt(a, a, gring[:, slot, :, j, :], MUL).then_inc(sem("gated"), 1)

                def rest_a(slot, m, j):
                    dve.wait_ge(sem("ahi_ready"), m * (2 * JG) + (slot * JG + L * NKEY + j + 1))
                    tt(alo[:, slot, j, :], aring[:, slot, j, :], ahi[:, slot, j, :].bitcast(f32), SUB).then_inc(sem("act_ready"), 1)

                UCUT = 4

                def rest_u(slot, m, k):
                    if k == 0:
                        dve.wait_ge(sem("uhi_ready"), 2 * m + (L * NG + slot + 1))
                    blocks = slice(k * JG * KD // UCUT, (k + 1) * JG * KD // UCUT)
                    last = tt(ulo[:, slot, blocks, :], uring[:, slot, blocks, :], uhi[:, slot, blocks, :].bitcast(f32), SUB)
                    if k == UCUT - 1:
                        last.then_inc(sem("u_ready"), 1)

                def turn(slot, m, nxt=None, nxt_m=None, new_m=None):
                    if nxt is not None:
                        gate(nxt, nxt_m)
                    for c in range(KD):
                        dve.wait_ge(sem("y_done"), m * (2 * KD) + (slot * KD + L * KD * NG + c + 1))
                        tt(split(xT[:, c, :]), both(4 + 2 * (c % 2)), split(xT[:, c, :]), ADD).then_inc(sem("y_free"), 1)
                        if nxt is not None and c < JG:
                            rest_a(nxt, nxt_m, c)
                        if new_m is not None and JG <= c < JG + UCUT:
                            rest_u(slot, new_m, c - JG)
                    dve.drain()

                dve.wait_ge(sem("hhi_ready"), L + 1)
                tt(hlo[:, :, :], hT[:, :, :], hhi[:, :, :].bitcast(f32), SUB).then_inc(sem("h_split"), 1)
                for slot in range(2):
                    for k in range(UCUT):
                        rest_u(slot, 0, k)
                gate(0, 0)
                for j in range(JG):
                    rest_a(0, 0, j)
                with dve.Fori(0, NG // 2 - 1) as m:
                    turn(0, m, 1, m, m + 1)
                    turn(1, m, 0, m + 1, m + 1)
                turn(0, NG // 2 - 1, 1, NG // 2 - 1)
                turn(1, NG // 2 - 1)
                signal("x_ready")

            dve.sem_inc(sem("y_free"), 2)
            peer(0)
            norm(2)

            dve.wait_ge(sem("odd_loads"), 16)
            dve.wait_ge(sem("gk_sample_mm"), 1)
            tt(gk, ps[:, 4:8, :], gbias.rearrange("p (a c) -> p a c", a=1).to_broadcast([P, GROUPS, 512]), ADD)
            tt(sm_a, ps[:, 2, 0:32].rearrange("p (h b) -> p h b", h=4),
               head_w[:, 11:15].rearrange("p (h b) -> p h b", b=1).to_broadcast([P, 4, NS_TOK]), ADD)
            dve.drain()
            stt(gk2, gk, -1.0, gk, MUL, ALU.max)
            stt(sm_a2, sm_a, -1.0, sm_a, MUL, ALU.max)
            tsc(gk, gk, 0.0, None, ALU.min)
            tsc(sm_a, sm_a, 0.0, None, ALU.min)
            signal("gk_abs")
            dve.wait_ge(sem("act_gk"), 4)
            tt(sm_a, sm_a, sm_a2, SUB).then_inc(sem("sm_gk"), 1)
            tt(gk, gk, gk2, SUB)
            dve.drain()
            tsc(gk, gk, 1.0 / 16, None, MUL)
            dve.memset(s_gla, 0.0)
            signal("odd_group")
            dve.sem_inc(sem("s_ready"), 1)
            scale = float(P) ** -0.5

            def chunks(v):
                return v.rearrange("p h (c i) -> p (h c) i", i=GC)
            with dve.Fori(0, GROUPS) as g:
                def at(name, per=1, k=1):
                    dve.wait_ge(sem(name), g * per + k)
                at("bt_mm")
                cp(bt, bank4(0))
                dve.drain()
                b16 = chunks(bt)
                tt(chunks(dm), b16, b16[:, :, GC // 2 - 1:GC // 2].to_broadcast([P, 16, GC]), SUB)
                tt(chunks(dl), b16[:, :, GC - 1:GC].to_broadcast([P, 16, GC]), b16, SUB).then_inc(sem("dm_ready"), 1)
                at("odd_cut")
                at("exps_ready")
                stt(qt, o_sl[:, 0:4, :], scale, e_q, MUL, MUL)
                tt(kt, o_sl[:, 4:8, :], e_k, MUL)
                tt(kc, o_sl[:, 4:8, :], dl, MUL).then_inc(sem("qk_ready"), 1)
                stt(qb, o_sl[:, 0:4, :], scale, e_b, MUL, MUL)
                at("gatt_mm")
                tsc(gatt, bank4(1), BIG, -BIG, ALU.min, ALU.max)
                cp(ko, bank4(4))
                dve.drain()
                tt(gatt, gatt, mask4(GLAMASK), MUL).then_inc(sem("gatt_ready"), 1)
                at("intra_mm")
                o = hT[:, :, ds(g * P, P)]
                cp(o, ps[:, 5:7, :].rearrange("p b (v i) -> p (b v) i", v=4)).then_inc(sem("intra_read"), 1)
                for c in range(P // GC):
                    at("inter_mm", P // GC, c + 1)
                    for h in range(4):
                        last = stt(s_gla[:, h, :], s_gla[:, h, :], e_b[:, h, (c + 1) * GC - 1:(c + 1) * GC],
                                   ps[:, 2 + 2 * (c % 2) + h // 2, (h % 2) * 256:(h % 2) * 256 + 256], MUL, ADD)
                    last.then_inc(sem("s_ready"), 1)
                tt(o, o, ps[:, 6:8, :].rearrange("p b (v i) -> p (b v) i", v=4), ADD)
                dve.drain()
                dve.sem_inc(sem("odd_group"), 1)

            tsc(sm_q, oproj[:, 0:4, NP_TOK:T], scale, None, MUL)
            signal("gla_rows_read")
            dve.wait_ge(sem("sm_alpha"), 1)
            dve.wait_ge(sem("odd_states"), 16)
            for h in range(4):
                v = sm_gla.rearrange("p (b h) d -> p h b d", h=4)[:, h]
                tt(v, v, sm_a[:, h, :].rearrange("p (b a) -> p b a", a=1).to_broadcast([P, NS_TOK, 256]), MUL)
            dve.drain()
            for r in range(2):
                dve.wait_ge(sem("gla_rows"), r + 1)
                for b in range(4):
                    for h in range(4):
                        s = sm_gla[:, (4 * r + b) * 4 + h, :]
                        stt(s, ps[:, 2 * b + h // 2, (h % 2) * 256:(h % 2) * 256 + 256],
                            oproj[:, 4 + h, NP_TOK + 4 * r + b:NP_TOK + 4 * r + b + 1], s, MUL, ADD)
                signal("gla_rows_read")
            dve.sem_inc(sem("gla_states_new"), 1)
            dve.wait_ge(sem("gla_o_mm"), 1)
            cp(hT[:, :, NP_TOK:T], ps[:, 0, 0:64].rearrange("p (k b) -> p k b", k=8))
            signal("odd_sample")
            dve.wait_ge(sem("roots4_ready"), 5)
            dve.wait_ge(sem("gates_silu"), 2)
            dve.reciprocal(o_r, o_r)
            dve.drain()
            for k in range(8):
                stt(hT[:, k, :], hT[:, k, :], head_w[:, 9 + k % 2:10 + k % 2], o_r[:, k // 2, :], MUL, MUL)
            dve.drain()
            tt(hT[:, :, :], hT[:, :, :], oproj[:, 16:24, :], MUL)
            signal("mix_ready")
            residual("odd_out")
            peer(1)
            norm(4)


INPUTS = dict(
    masks=(P, NMASK, P), xT=(P, KD, T), ln=(P, 5, KD), conv_w=(P, 20, 4), conv_b=(P, 20), small_w=(P, KD, 16),
    glr_w=(P, KD, 16), head_w=(P, 16), gate2=(16, 512), small_b=(1, 16), a_log=(1, 12), gbias=(1, 512),
    conv_buf=(P, 3, 20, NS_TOK), s_dn=(P, 32 * P), s_ssm=(P, NS_TOK * 512), s_gla=(P, 32 * 256),
    keys0=(P, 16, NKEY), keys1=(P, 16, NKEY), weights=(NBLOCKS, P, D),
    u0=(NG, P, JG * D), u1=(NG, P, JG * D), v0=(NG, P, JG * D), v1=(NG, P, JG * D))
OUTPUTS = dict(
    o_y=(P, KD, T), o_conv_p=(P, 3, 20), o_conv_s=(P, 3, 20, NS_TOK), o_dn=(P, 9, 512), o_ssm=(P, 9, 512),
    o_gla=(P, 9, 1024))


def constant_masks():
    import numpy as np
    r, c = np.arange(P)[:, None], np.arange(P)[None, :]
    m = [r == c, r == r + 0 * c, c >= r, c > r]
    for l in range(LEVELS):
        s = 1 << l
        m.append((r // (2 * s) == c // (2 * s)) & (r // s < c // s))
    m.append((r // GC == c // GC) & (c >= r))
    return np.ascontiguousarray(np.stack(m, axis=1).astype(np.float32))


def kernel(**inp):
    import numpy as np
    import concourse.bacc as bacc
    from concourse.bass_utils import run_bass_kernel_spmd

    A = {k: np.asarray(v) for k, v in inp.items()}
    f = np.ascontiguousarray

    def rows(w):
        return w.reshape(KD, P, -1).transpose(1, 0, 2)

    def blocks(w):
        return w.reshape(KD, P, -1, P).transpose(2, 1, 0, 3).reshape(-1, P, D)

    def cols(v):
        return v.reshape(-1, P).T

    we, wo = A["w_in_even"][0], A["w_in_odd"][0]
    qkv, a_in, b_in, gate, z, xbc, dt_in = np.split(we, [1536, 1540, 1544, 2056, 2568, 3592], axis=1)
    qk, v_in, glr, og = np.split(wo, [1024, 2048, 2064], axis=1)
    x = np.concatenate([A["x_prompt"][0], A["x_sample"][:, 0]], axis=0)
    zero = np.zeros
    keys = [np.stack([A["peer_keys1"][l], A["peer_keys2"][l]], axis=1).reshape(16, NKEY, P).transpose(2, 0, 1)
            for l in range(2)]
    conv_buf = np.concatenate([A["state_dn_conv"][0], A["state_ssm_conv"][0]], axis=2)
    ins = dict(
        masks=constant_masks(),
        xT=x.T.reshape(KD, P, T).transpose(1, 0, 2),
        ln=np.stack([A["ln_mix"][0], A["ln_ffn"][0], A["ln_mix"][1], A["ln_ffn"][1], A["ln_final"]])
        .reshape(5, KD, P).transpose(2, 0, 1),
        conv_w=np.concatenate([A["dn_conv_w"][0], A["ssm_conv_w"][0]], axis=1).reshape(4, 20, P).transpose(2, 1, 0),
        conv_b=np.concatenate([zero((12, P), np.float32), A["ssm_conv_b"][0].reshape(8, P)], axis=0).T,
        small_w=rows(np.concatenate([a_in, dt_in, b_in], axis=1)),
        glr_w=rows(glr),
        head_w=np.concatenate([cols(A["dn_norm_w"][0]), cols(A["ssm_norm_w"][0]),
                               cols(np.repeat(A["ssm_d"][0], 64)), cols(A["gla_norm_w"][0]),
                               cols(A["gla_b_gate"][0]), zero((P, 1), np.float32)], axis=1),
        gate2=A["gla_w_gate2"][0],
        small_b=np.concatenate([A["dn_dt_bias"][0], A["ssm_dt_bias"][0], zero(4, np.float32)])[None],
        a_log=np.concatenate([A["dn_a_log"][0], A["ssm_a_log"][0]])[None],
        gbias=A["gla_b_gate"][0][None],
        conv_buf=conv_buf.reshape(NS_TOK, 3, 20, P).transpose(3, 1, 2, 0),
        s_dn=A["state_dn"][0].transpose(2, 0, 1, 3).reshape(P, -1),
        s_ssm=A["state_ssm"][0].transpose(3, 0, 1, 2).reshape(P, -1),
        s_gla=A["state_gla"][0].transpose(2, 0, 1, 3).reshape(P, -1),
        keys0=keys[0], keys1=keys[1],
        weights=np.concatenate([blocks(np.concatenate([qkv, xbc, gate, z], axis=1)), blocks(A["w_out_even"][0]),
                                blocks(A["peer_w_q"][0]), blocks(np.concatenate([qk, v_in, og], axis=1)),
                                blocks(A["w_out_odd"][0]), blocks(A["peer_w_q"][1])], axis=0),
    )
    for l in range(2):
        u = A["peer_u"][l].reshape(NKEY, NG, JG, KD, P)
        ins[f"u{l}"] = u.transpose(1, 4, 2, 3, 0).reshape(NG, P, JG * D)
        v = A["peer_v"][l].reshape(NKEY, NG, JG, D)
        ins[f"v{l}"] = v.transpose(1, 0, 2, 3).reshape(NG, P, JG * D)
    ins = {k: f(v) for k, v in ins.items()}

    nc = bacc.Bacc("TRN2", target_bir_lowering=False, num_devices=1)
    f32 = mybir.dt.float32
    io = {k: nc.dram_tensor("in_" + k, s, f32, kind="ExternalInput").ap() for k, s in INPUTS.items()}
    for k, s in INPUTS.items():
        assert ins[k].shape == s and ins[k].dtype == np.float32, (k, ins[k].shape, s)
    io.update({k: nc.dram_tensor("out_" + k, s, f32, kind="ExternalOutput").ap() for k, s in OUTPUTS.items()})
    for k in ("keys", "u", "v"):
        io[k] = [io[f"{k}0"], io[f"{k}1"]]
    io["gates"] = nc.dram_tensor("gates", (P, NT, NKEY, TILE), f32, kind="Internal").ap()
    build_program(nc, io)
    r = run_bass_kernel_spmd(nc, [{"in_" + k: v for k, v in ins.items()}], core_ids=[0]).results[0]

    y = r["out_o_y"].transpose(2, 1, 0).reshape(T, D)
    tail = r["out_o_conv_p"].transpose(1, 2, 0).reshape(1, 1, 3, 2560)
    new = r["out_o_conv_s"].transpose(3, 1, 2, 0).reshape(1, NS_TOK, 3, 2560)
    dn = r["out_o_dn"].reshape(P, 9, 4, P).transpose(1, 2, 0, 3)[None]
    ssm = r["out_o_ssm"].reshape(P, 9, 8, 64).transpose(1, 2, 3, 0)[None]
    gla = r["out_o_gla"].reshape(P, 9, 4, 256).transpose(1, 2, 0, 3)[None]
    return (f(y[None, :NP_TOK]), f(y[NP_TOK:, None]), f(tail[..., :1536]), f(dn[:, :1]), f(tail[..., 1536:]),
            f(ssm[:, :1]), f(gla[:, :1]), f(new[..., :1536]), f(dn[:, 1:]), f(new[..., 1536:]), f(ssm[:, 1:]),
            f(gla[:, 1:]))
```

```python
import concourse.bass as bass
from concourse import mybir
from contextlib import ExitStack

P = 128
D = 1024
KD = D // P
NP_TOK = 512
NS_TOK = 8
T = NP_TOK + NS_TOK
TH = T // 2
GROUPS = NP_TOK // P
EPS = 1e-6
NKEY = 128
TOPK = 16
PH = 8
TILE = 104
NT = T // TILE
JG = 2
NG = NKEY // JG
AT = 4
AG = AT * NT
NN = NG - AG
VSLOT = (0, 2, 1, 3)
ASLOT = (2, 3, 0, 1)
GT = 8
GS = TILE // GT
GTURN = 6
WSLOTS = 4
GEMMS = [("even_in", 28), ("even_out", 8), ("query0", 16), ("odd_in", 24), ("odd_out", 8), ("query1", 16)]
BLOCKS = dict(GEMMS)
BASE = {name: sum(b for _, b in GEMMS[:k]) for k, (name, _) in enumerate(GEMMS)}
NBLOCKS = sum(BLOCKS.values())
IDENT, ONES, CAUSAL, STRICT, LEVEL0 = 0, 1, 2, 3, 4
LEVELS = 7
GLAMASK = LEVEL0 + LEVELS
NMASK = GLAMASK + 1
GC = 32
BIG = 1e30
ARENA = 38224
NLOADS = 11


def build_program(nc, io):
    f32, f16, u32 = mybir.dt.float32, mybir.dt.float16, mybir.dt.uint32
    f32r = mybir.dt.float32r
    ALU = mybir.AluOpType
    ACT = mybir.ActivationFunctionType
    X = mybir.AxisListType.X
    ds = bass.ds

    with ExitStack() as ctx:
        def sb(name, shape, dt=f32):
            return ctx.enter_context(nc.sbuf_tensor(name, shape, dt))

        sems = {}

        def sem(name):
            if name not in sems:
                sems[name] = ctx.enter_context(nc.semaphore(name))
            return sems[name]

        xT = sb("xT", [P, KD, T])
        h_at = nc.sbuf_base
        hT = sb("hT", [P, KD, T])
        assert nc.sbuf_base == h_at + 4 * KD * T
        wring = sb("wring", [P, WSLOTS, KD, P])
        masks = sb("masks", [P, NMASK, P])
        ln = sb("ln", [P, 5, KD])
        iota = sb("iota", [P, NKEY], f16)
        eps = sb("eps", [P, 4])
        conv_w = sb("conv_w", [P, 20, 4])
        conv_b = sb("conv_b", [P, 20])
        small_w = sb("small_w", [P, KD, 16])
        glr_w = sb("glr_w", [P, KD, 16])
        small_b = sb("small_b", [P, 16])
        a_log = sb("a_log", [P, 12])
        head_w = sb("head_w", [P, 16])
        gate2 = sb("gate2", [16, 512])
        arena_at = nc.sbuf_base
        arena = sb("arena", [P, ARENA])
        assert nc.sbuf_base == arena_at + 4 * ARENA
        ps = ctx.enter_context(nc.psum_tensor("ps", [P, 8, 512], f32))
        ident = masks[:, IDENT, :]
        ones = masks[:, ONES, :]
        causal = masks[:, CAUSAL, :]

        def mask4(k):
            return masks[:, k:k + 1, :].to_broadcast([P, 4, P])

        class Region:

            def __init__(self, at, end=ARENA):
                self.at, self.end = at, end

            def take_r(self, name, *shape):
                at = arena_at + 4 * self.at
                self.take(*shape)
                return at_byte(name, at, *shape)

            def take(self, *shape, dt=f32):
                n = 1
                for x in shape:
                    n *= x
                words = n // 2 if dt == f16 else n
                v = arena[:, self.at:self.at + words]
                self.at += words
                assert self.at <= self.end, (self.at, self.end)
                if dt != f32:
                    v = v.bitcast(dt)
                if len(shape) == 2:
                    v = v.rearrange("p (a b) -> p a b", a=shape[0])
                if len(shape) == 3:
                    v = v.rearrange("p (a b c) -> p a b c", a=shape[0], b=shape[1])
                return v

        def at_byte(name, at, *shape):
            return nc.alloc_sbuf_tensor_at(name, [P, *shape], f32r, offset=at)

        def both(bank, rows=P):
            return ps[0:rows, bank:bank + 2, 0:TH]

        def split(v):
            return v.rearrange("p (b t) -> p b t", b=2)

        def bank4(bank):
            return ps[:, bank, :].rearrange("p (h i) -> p h i", h=4)

        ev = Region(0)
        proj = ev.take(28, T)
        conv = ev.take(20, T)
        sq4 = ev.take(4, T)
        g_raw = ev.take(5, 16)
        g_abs = ev.take(5, 16)
        g_sp = ev.take(5, 16)
        g12 = ev.take(5, 12)
        beta = ev.take(5, 4)
        neg_a = ev.take(12)
        s_dn = ev.take(4, P)
        s_ssm = ev.take(512)
        buf_c = ev.take(3, 20, NS_TOK)
        new_c = ev.take(3, 20, NS_TOK)
        acc_c = ev.take(20, NS_TOK)
        tmp_c = ev.take(20, NS_TOK)
        tail_c = ev.take(3, 20)
        (kb, nmat, qkt, kbt, kout, vb, pmat, xmat, vt, wt, vn, qi, xd, xo) = [ev.take(4, P) for _ in range(14)]
        ci = ev.take(8, P)
        xd8, xo8 = [v.rearrange("p b (a c) -> p (b a) c", a=2) for v in (xd, xo)]
        sc = Region(0, 20 * T)
        w_sl = sc.take(20, P)
        g_sl = sc.take(12)
        b_sl = sc.take(4)
        d_sl = sc.take(8)
        gct = sc.take(12)
        egc = sc.take(12)
        dec = sc.take(12, P)
        erow = sc.take(12, P)
        nl = sc.take(6, 512)
        btk = sc.take(2, P)
        att = sc.take(8, P)
        b_e = sc.take(4)
        sm = Region(0, 20 * T)
        sm_dn = wring[:, :, :, :].rearrange("p s k c -> p (s k) c")
        sm_ssm = sm.take(NS_TOK, 512)
        sm_r = sm.take(4, NS_TOK)
        sm_xd = sm.take(4, NS_TOK)
        sm_val = sm.take(24)
        sm_diag = sm.take(NS_TOK, 24)
        sm_bc = sm.take(NS_TOK, 24)

        od = Region(0)
        oproj = od.take(24, T)
        glrT = od.take(T)
        gk = od.take(GROUPS, 512)
        gk2 = od.take(GROUPS, 512)
        gbias = od.take(512)
        s_gla = od.take(4, 256)
        o_sl = od.take(16, P)
        gk_sl = od.take(512)
        (bt, dm, dl, e_q, e_k, e_b, kc, ko, gatt) = [od.take(4, P) for _ in range(9)]
        (qt, kt, qb) = [od.take(4, P) for _ in range(3)]
        vtok = od.take(8, P)
        sm_gla = od.take(32, 256)
        sm_a = od.take(4, NS_TOK)
        sm_a2 = od.take(4, NS_TOK)
        sm_q = od.take(4, NS_TOK)
        osq = Region(0, 16 * T)
        o_sq = osq.take(8, T)
        o_r = osq.take(4, T)

        pr = Region(0)
        ulo = Region(pr.at).take_r("u_lo", 2, JG * KD, P)
        uring = pr.take(2, JG * KD, P)
        idx1T = pr.take(T, dt=f16)
        idx2T = pr.take(T, dt=f16)
        gT = pr.take(T)
        r0 = pr.at
        stage = [pr.take(NKEY, TILE) for _ in range(2)]
        h0 = pr.at
        hot_j = pr.take(4, GT, NKEY)
        hot_i = wring[:, :, :, :]
        assert (WSLOTS, KD, P) == (4, GT, NKEY)

        def place(s):
            return s % 3 if s < GTURN else 3
        ex = Region(r0 + NKEY * TILE, h0)
        hhi = ex.take_r("h_hi", KD, T)
        uhi = ex.take_r("u_hi", 2, JG * KD, P)
        vlo = Region(ex.at).take_r("v_lo", 2, JG, D)
        vring = ex.take(2, JG, D)
        nm = Region(r0 + NKEY * TILE)
        nsq = nm.take(2, T)
        nacc = nm.take(T)
        nrt = nm.take(T)
        ex = Region(r0, r0 + NKEY * TILE)
        vhi = ex.take_r("v_hi", 2, JG, D)
        gring = ex.take(2, NT * JG, TILE).rearrange("p s (n j) t -> p s n j t", j=JG)
        alo2 = Region(ex.at).take_r("a_lo2", 2, JG, T)
        aring2 = ex.take(2, JG, T)
        ahi2 = ex.take_r("a_hi2", 2, JG, T)
        ex = Region(h0)
        alo = Region(ex.at).take_r("a_lo", 2, JG, T)
        hlo = at_byte("h_lo", h_at, KD, T)
        aring = ex.take(2, JG, T)
        ahi = ex.take_r("a_hi", 2, JG, T)

        def a_of(slot):
            return [v[:, slot % 2] for v in ((aring, ahi, alo) if slot < 2 else (aring2, ahi2, alo2))]

        tk = Region(r0)
        query = tk.take(2 * PH, T)
        score = tk.take(2 * PH, NKEY)
        cand = tk.take(PH, TOPK * TOPK)
        eq = tk.take(PH * TOPK, TOPK)
        topv = tk.take(2 * PH, TOPK)
        topi = tk.take(2 * PH, TOPK, dt=u32)
        topf = tk.take(2 * PH, TOPK)
        keys = tk.take(2 * PH, NKEY)
        bests = tk.take(PH, TOPK)
        bestj = tk.take(PH, TOPK, dt=u32)
        posu = tk.take(PH, TOPK, dt=u32)
        posf = tk.take(PH, TOPK)
        diff = tk.take(PH, TOPK)
        query_tile = tk.take(2 * PH, TILE)
        res = tk.take(3, P)
        ahead = tk.take(2, JG, T)
        assert tk.at <= h0
        ssum = tk.take(PH)
        iota16 = tk.take(TOPK)

        block = ctx.enter_context(nc.Block())

        @block.sync
        def _(sp):
            n = 0
            for dst, src in ((masks[:, :, :], io["masks"]), (xT[:, :, :], io["xT"]), (ln[:, :, :], io["ln"]),
                             (conv_w[:, :, :], io["conv_w"]), (conv_b[:, :], io["conv_b"]),
                             (small_w[:, :, :], io["small_w"]), (glr_w[:, :, :], io["glr_w"]),
                             (head_w[:, :], io["head_w"]), (gate2[:, :], io["gate2"]),
                             (small_b[:, :], io["small_b"].to_broadcast([P, 16])),
                             (a_log[:, :], io["a_log"].to_broadcast([P, 12]))):
                sp.dma_start(dst, src).then_inc(sem("params"), 16)
                n += 1
            assert n == NLOADS

            def load_block(i, u, base):
                sp.dma_start(wring[:, u, :, :].rearrange("p k c -> p (k c)"),
                             io["weights"][ds(WSLOTS * i + (base + u), 1)].rearrange("a p c -> (a p) c"))\
                    .then_inc(sem(f"w_loaded{u}"), 16)

            def stream(name):
                base = BASE[name]
                if base == 0:
                    for u in range(WSLOTS):
                        load_block(0, u, 0)
                with sp.Fori(int(base == 0), BLOCKS[name] // WSLOTS) as i:
                    for u in range(WSLOTS):
                        sp.wait_ge(sem("gemm_done"), WSLOTS * i + (base + u - WSLOTS + 1))
                        load_block(i, u, base)

            def experts(L):
                def load(what, ring, slot, g, place=None):
                    sp.dma_start(ring[:, slot].rearrange("p a b -> p (a b)"),
                                 io[what][L][ds(g, 1)].rearrange("a p c -> (a p) c"))\
                        .then_inc(sem(f"{what}_loaded{slot if place is None else place}"), 16)

                def load_v(place, g):
                    load("v", vring if place < 2 else uring, place % 2, g, place)

                def load_gates(slot, g):
                    sp.dma_start(gring[:, slot],
                                 io["gates"][:, :, ds(g * JG, JG), :]).then_inc(sem(f"g_loaded{slot}"), 16)

                def store_gates(n, slot):
                    sp.wait_ge(sem("gate_free"), n * GS + (L * NT * GS + GS + 3))
                    sp.dma_start(io["gates"][:, ds(n, 1)].rearrange("p a j t -> p (a j t)"),
                                 stage[slot].rearrange("p j t -> p (j t)")).then_inc(sem(f"stored{slot}"), 16)

                sp.wait_ge(sem("h_ready"), 2 * L + 2)
                for slot in range(2):
                    load("u", uring, slot, slot)
                with sp.Fori(0, AG // 2) as m:
                    for slot in range(2):
                        sp.wait_ge(sem("half_done"), m * (4 * JG) + (2 * JG * (slot + 1) + 2 * L * AG * JG))
                        load("u", uring, slot, 2 * m + (slot + 2))
                        sp.wait_ge(sem("half_free"), m * (4 * JG) + (2 * JG * (slot + 1) + 2 * L * AG * JG + 2))
                        sp.dma_start(io["ahead"][ds(2 * m + slot, 1)].rearrange("a p c -> (a p) c"),
                                     ahead[:, slot].rearrange("p j t -> p (j t)")).then_inc(sem(f"put{slot}"), 16)
                with sp.Fori(0, NT // 2) as i:
                    store_gates(2 * i, 0)
                    store_gates(2 * i + 1, 1)
                store_gates(NT - 1, 0)
                sp.wait_ge(sem("stored1"), 16 * (NT // 2) * (L + 1) + 16)
                for slot in range(2):
                    load_v(slot, AG + slot)
                sp.wait_ge(sem("stored0"), 16 * (NT // 2 + 1) * (L + 1) + 16)
                for slot in range(2):
                    load_gates(slot, AG + slot)
                with sp.Fori(1, NN // 2) as m:
                    for slot in range(2):
                        sp.wait_ge(sem("pre_done"), m * (2 * JG) + (JG * (slot - 1) + L * NN * JG))
                        load("u", uring, slot, 2 * m + (slot + AG))
                        sp.wait_ge(sem("gated"), m * (2 * JG) + (JG * (slot - 1) + L * NKEY))
                        load_gates(slot, 2 * m + (slot + AG))
                        sp.wait_ge(sem("y_done"), m * (2 * KD) + (KD * (slot - 1) + L * KD * NG))
                        load_v(slot, 2 * m + (slot + AG))

                for slot in range(2):
                    sp.wait_ge(sem(f"put{slot}"), 16 * (AG // 2) * (L + 1) + 16)

                def load_act(slot, g):
                    sp.dma_start(a_of(slot)[0].rearrange("p j t -> p (j t)"),
                                 io["ahead"][ds(g, 1)].rearrange("a p c -> (a p) c"))\
                        .then_inc(sem(f"a_loaded{slot}"), 16)

                def turn(slot, g):
                    sp.wait_ge(sem("gated"), g * JG + (L * NKEY + (NN - 1) * JG))
                    load_gates(slot, g)
                    sp.wait_ge(sem("y_done"), g * KD + (L * KD * NG + (NN - 1) * KD))
                load_act(ASLOT[0], 0)
                load_act(ASLOT[1], 1)
                turn(0, 0)
                load_v(VSLOT[0], 0)
                load_v(VSLOT[1], 1)
                load_act(ASLOT[2], 2)
                turn(1, 1)
                load_v(VSLOT[2], 2)
                load_v(VSLOT[3], 3)
                load_act(ASLOT[3], 3)
                with sp.Fori(0, AG // 4 - 1) as m:
                    for k in range(4):
                        turn(k % 2, 4 * m + (k + 2))
                        load_act(ASLOT[k], 4 * m + (k + 4))
                        load_v(VSLOT[k], 4 * m + (k + 4))
                for k in range(2):
                    turn(k, AG - 2 + k)

            for slot in range(2):
                sp.sem_inc(sem(f"stored{slot}"), 16)
                sp.sem_inc(sem(f"put{slot}"), 16)
            stream("even_in")
            sp.wait_ge(sem("dn_stored"), 16)
            sp.wait_ge(sem("sm_o_mm"), 1)
            stream("even_out")
            stream("query0")
            experts(0)
            stream("odd_in")
            stream("odd_out")
            stream("query1")
            experts(1)

        @block.gpsimd
        def _(pool):
            pool.iota(iota[:, :], pattern=[[1, NKEY]], base=0, channel_multiplier=0,
                      allow_small_or_imprecise_dtypes=True).then_inc(sem("iota_ready"), 1)
            pool.dma_start(buf_c, io["conv_buf"]).then_inc(sem("buf_loaded"), 16)
            pool.wait_ge(sem("conv_done"), 21)
            pool.dma_start(io["o_conv_s"], new_c).then_inc(sem("stored"), 16)
            pool.dma_start(io["o_conv_p"], tail_c).then_inc(sem("stored"), 16)
            pool.wait_ge(sem("gemm_done"), BLOCKS["even_in"])
            pool.dma_start(sm_dn.rearrange("p a d -> p (a d)"), io["s_dn"]).then_inc(sem("dn_states"), 16)
            with pool.Fori(0, GROUPS) as g:
                pool.wait_ge(sem("n_ready"), g + 1)
                for l in range(1, LEVELS):
                    pool.tensor_tensor(nl[:, l - 1, :].rearrange("p (h i) -> p h i", h=4), nmat, mask4(LEVEL0 + l),
                                       ALU.mult).then_inc(sem("nl_ready"), 1)
            pool.wait_ge(sem("even_group"), GROUPS + 1)
            pool.dma_start(io["o_dn"][:, 0, :], s_dn.rearrange("p h d -> p (h d)")).then_inc(sem("stored"), 16)
            pool.dma_start(io["o_ssm"][:, 0, :], s_ssm).then_inc(sem("stored"), 16)
            pool.dma_start(sm_ssm.rearrange("p a d -> p (a d)"), io["s_ssm"]).then_inc(sem("even_states"), 16)
            pool.wait_ge(sem("dn_states_new"), 1)
            pool.dma_start(io["o_dn"][:, 1:9, :], sm_dn.rearrange("p (b h) d -> p b (h d)", b=NS_TOK))\
                .then_inc(sem("dn_stored"), 16)
            pool.wait_ge(sem("even_sample"), 1)
            pool.dma_start(io["o_ssm"][:, 1:9, :], sm_ssm).then_inc(sem("even_stored"), 16)

            def peer(L):
                pool.wait_ge(sem("h_ready"), 2 * L + 2)
                pool.dma_start(keys, io["keys"][L]).then_inc(sem("keys_loaded"), 16)
                pool.wait_ge(sem("gemm_free"), BASE[f"query{L}"] + BLOCKS[f"query{L}"] + 2)
                with pool.Fori(0, NT) as n:
                    pool.wait_ge(sem("score_mm"), n + (L * NT + 1))
                    pool.tensor_copy(query_tile, query[:, :, ds(n * TILE, TILE)]).then_inc(sem("query_ready"), 1)

                def step(n, s):
                    pool.wait_ge(sem("hot_eq_ready"), n + (L * NT * GS + 1))
                    hot = hot_j[:, place(s)]
                    pool.tensor_tensor(hot, hot, gT[:, ds(n * GT, GT)].rearrange("p (t a) -> p t a", a=1)
                                       .to_broadcast([P, GT, NKEY]), ALU.mult).then_inc(sem("hot_j_ready"), 1)
                with pool.Fori(0, NT) as n:
                    with pool.Fori(0, GS // GTURN) as i:
                        for s in range(GTURN):
                            step(n * GS + i * GTURN + s, s)
                    step(n * GS + (GS - 1), GTURN)
                def rest_v(place, t):
                    pool.wait_ge(sem("vhi_ready"), t + (L * NG + 1))
                    hi, lo, full = (uhi, ulo, uring) if place >= 2 else (vhi, vlo, vring)
                    k = place % 2
                    pool.tensor_tensor(lo[:, k], full[:, k], hi[:, k].bitcast(f32),
                                       ALU.subtract).then_inc(sem("v_ready"), 1)

                def rest_u(slot, m):
                    pool.wait_ge(sem("uhi_ready"), 2 * m + (L * NN + slot + 1))
                    pool.tensor_tensor(ulo[:, slot], uring[:, slot], uhi[:, slot].bitcast(f32),
                                       ALU.subtract).then_inc(sem("u_ready"), 1)
                rest_v(0, 0)
                with pool.Fori(0, NN // 2 - 1) as m:
                    rest_u(0, m + 1)
                    rest_v(1, 2 * m + 1)
                    rest_u(1, m + 1)
                    rest_v(0, 2 * m + 2)
                rest_v(1, NN - 1)
                with pool.Fori(0, AG // 4) as m:
                    for k in range(4):
                        rest_v(VSLOT[k], 4 * m + (k + NN))

            peer(0)
            pool.wait_ge(sem("h_ready"), 3)
            pool.dma_start(gbias, io["gbias"].to_broadcast([P, 512])).then_inc(sem("odd_loads"), 16)
            pool.dma_start(sm_gla.rearrange("p a d -> p (a d)"), io["s_gla"]).then_inc(sem("odd_states"), 16)
            pool.wait_ge(sem("odd_group"), GROUPS + 1)
            pool.dma_start(io["o_gla"][:, 0, :], s_gla.rearrange("p h d -> p (h d)")).then_inc(sem("odd_stored"), 16)
            pool.wait_ge(sem("odd_sample"), 1)
            pool.dma_start(io["o_gla"][:, 1:9, :], sm_gla.rearrange("p (b h) d -> p b (h d)", b=NS_TOK))\
                .then_inc(sem("odd_stored"), 16)
            peer(1)
            pool.wait_ge(sem("h_ready"), 5)
            pool.dma_start(io["o_y"], hT[:, :, :]).then_inc(sem("stored"), 16)
            pool.wait_ge(sem("stored"), 16 * 5)
            pool.wait_ge(sem("dn_stored"), 16)
            pool.wait_ge(sem("even_stored"), 16)
            pool.wait_ge(sem("odd_stored"), 32)

        @block.tensor
        def _(pe):
            def mm(out, lhsT, rhs, start=True, stop=True):
                return pe.matmul(out, lhsT, rhs, start=start, stop=stop)

            def norm(k):
                pe.wait_ge(sem("squares_added"), (k + 1) * KD)
                for h in range(2):
                    last = mm(ps[:, h, 0:TH], ones, nacc[:, h * TH:(h + 1) * TH])
                last.then_inc(sem("ssq_ready"), 1)

            def gemm(name):
                base = BASE[name]
                with pe.Fori(0, BLOCKS[name] // WSLOTS) as i:
                    for u in range(WSLOTS):
                        pe.wait_ge(sem(f"w_loaded{u}"), i * 16 + 16 * (base // WSLOTS + 1))
                        pe.wait_ge(sem("gemm_free"), WSLOTS * i + (base + u + 1))
                        for h in range(2):
                            for c in range(KD):
                                last = mm(ps[:, 2 * (u % 2) + h, 0:TH], wring[:, u, c, :],
                                          hT[:, c, h * TH:(h + 1) * TH], c == 0, c == KD - 1)
                        last.then_inc(sem("gemm_done"), 1)

            def root_sums(count, nblocks, per):
                pe.wait_ge(sem("sq4_ready"), count)
                for b in range(nblocks // per):
                    for h in range(2):
                        for k in range(per):
                            last = mm(ps[:, 2 * b + h, 0:TH], ones, sq_src[0][:, b * per + k, h * TH:(h + 1) * TH],
                                      k == 0, k == per - 1)
                last.then_inc(sem("sums4_ready"), 1)

            sq_src = [sq4]

            pe.wait_ge(sem("params"), 16 * NLOADS)
            norm(0)
            pe.wait_ge(sem("h_ready"), 1)
            gemm("even_in")

            pe.wait_ge(sem("gemm_free"), BASE["even_out"] + 2)
            for n in range(5):
                rows = P if n < 4 else NS_TOK
                for c in range(KD):
                    last = mm(ps[0:rows, 0, 16 * n:16 * n + 16], hT[:, c, n * P:n * P + rows], small_w[:, c, :],
                              c == 0, c == KD - 1)
            last.then_inc(sem("gates_mm"), 1)

            pe.wait_ge(sem("gates_read"), 1)
            root_sums(1, 4, 1)
            root_sums(2, 4, 1)

            with pe.Fori(0, GROUPS) as g:
                def at(name, per=1, k=1):
                    pe.wait_ge(sem(name), g * per + k)
                at("gates_cut")
                for h in range(12):
                    mm(ps[:, h // 4, (h % 4) * P:(h % 4 + 1) * P], g_sl[:, h:h + 1].to_broadcast([P, P]), causal)
                mm(ps[:, 3, 0:12], causal, g_sl)
                for h in range(4):
                    last = mm(ps[:, 4, h * P:(h + 1) * P], b_sl[:, h:h + 1].to_broadcast([P, P]), ident)
                last.then_inc(sem("rows_ready"), 1)
                at("kb_ready")
                for h in range(4):
                    mm(ps[:, 5, h * P:(h + 1) * P], w_sl[:, 4 + h, :], kb[:, h, :])
                for h in range(4):
                    mm(ps[:, 6, h * P:(h + 1) * P], w_sl[:, 4 + h, :], w_sl[:, h, :])
                for h in range(4):
                    pe.transpose(ps[:, 7, h * P:(h + 1) * P], w_sl[:, 4 + h, :], ident)
                for h in range(4):
                    last = pe.transpose(ps[:, 0, h * P:(h + 1) * P], w_sl[:, 8 + h, :], ident)
                last.then_inc(sem("kk_ready"), 1)
                for j in range(2):
                    mm(ps[:, 1, j * P:(j + 1) * P], w_sl[:, 16 + j, :], w_sl[:, 18 + j, :])
                for b in range(4):
                    pe.transpose(ps[:, 2, b * P:(b + 1) * P], w_sl[:, 12 + b, :], ident)
                for j in range(2):
                    last = pe.transpose(ps[:, 3, j * P:(j + 1) * P], w_sl[:, 16 + j, :], ident)
                last.then_inc(sem("ssm_mm"), 1)
                at("p0_ready")
                for h in range(4):
                    last = pe.transpose(ps[:, 5, h * P:(h + 1) * P], pmat[:, h, :], ident)
                last.then_inc(sem("x0_ready"), 1)
                for l in range(1, LEVELS):
                    at("px_ready", LEVELS, l)
                    at("nl_ready", LEVELS - 1, l)
                    for h in range(4):
                        last = mm(ps[:, 6, h * P:(h + 1) * P], nl[:, l - 1, h * P:(h + 1) * P], xmat[:, h, :])
                    last.then_inc(sem("vt_mm"), 1)
                    at("vt_ready", LEVELS - 1, l)
                    for h in range(4):
                        last = mm(ps[:, 7, h * P:(h + 1) * P], vt[:, h, :], pmat[:, h, :])
                    if l < LEVELS - 1:
                        for h in range(4):
                            last = mm(ps[:, 0, h * P:(h + 1) * P], pmat[:, h, :], vt[:, h, :])
                    last.then_inc(sem("z_mm"), 1)
                at("px_ready", LEVELS, LEVELS)
                for h in range(4):
                    last = mm(ps[:, 5, h * P:(h + 1) * P], kbt[:, h, :], pmat[:, h, :])
                last.then_inc(sem("wt_mm"), 1)
                at("wt_ready")
                for h in range(4):
                    mm(ps[:, 6, h * P:(h + 1) * P], pmat[:, h, :], vb[:, h, :], True, False)
                    last = mm(ps[:, 6, h * P:(h + 1) * P], wt[:, h, :], s_dn[:, h, :], False, True)
                last.then_inc(sem("vn_mm"), 1)
                at("vn_ready")
                for h in range(4):
                    mm(ps[:, 7, h * P:(h + 1) * P], s_dn[:, h, :], qi[:, h, :], True, False)
                    mm(ps[:, 7, h * P:(h + 1) * P], vn[:, h, :], qkt[:, h, :], False, True)
                for h in range(4):
                    last = mm(ps[:, 0, h * P:(h + 1) * P], kout[:, h, :], vn[:, h, :])
                last.then_inc(sem("o_mm"), 1)
                at("att_ready")
                for h in range(8):
                    out = ps[64 * (h % 2):64 * (h % 2) + 64, 4, (h // 2) * P:(h // 2 + 1) * P]
                    mm(out, xd[:, h // 2, 64 * (h % 2):64 * (h % 2) + 64], att[:, h, :], True, False)
                    mm(out, s_ssm[:, 64 * h:64 * h + 64], ci[:, h, :], False, True)
                for j in range(2):
                    last = mm(ps[:, 5, j * 256:(j + 1) * 256], btk[:, j, :],
                              xo[:, 2 * j:2 * j + 2, :].rearrange("p a b -> p (a b)"))
                last.then_inc(sem("ssm_out_mm"), 1)

            pe.wait_ge(sem("even_group"), GROUPS + 1)
            pe.wait_ge(sem("diag_ready"), 1)
            mm(ps[:, 0, 0:192], ones[0:NS_TOK, :], sm_diag[0:NS_TOK, :, :].rearrange("p b c -> p (b c)"))\
                .then_inc(sem("bc_mm"), 1)
            pe.wait_ge(sem("dn_states"), 16)
            for h in range(4):
                for b in range(NS_TOK):
                    last = mm(ps[:, 1, h * 8 + b:h * 8 + b + 1], sm_dn[:, b * 4 + h, :],
                              conv[:, 4 + h, NP_TOK + b:NP_TOK + b + 1])
            last.then_inc(sem("r_mm"), 1)
            pe.wait_ge(sem("delta_ready"), 1)
            for b in range(NS_TOK):
                for h in range(4):
                    last = mm(ps[:, b, h * P:(h + 1) * P], sm_r[:, h, b:b + 1].to_broadcast([P, P]), ident)
                last.then_inc(sem("delta_rows"), 1)
            pe.wait_ge(sem("dn_states_new"), 1)
            for h in range(4):
                for b in range(NS_TOK):
                    last = mm(ps[:, 0, h * 8 + b:h * 8 + b + 1], sm_dn[:, b * 4 + h, :],
                              conv[:, h, NP_TOK + b:NP_TOK + b + 1])
            last.then_inc(sem("sm_o_mm"), 1)
            pe.wait_ge(sem("sm_o_read"), 1)
            for b in range(NS_TOK):
                for k in range(4):
                    last = mm(ps[:, b, k * P:(k + 1) * P], sm_xd[:, k, b:b + 1].to_broadcast([P, P]), ident)
                last.then_inc(sem("x_rows"), 1)
            pe.wait_ge(sem("ssm_states_new"), 1)
            for k in range(4):
                for b in range(NS_TOK):
                    last = mm(ps[:, 0, k * 8 + b:k * 8 + b + 1], sm_ssm[:, b, k * P:(k + 1) * P],
                              conv[:, 18 + k // 2, NP_TOK + b:NP_TOK + b + 1])
            last.then_inc(sem("sm_y_mm"), 1)

            root_sums(3, 4, 1)
            root_sums(4, 4, 2)
            pe.wait_ge(sem("mix_ready"), 1)
            gemm("even_out")

            def retrieval(L):
                pe.wait_ge(sem("gemm_free"), BASE[f"query{L}"] + BLOCKS[f"query{L}"] + 2)
                pe.wait_ge(sem("keys_loaded"), 16 * (L + 1))

                def scores(n):
                    pe.wait_ge(sem("query_ready"), n + (L * NT + 1))
                    pe.wait_ge(sem("score_free"), n + (L * NT + 1))
                    for k in range(2 * PH):
                        last = mm(ps[0:TILE, k // 4, (k % 4) * P:(k % 4 + 1) * P],
                                  query_tile[:, k, :], keys[:, k, :])
                    last.then_inc(sem("score_mm"), 1)

                def pre_ahead(slot, m):
                    pe.wait_ge(sem(f"u_loaded{slot}"), 16 * m + 16 * (L * NG // 2 + 1))
                    for j in range(JG):
                        for h in range(2):
                            pe.wait_ge(sem("half_free"), m * (4 * JG) + (2 * JG * slot + 2 * L * AG * JG + 2 * j + h + 1))
                            for c in range(KD):
                                last = mm(ps[:, 5 + h, 0:TH], uring[:, slot, j * KD + c, :],
                                          hT[:, c, h * TH:(h + 1) * TH], c == 0, c == KD - 1)
                            last.then_inc(sem("half_done"), 1)

                def tile(n):
                    for k in range(AT):
                        pre_ahead(k % 2, n * (AT // 2) + k // 2)
                    pe.wait_ge(sem("chosen"), n + (L * NT + 1))
                    for k in range(3):
                        last = pe.transpose(ps[:, 4, k * TILE:(k + 1) * TILE], res[0:TILE, k, :], ident[0:TILE, 0:TILE])
                    last.then_inc(sem("chosen_mm"), 1)
                scores(0)
                with pe.Fori(0, NT - 1) as n:
                    scores(n + 1)
                    tile(n)
                tile(NT - 1)
                pe.wait_ge(sem("half_free"), 2 * (L + 1) * AG * JG + 2)

            def step(n, s, L):
                k = n + (L * NT * GS + 1)
                pe.wait_ge(sem("hot_i_ready"), k)
                pe.wait_ge(sem("hot_j_ready"), k)
                pe.wait_ge(sem("gate_free"), k)
                for t in range(GT):
                    last = mm(ps[:, 2 * place(s) + t // 4, (t % 4) * P:(t % 4 + 1) * P],
                              hot_i[:, place(s), t, :], hot_j[:, place(s), t, :])
                last.then_inc(sem("gate_mm"), 1)

            def experts(L):
                with pe.Fori(0, NT) as n:
                    with pe.Fori(0, GS // GTURN) as i:
                        for s in range(GTURN):
                            step(n * GS + i * GTURN + s, s, L)
                    step(n * GS + (GS - 1), GTURN, L)

                def product(bank, w, w_hi, x, x_hi, first, final):
                    for h in range(2):
                        cols = slice(h * TH, (h + 1) * TH)
                        mm(ps[:, bank + h, 0:TH], w_hi, x[:, cols], first, False)
                        mm(ps[:, bank + h, 0:TH], w_hi, x_hi[:, cols], False, False)
                    for h in range(2):
                        cols = slice(h * TH, (h + 1) * TH)
                        last = mm(ps[:, bank + h, 0:TH], w, x_hi[:, cols], False, final)
                    return last

                def pre(slot, m, first=False):
                    pe.wait_ge(sem("u_ready"), 2 * m + (L * NN + slot + 1))
                    for j in range(JG):
                        pe.wait_ge(sem("pre_free"), m * (2 * JG) + (slot * JG + L * NN * JG + j + 1))
                        for c in range(KD):
                            if first and j == 0:
                                pe.wait_ge(sem("h_split"), L * KD + c + 1)
                            last = product(2 * j, ulo[:, slot, j * KD + c, :], uhi[:, slot, j * KD + c, :],
                                           hlo[:, c, :], hhi[:, c, :], c == 0, c == KD - 1)
                        last.then_inc(sem("pre_done"), 1)

                def out(slot, t, place):
                    _, a_hi, a_lo = a_of(slot)
                    """The output of the t-th group, for all tokens."""
                    pe.wait_ge(sem("v_ready"), t + (L * NG + 1))
                    pe.wait_ge(sem("act_ready"), t * JG + (L * NKEY + JG))
                    for c in range(KD):
                        pe.wait_ge(sem("y_free"), t * KD + (L * KD * NG + c + 1))
                        for j in range(JG):
                            if place < 2:
                                lo, hi = (v[:, place, j, c * P:(c + 1) * P] for v in (vlo, vhi))
                            else:
                                lo, hi = (v[:, place - 2, j * KD + c, :] for v in (ulo, uhi))
                            last = product(4 + 2 * (c % 2), lo, hi, a_lo[:, j, :], a_hi[:, j, :],
                                           j == 0, j == JG - 1)
                        last.then_inc(sem("y_done"), 1)

                pe.wait_ge(sem("gate_free"), (L + 1) * NT * GS + 3)
                pre(0, 0, True)
                with pe.Fori(0, NN // 2 - 1) as m:
                    pre(1, m)
                    out(0, 2 * m, 0)
                    pre(0, m + 1)
                    out(1, 2 * m + 1, 1)
                pre(1, NN // 2 - 1)
                out(0, NN - 2, 0)
                out(1, NN - 1, 1)
                with pe.Fori(0, AG // 4) as m:
                    for k in range(4):
                        out(ASLOT[k], 4 * m + (k + NN), VSLOT[k])

            def peer(L):
                norm(2 * L + 1)
                pe.wait_ge(sem("h_ready"), 2 * L + 2)
                gemm(f"query{L}")
                retrieval(L)
                experts(L)

            pe.sem_inc(sem("score_mm"), 1)
            pe.sem_inc(sem("gate_mm"), 3)
            peer(0)
            norm(2)
            pe.wait_ge(sem("h_ready"), 3)
            gemm("odd_in")

            pe.wait_ge(sem("gemm_free"), BASE["odd_out"] + 2)
            for h in range(2):
                for c in range(KD):
                    last = mm(ps[0:16, h, 0:TH], glr_w[:, c, :], hT[:, c, h * TH:(h + 1) * TH], c == 0, c == KD - 1)
            last.then_inc(sem("glr_mm"), 1)
            pe.wait_ge(sem("glr_ready"), 1)
            for n in range(GROUPS):
                last = mm(ps[:, 4 + n, :], glrT[0:16, n * P:(n + 1) * P], gate2[:, :])
            last.then_inc(sem("gk_mm"), 1)
            for h in range(4):
                last = mm(ps[:, 2, h * 8:(h + 1) * 8], gate2[:, h * P:(h + 1) * P], glrT[0:16, NP_TOK:T])
            last.then_inc(sem("gk_sample_mm"), 1)

            with pe.Fori(0, GROUPS) as g:
                def at(name, per=1, k=1):
                    pe.wait_ge(sem(name), g * per + k)
                at("odd_cut")
                for h in range(4):
                    last = mm(ps[:, 0, h * P:(h + 1) * P], gk_sl[:, h * P:(h + 1) * P], masks[:, GLAMASK, :])
                last.then_inc(sem("bt_mm"), 1)
                for b in range(8):
                    last = pe.transpose(ps[:, 2 + b // 4, (b % 4) * P:(b % 4 + 1) * P], o_sl[:, 8 + b, :], ident)
                last.then_inc(sem("v_mm"), 1)
                at("qk_ready")
                for h in range(4):
                    mm(ps[:, 1, h * P:(h + 1) * P], kt[:, h, :], qt[:, h, :])
                for h in range(4):
                    last = pe.transpose(ps[:, 4, h * P:(h + 1) * P], kc[:, h, :], ident)
                last.then_inc(sem("gatt_mm"), 1)
                at("gatt_ready")
                at("vtok_ready")
                for b in range(8):
                    last = mm(ps[:, 5 + b // 4, (b % 4) * P:(b % 4 + 1) * P], vtok[:, b, :], gatt[:, b // 2, :])
                last.then_inc(sem("intra_mm"), 1)
                at("intra_read")
                for c in range(P // GC):
                    at("s_ready", P // GC, c + 1)
                    for h in range(4):
                        mm(ps[:, 2 + 2 * (c % 2) + h // 2, (h % 2) * 256:(h % 2) * 256 + 256],
                           ko[c * GC:(c + 1) * GC, h, :],
                           vtok[c * GC:(c + 1) * GC, 2 * h:2 * h + 2, :].rearrange("p a b -> p (a b)"))
                    for b in range(8):
                        last = mm(ps[:, 6 + b // 4, (b % 4) * P + c * GC:(b % 4) * P + (c + 1) * GC],
                                  s_gla[:, b // 2, (b % 2) * P:(b % 2 + 1) * P],
                                  qb[:, b // 2, c * GC:(c + 1) * GC])
                    last.then_inc(sem("inter_mm"), 1)

            pe.wait_ge(sem("odd_group"), GROUPS + 1)
            for r in range(2):
                pe.wait_ge(sem("gla_rows_read"), r + 1)
                for b in range(4):
                    for h in range(4):
                        for k in range(2):
                            o = (h * 2 + k) * P
                            last = mm(ps[:, 2 * b + o // 512, o % 512:o % 512 + P],
                                      oproj[:, 8 + 2 * h + k, NP_TOK + 4 * r + b:NP_TOK + 4 * r + b + 1].to_broadcast([P, P]),
                                      ident)
                last.then_inc(sem("gla_rows"), 1)
            pe.wait_ge(sem("gla_states_new"), 1)
            for b in range(NS_TOK):
                for k in range(8):
                    last = mm(ps[:, 0, k * 8 + b:k * 8 + b + 1],
                              sm_gla[:, b * 4 + k // 2, (k % 2) * P:(k % 2 + 1) * P], sm_q[:, k // 2, b:b + 1])
            last.then_inc(sem("gla_o_mm"), 1)
            sq_src[0] = o_sq
            root_sums(5, 8, 2)
            pe.wait_ge(sem("mix_ready"), 2)
            gemm("odd_out")
            peer(1)
            norm(4)

        @block.scalar
        def _(act):
            def f(out, in_, func, **k):
                return act.activation(out, in_, func, **k)

            def norm(k):
                for c in range(KD):
                    if k % 2:
                        act.wait_ge(sem("gemm_free"), BASE[("even_out", "odd_out")[k // 2]] + c + 3)
                    elif k:
                        act.wait_ge(sem("y_free"), (k // 2 * NG - 1) * KD + c + 3)
                    if c >= 2:
                        act.wait_ge(sem("squares_added"), k * KD + c - 1)
                    f(nsq[:, c % 2, :], xT[:, c, :], ACT.Square).then_inc(sem("squares_ready"), 1)
                act.wait_ge(sem("ssq_ready"), k + 1)
                f(split(nrt), both(0), ACT.Sqrt, scale=1.0 / D, bias=eps[:, 0:1]).then_inc(sem("root_ready"), 1)

            def copy(name, dst, i, u, func):
                act.wait_ge(sem("gemm_done"), WSLOTS * i + (BASE[name] + u + 1))
                f(dst[:, ds(WSLOTS * i + u, 1), :].rearrange("p a (b t) -> p (a b) t", b=2),
                  both(2 * (u % 2)), func).then_inc(sem("gemm_free"), 1)

            def copies(name, dst, first=0, end=None, func=ACT.Copy):
                with act.Fori(first, end or BLOCKS[name] // WSLOTS) as i:
                    for u in range(WSLOTS):
                        copy(name, dst, i, u, func)

            act.wait_ge(sem("params"), 16 * NLOADS)
            act.wait_ge(sem("eps_ready"), 1)
            act.sem_inc(sem("gemm_free"), 2)
            act.sem_inc(sem("half_free"), 2)
            act.sem_inc(sem("gate_free"), 3)
            act.sem_inc(sem("pre_free"), 2)
            act.sem_inc(sem("score_free"), 1)
            norm(0)
            def silu_conv(i, u):
                act.wait_ge(sem("conv_done"), WSLOTS * i + (u + 1 - WSLOTS))
                x = conv[:, ds(WSLOTS * i + (u - WSLOTS), 1), 0:NP_TOK]
                f(x, x, ACT.Silu)
            for u in range(WSLOTS):
                copy("even_in", proj, 0, u, ACT.Copy)
            with act.Fori(1, 5) as i:
                for u in range(WSLOTS):
                    copy("even_in", proj, i, u, ACT.Copy)
                    silu_conv(i, u)
            for u in range(WSLOTS):
                copy("even_in", proj, 5, u, ACT.Silu)
                silu_conv(5, u)
            for u in range(WSLOTS):
                copy("even_in", proj, 6, u, ACT.Silu)
            act.wait_ge(sem("gates_abs"), 1)
            f(g_abs, g_abs, ACT.Exp, scale=-1.0).then_inc(sem("act_gates"), 1)
            act.wait_ge(sem("act_gates"), 1)
            f(g_abs, g_abs, ACT.Ln, bias=eps[:, 2:3]).then_inc(sem("act_gates"), 1)
            f(neg_a, a_log[:, :], ACT.Exp).then_inc(sem("act_gates"), 1)
            f(beta, g_raw[:, :, 12:16], ACT.Sigmoid).then_inc(sem("act_gates"), 1)
            act.wait_ge(sem("conv_done"), 21)
            x = conv[:, :, NP_TOK:T]
            f(x, x, ACT.Silu).then_inc(sem("conv_silu"), 1)
            act.wait_ge(sem("conv_silu"), 1)
            for r in range(2):
                if r:
                    act.wait_ge(sem("l2_done"), r)
                f(sq4, conv[:, 4 * r:4 * r + 4, :], ACT.Square).then_inc(sem("sq4_ready"), 1)
                act.wait_ge(sem("sums4_ready"), r + 1)
                f(sq4.rearrange("p a (b t) -> p (a b) t", b=2), ps[:, :, 0:TH], ACT.Sqrt,
                  scale=(float(P), 1.0)[r], bias=eps[:, 1 - r:2 - r]).then_inc(sem("roots4_ready"), 1)

            with act.Fori(0, GROUPS) as g:
                def at(name, per=1, k=1):
                    act.wait_ge(sem(name), g * per + k)
                at("even_group")
                f(w_sl, conv[:, :, ds(g * P, P)], ACT.Copy).then_inc(sem("w_cut"), 1)
                at("dec_ready")
                f(dec, dec, ACT.Exp).then_inc(sem("dec_exp"), 1)
                f(egc, gct, ACT.Exp)
                f(erow, ps[:, 0:3, :].rearrange("p b (h i) -> p (b h) i", h=4), ACT.Exp).then_inc(sem("erow_ready"), 1)
                for l in range(1, LEVELS):
                    at("vt_mm", LEVELS - 1, l)
                    f(vt, bank4(6), ACT.Copy).then_inc(sem("vt_ready"), 1)
                at("wt_mm")
                f(wt, bank4(5), ACT.Copy, scale=-1.0).then_inc(sem("wt_ready"), 1)
                at("vn_mm")
                f(vn, bank4(6), ACT.Copy).then_inc(sem("vn_ready"), 1)

            act.wait_ge(sem("even_group"), GROUPS + 1)
            f(sm_val[0:NS_TOK, 0:12], g12[0:NS_TOK, 4, :], ACT.Exp).then_inc(sem("sm_exp"), 1)

            act.wait_ge(sem("even_sample"), 1)
            f(sq4, hT[:, 0:4, :], ACT.Square).then_inc(sem("sq4_ready"), 1)
            act.wait_ge(sem("sums4_ready"), 3)
            f(sq4.rearrange("p a (b t) -> p (a b) t", b=2), ps[:, :, 0:TH], ACT.Sqrt,
              scale=1.0 / P, bias=eps[:, 0:1]).then_inc(sem("roots4_ready"), 1)
            act.wait_ge(sem("ssm_gated"), 1)
            f(sq4, hT[:, 4:8, :], ACT.Square).then_inc(sem("sq4_ready"), 1)
            act.wait_ge(sem("sums4_ready"), 4)
            f(sq4[:, 0:2, :].rearrange("p a (b t) -> p (a b) t", b=2), ps[:, 0:4, 0:TH], ACT.Sqrt,
              scale=1.0 / 256, bias=eps[:, 0:1]).then_inc(sem("roots4_ready"), 1)

            def peer(L):
                norm(2 * L + 1)
                copies(f"query{L}", query)

                def scores(n):
                    act.wait_ge(sem("score_mm"), n + (L * NT + 2))
                    act.wait_ge(sem("topk_free"), n + (L * (NT + 1) + 1))
                    f(score[0:TILE].rearrange("p (b k) i -> p b (k i)", b=4), ps[0:TILE, 0:4, :], ACT.Copy)\
                        .then_inc(sem("score_ready"), 1)
                    act.wait_ge(sem("score_ready"), n + (L * NT + 1))
                    act.sem_inc(sem("score_free"), 1)

                def best(n):
                    act.wait_ge(sem("best_diff"), n + (L * NT + 1))
                    f(diff[0:TILE], diff[0:TILE], ACT.Exp).then_inc(sem("best_exp"), 1)

                def gelu_ahead(slot, m):
                    act.wait_ge(sem(f"put{slot}"), 16 * m + 16 * (L * AG // 2 + 1))
                    for k in range(2 * JG):
                        act.wait_ge(sem("half_done"), m * (4 * JG) + (2 * JG * slot + 2 * L * AG * JG + k + 1))
                        f(ahead[:, slot, k // 2, (k % 2) * TH:(k % 2 + 1) * TH], ps[:, 5 + k % 2, 0:TH],
                          ACT.Gelu_apprx_tanh).then_inc(sem("half_free"), 1)

                def tile_ahead(n, more=True):
                    for k in range(AT):
                        gelu_ahead(k % 2, n * (AT // 2) + k // 2)
                        if k == 1 and more:
                            scores(n + 1)
                        if k == 2:
                            best(n)
                scores(0)
                with act.Fori(0, NT - 1) as n:
                    tile_ahead(n)
                tile_ahead(NT - 1, False)
                for slot in range(2):
                    act.wait_ge(sem(f"put{slot}"), 16 * (AG // 2) * (L + 1) + 16)

                def step(tile, slot, k, s):
                    act.wait_ge(sem("gate_mm"), tile * GS + k + (L * NT * GS + 4))
                    f(stage[slot][:, :, ds(k * GT, GT)].rearrange("p j (b t) -> p j b t", b=2),
                      ps[:, 2 * place(s):2 * place(s) + 2, :].rearrange("p b (t j) -> p j b t", j=NKEY), ACT.Copy)\
                        .then_inc(sem("gate_free"), 1)

                def tile(n, slot, stored):
                    act.wait_ge(sem(f"stored{slot}"), stored)
                    with act.Fori(0, GS // GTURN) as i:
                        for s in range(GTURN):
                            step(n, slot, GTURN * i + s, s)
                    step(n, slot, GS - 1, GTURN)
                with act.Fori(0, NT // 2) as i:
                    tile(2 * i, 0, 16 * i + 16 * (L * (NT // 2 + 1) + 1))
                    tile(2 * i + 1, 1, 16 * i + 16 * (L * (NT // 2) + 1))
                tile(NT - 1, 0, 16 * (NT // 2) + 16 * (L * (NT // 2 + 1) + 1))

                def cut_u(slot, m):
                    act.wait_ge(sem(f"u_loaded{slot}"), 16 * m + 16 * (L * NG // 2 + AG // 2 + 1))
                    f(uhi[:, slot], uring[:, slot], ACT.Copy).then_inc(sem("uhi_ready"), 1)

                def cut_v(place, count):
                    before = L * (NN // 2 + AG // 4 if place < 2 else AG // 4)
                    act.wait_ge(sem(f"v_loaded{place}"), 16 * count + 16 * (before + 1))
                    hi, full = (uhi, uring) if place >= 2 else (vhi, vring)
                    f(hi[:, place % 2], full[:, place % 2], ACT.Copy).then_inc(sem("vhi_ready"), 1)

                def gelu(slot, m, js=range(JG)):
                    for j in js:
                        act.wait_ge(sem("pre_done"), m * (2 * JG) + (slot * JG + L * NN * JG + j + 1))
                        f(split(aring[:, slot, j, :]), both(2 * j), ACT.Gelu_apprx_tanh).then_inc(sem("pre_free"), 1)

                def cut_a(slot, t):
                    full, hi, _ = a_of(slot)
                    for j in range(JG):
                        act.wait_ge(sem("gated"), t * JG + (L * NKEY + j + 1))
                        f(hi[:, j, :], full[:, j, :], ACT.Copy).then_inc(sem("ahi_ready"), 1)

                def group(slot, m, new_m=None):
                    act.wait_ge(sem("y_free"), m * (2 * KD) + (slot * KD + (L * NG - 1) * KD + 2))
                    gelu(slot, m, range(1))
                    if new_m is not None:
                        cut_u(1 - slot, new_m)
                    gelu(slot, m, range(1, JG))
                    cut_a(slot, 2 * m + slot)
                    cut_v(slot, m)

                act.wait_ge(sem("stored1"), 16 * (NT // 2) * (L + 1) + 16)
                for c in range(KD):
                    f(hhi[:, c, :], hT[:, c, :], ACT.Copy).then_inc(sem("hhi_ready"), 1)
                cut_u(0, 0)
                cut_u(1, 0)
                gelu(0, 0)
                act.wait_ge(sem("stored0"), 16 * (NT // 2 + 1) * (L + 1) + 16)
                cut_a(0, 0)
                cut_v(0, 0)
                with act.Fori(0, NN // 2 - 1) as m:
                    group(1, m, m + 1)
                    group(0, m + 1, m + 1)
                group(1, NN // 2 - 1)

                def v_count(place, m):
                    return m + (NN // 2 if place < 2 else 0)
                cut_v(VSLOT[0], v_count(VSLOT[0], 0))
                with act.Fori(0, AG // 4 - 1) as m:
                    for k in range(4):
                        cut_a(ASLOT[k], 4 * m + (k + NN))
                        after = VSLOT[(k + 1) % 4]
                        cut_v(after, v_count(after, m + (k + 1) // 4))
                for k in range(4):
                    cut_a(ASLOT[k], NG - 4 + k)
                    if k < 3:
                        cut_v(VSLOT[k + 1], v_count(VSLOT[k + 1], AG // 4 - 1))

            act.wait_ge(sem("even_stored"), 16)
            act.wait_ge(sem("stored"), 64)
            peer(0)
            norm(2)
            copies("odd_in", oproj, 0, 4)
            copies("odd_in", oproj, 4, 6, ACT.Silu)
            act.wait_ge(sem("glr_mm"), 1)
            f(split(glrT[0:16]), both(0, 16), ACT.Copy).then_inc(sem("glr_ready"), 1)
            act.wait_ge(sem("gk_abs"), 1)
            f(gk2, gk2, ACT.Exp, scale=-1.0).then_inc(sem("act_gk"), 1)
            f(sm_a2, sm_a2, ACT.Exp, scale=-1.0).then_inc(sem("act_gk"), 1)
            act.wait_ge(sem("act_gk"), 2)
            f(gk2, gk2, ACT.Ln, bias=eps[:, 2:3]).then_inc(sem("act_gk"), 1)
            f(sm_a2, sm_a2, ACT.Ln, bias=eps[:, 2:3]).then_inc(sem("act_gk"), 1)
            act.wait_ge(sem("sm_gk"), 1)
            f(sm_a, sm_a, ACT.Exp, scale=1.0 / 16).then_inc(sem("sm_alpha"), 1)
            with act.Fori(0, GROUPS) as g:
                def at(name, per=1, k=1):
                    act.wait_ge(sem(name), g * per + k)
                at("odd_group")
                f(gk_sl, gk[:, ds(g, 1), :].rearrange("p a b -> p (a b)"), ACT.Copy)
                f(o_sl, oproj[:, 0:16, ds(g * P, P)], ACT.Copy).then_inc(sem("odd_cut"), 1)
                at("v_mm")
                f(vtok, ps[:, 2:4, :].rearrange("p b (v i) -> p (b v) i", v=4), ACT.Copy).then_inc(sem("vtok_ready"), 1)
                at("dm_ready")
                f(e_q, dm, ACT.Exp)
                f(e_k, dm, ACT.Exp, scale=-1.0)
                f(e_b, bt, ACT.Exp)
                f(dl, dl, ACT.Exp).then_inc(sem("exps_ready"), 1)
            act.wait_ge(sem("odd_sample"), 1)
            f(o_sq, hT[:, :, :], ACT.Square).then_inc(sem("sq4_ready"), 1)
            act.wait_ge(sem("sums4_ready"), 5)
            f(o_r.rearrange("p a (b t) -> p (a b) t", b=2), ps[:, :, 0:TH], ACT.Sqrt,
              scale=1.0 / 256, bias=eps[:, 0:1]).then_inc(sem("roots4_ready"), 1)
            act.wait_ge(sem("odd_stored"), 32)
            peer(1)
            norm(4)

        @block.vector
        def _(dve):
            tt, stt, tsc, cp = dve.tensor_tensor, dve.scalar_tensor_tensor, dve.tensor_scalar, dve.tensor_copy
            SUB, ADD, MUL = ALU.subtract, ALU.add, ALU.mult

            def signal(name):
                dve.drain()
                dve.sem_inc(sem(name), 1)

            def add_squares(k, c, slot):
                dve.drain()
                dve.wait_ge(sem("squares_ready"), k * KD + c + 1)
                tt(nacc, nacc, nsq[:, slot, :], ADD).then_inc(sem("squares_added"), 1)

            def norm(k):
                dve.wait_ge(sem("root_ready"), k + 1)
                dve.reciprocal(nrt, nrt)
                dve.drain()
                for c in range(KD):
                    last = stt(hT[:, c, :], xT[:, c, :], ln[:, k, c:c + 1], nrt, MUL, MUL)
                last.then_inc(sem("h_ready"), 1)

            def residual(name, k):
                base = BASE[name]
                dve.memset(nacc, 0.0)
                with dve.Fori(0, BLOCKS[name] // WSLOTS) as i:
                    for u in range(WSLOTS):
                        dve.wait_ge(sem("gemm_done"), WSLOTS * i + (base + u + 1))
                        x = xT[:, ds(WSLOTS * i + u, 1), :].rearrange("p a (b t) -> p (a b) t", b=2)
                        tt(x, both(2 * (u % 2)), x, ADD).then_inc(sem("gemm_free"), 1)
                        add_squares(k, WSLOTS * i + u, u % 2)

            for c, v in enumerate((EPS, P * EPS, 1.0)):
                dve.memset(eps[:, c:c + 1], v)
            dve.memset(g_raw, 0.0)
            signal("eps_ready")
            dve.wait_ge(sem("params"), 16 * NLOADS)
            dve.memset(nacc, 0.0)
            for c in range(KD):
                add_squares(0, c, c % 2)
            norm(0)

            with dve.Fori(0, 20) as n:
                dve.wait_ge(sem("gemm_free"), n + 3)

                def blk(v, a, b):
                    return v[:, ds(n, 1), a:b].rearrange("p a t -> p (a t)")
                w = conv_w[:, ds(n, 1), :].rearrange("p a w -> p (a w)")
                tsc(blk(conv, 0, NP_TOK), blk(proj, 0, NP_TOK), w[:, 3:4],
                    conv_b[:, ds(n, 1)], MUL, ADD)
                for s in range(1, 4):
                    dve.drain()
                    stt(blk(conv, s, NP_TOK), blk(proj, 0, NP_TOK - s), w[:, 3 - s:4 - s],
                        blk(conv, s, NP_TOK), MUL, ADD)
                dve.drain()
                dve.sem_inc(sem("conv_done"), 1)
            dve.wait_ge(sem("buf_loaded"), 16)
            x_new = proj[:, 0:20, NP_TOK:T]

            def wcol(k):
                return conv_w[:, :, k:k + 1].to_broadcast([P, 20, NS_TOK])
            tt(acc_c, x_new, wcol(3), MUL)
            for k in range(3):
                tt(tmp_c, buf_c[:, k], wcol(k), MUL)
                dve.drain()
                tt(acc_c, acc_c, tmp_c, ADD)
                dve.drain()
                cp(new_c[:, k], x_new if k == 2 else buf_c[:, k + 1])
                cp(tail_c[:, k, :], proj[:, 0:20, NP_TOK - 3 + k:NP_TOK - 2 + k].rearrange("p n a -> p (n a)"))
            tt(conv[:, :, NP_TOK:T], acc_c, conv_b[:, :].rearrange("p (n a) -> p n a", a=1).to_broadcast([P, 20, NS_TOK]), ADD)
            signal("conv_done")

            dve.wait_ge(sem("gates_mm"), 1)
            cp(g_raw[:, 0:4, :], ps[:, 0, 0:64].rearrange("p (n c) -> p n c", n=4))
            cp(g_raw[0:NS_TOK, 4, :], ps[0:NS_TOK, 0, 64:80])
            signal("gates_read")
            bias = small_b[:, :].rearrange("p (a c) -> p a c", a=1).to_broadcast([P, 5, 16])
            tt(g_raw, g_raw, bias, ADD)
            dve.drain()
            stt(g_abs, g_raw, -1.0, g_raw, MUL, ALU.max)
            tsc(g_sp, g_raw, 0.0, None, ALU.max)
            signal("gates_abs")
            dve.wait_ge(sem("act_gates"), 4)
            tt(g_sp, g_sp, g_abs, ADD)
            tsc(neg_a, neg_a, -1.0, None, MUL)
            dve.drain()
            tt(g12, g_sp[:, :, 0:12], neg_a.rearrange("p (a c) -> p a c", a=1).to_broadcast([P, 5, 12]), MUL)
            for r in range(2):
                dve.wait_ge(sem("roots4_ready"), r + 1)
                dve.reciprocal(sq4, sq4)
                dve.drain()
                tt(conv[:, 4 * r:4 * r + 4, :], conv[:, 4 * r:4 * r + 4, :], sq4, MUL)
                signal("l2_done")
            dve.memset(s_dn, 0.0)
            dve.memset(s_ssm, 0.0)
            signal("even_group")

            def bc(v, n):
                return v.rearrange("p (k a) -> p k a", a=1).to_broadcast([P, v.shape[1], n])

            def at_end(v):
                return v[:, :, P - 1:P]

            with dve.Fori(0, GROUPS) as g:
                def at(name, per=1, k=1):
                    dve.wait_ge(sem(name), g * per + k)

                def cut(v, a, b):
                    return v[:, ds(g, 1), a:b].rearrange("p a c -> p (a c)")
                cp(g_sl, cut(g12, 0, 12))
                cp(b_sl, cut(beta, 0, 4))
                cp(d_sl, cut(g_sp, 4, 12)).then_inc(sem("gates_cut"), 1)
                at("rows_ready")
                cp(gct, ps[:, 3, 0:12])
                dve.drain()
                tt(dec, ps[:, 0:3, :].rearrange("p b (h i) -> p (b h) i", h=4), bc(gct, P), SUB)
                dve.drain()
                tsc(dec, dec, 0.0, None, ALU.min).then_inc(sem("dec_ready"), 1)
                at("erow_ready")
                tt(dec, dec, masks[:, CAUSAL:CAUSAL + 1, :].to_broadcast([P, 12, P]), MUL)
                tt(b_e, b_sl, egc[:, 0:4], MUL)
                at("w_cut")
                tt(kb, w_sl[:, 4:8, :], bank4(4), MUL).then_inc(sem("kb_ready"), 1)
                tt(qi, w_sl[:, 0:4, :], erow[:, 0:4, :], MUL)
                at("kk_ready")
                tt(nmat, bank4(5), dec[:, 0:4, :], MUL)
                dve.drain()
                tt(nmat, nmat, mask4(STRICT), MUL).then_inc(sem("n_ready"), 1)
                tt(qkt, bank4(6), dec[:, 0:4, :], MUL)
                dve.drain()
                tt(pmat, nmat, mask4(LEVEL0), MUL)
                tt(kbt, bank4(7), bc(b_e, P), MUL)
                tt(kout, bank4(7), at_end(dec[:, 0:4, :]).to_broadcast([P, 4, P]), MUL)
                tt(vb, bank4(0), bc(b_sl, P), MUL)
                dve.drain()
                tt(pmat, mask4(IDENT), pmat, SUB).then_inc(sem("p0_ready"), 1)
                at("x0_ready")
                cp(xmat, bank4(5)).then_inc(sem("px_ready"), 1)
                at("ssm_mm")

                def ssm_work(l):
                    if l == 1:
                        cp(btk, ps[:, 3, 0:256].rearrange("p (a b) -> p a b", a=2))
                    if l == 2:
                        tt(xd8, ps[:, 2, :].rearrange("p (h c) -> p h c", h=8), bc(d_sl, 64), MUL)
                    if l == 3:
                        dve.drain()
                        tt(xo8, xd8, at_end(dec[:, 4:12, :]).to_broadcast([P, 8, 64]), MUL)
                    if l == 4:
                        for j in range(2):
                            tt(att[:, 4 * j:4 * j + 4, :], dec[:, 4 + 4 * j:8 + 4 * j, :],
                               ps[:, 1, j * P:(j + 1) * P].rearrange("p (a i) -> p a i", a=1).to_broadcast([P, 4, P]), MUL)
                    if l == 5:
                        for j in range(2):
                            last = tt(ci[:, 4 * j:4 * j + 4, :], erow[:, 4 + 4 * j:8 + 4 * j, :],
                                      w_sl[:, 18 + j:19 + j, :].to_broadcast([P, 4, P]), MUL)
                        last.then_inc(sem("att_ready"), 1)
                for l in range(1, LEVELS):
                    ssm_work(l)
                    at("z_mm", LEVELS - 1, l)
                    last = tt(pmat, pmat, bank4(7), SUB)
                    if l < LEVELS - 1:
                        last = tt(xmat, xmat, bank4(0), SUB)
                    last.then_inc(sem("px_ready"), 1)
                at("o_mm")
                cp(hT[:, 0:4, ds(g * P, P)], bank4(7))
                for h in range(4):
                    stt(s_dn[:, h, :], s_dn[:, h, :], erow[:, h, P - 1:P], ps[:, 0, h * P:(h + 1) * P], MUL, ADD)
                at("ssm_out_mm")
                cp(hT[:, 4:8, ds(g * P, P)], bank4(4))
                s8 = s_ssm.rearrange("p (h c) -> p h c", h=8)
                tt(s8, s8, at_end(erow[:, 4:12, :]).to_broadcast([P, 8, 64]), MUL)
                dve.drain()
                tt(s_ssm, s_ssm, ps[:, 5, :], ADD)
                dve.drain()
                dve.sem_inc(sem("even_group"), 1)

            dve.wait_ge(sem("sm_exp"), 1)
            cp(sm_val[0:NS_TOK, 12:16], beta[0:NS_TOK, 4, :])
            cp(sm_val[0:NS_TOK, 16:24], g_sp[0:NS_TOK, 4, 4:12])
            dve.drain()
            tt(sm_diag[0:NS_TOK], sm_val[0:NS_TOK].rearrange("p (a c) -> p a c", a=1).to_broadcast([NS_TOK, NS_TOK, 24]),
               ident[0:NS_TOK, 0:NS_TOK].rearrange("p (b a) -> p b a", a=1).to_broadcast([NS_TOK, NS_TOK, 24]), MUL)\
                .then_inc(sem("diag_ready"), 1)
            dve.wait_ge(sem("bc_mm"), 1)
            cp(sm_bc, ps[:, 0, 0:192].rearrange("p (b c) -> p b c", b=NS_TOK))
            dve.drain()
            dve.wait_ge(sem("r_mm"), 1)
            tt(sm_r, ps[:, 1, 0:32].rearrange("p (h b) -> p h b", h=4), sm_bc[:, :, 0:4].rearrange("p b h -> p h b"), MUL)
            dve.drain()
            tt(sm_r, conv[:, 8:12, NP_TOK:T], sm_r, SUB)
            dve.drain()
            tt(sm_r, sm_r, sm_bc[:, :, 12:16].rearrange("p b h -> p h b"), MUL).then_inc(sem("delta_ready"), 1)
            for h in range(4):
                v = sm_dn.rearrange("p (b h) d -> p h b d", h=4)[:, h]
                tt(v, v, sm_bc[:, :, h:h + 1].to_broadcast([P, NS_TOK, P]), MUL)
            dve.drain()
            for b in range(NS_TOK):
                dve.wait_ge(sem("delta_rows"), b + 1)
                for h in range(4):
                    s = sm_dn[:, b * 4 + h, :]
                    stt(s, ps[:, b, h * P:(h + 1) * P], conv[:, 4 + h, NP_TOK + b:NP_TOK + b + 1], s, MUL, ADD)
            signal("dn_states_new")
            dve.wait_ge(sem("even_states"), 16)
            for half in range(2):
                r = slice(64 * half, 64 * half + 64)
                tt(sm_xd[r], conv[r, 12:16, NP_TOK:T], sm_bc[r, :, 16 + half:24:2].rearrange("p b k -> p k b"), MUL)
            for h in range(8):
                v = sm_ssm[:, :, 64 * h:64 * h + 64]
                tt(v, v, sm_bc[:, :, 4 + h:5 + h].to_broadcast([P, NS_TOK, 64]), MUL)
            dve.wait_ge(sem("sm_o_mm"), 1)
            cp(hT[:, 0:4, NP_TOK:T], ps[:, 0, 0:32].rearrange("p (h b) -> p h b", h=4))
            signal("sm_o_read")
            for b in range(NS_TOK):
                dve.wait_ge(sem("x_rows"), b + 1)
                for j in range(2):
                    s = sm_ssm[:, b, 256 * j:256 * j + 256]
                    stt(s, ps[:, b, 256 * j:256 * j + 256], conv[:, 16 + j, NP_TOK + b:NP_TOK + b + 1], s, MUL, ADD)
            signal("ssm_states_new")
            dve.wait_ge(sem("sm_y_mm"), 1)
            cp(hT[:, 4:8, NP_TOK:T], ps[:, 0, 0:32].rearrange("p (h b) -> p h b", h=4))
            signal("even_sample")

            for k in range(4):
                stt(hT[:, 4 + k, :], conv[:, 12 + k, :], head_w[:, 5 + k:6 + k], hT[:, 4 + k, :], MUL, ADD)
            dve.drain()
            tt(hT[:, 4:8, :], hT[:, 4:8, :], proj[:, 24:28, :], MUL)
            dve.wait_ge(sem("roots4_ready"), 3)
            dve.reciprocal(sq4, sq4)
            dve.drain()
            tt(hT[:, 0:4, :], hT[:, 0:4, :], sq4, MUL)
            signal("ssm_gated")
            stt(hT[:, 0:4, :], hT[:, 0:4, :], head_w[:, 0:1], proj[:, 20:24, :], MUL, MUL)
            dve.wait_ge(sem("roots4_ready"), 4)
            dve.reciprocal(sq4[:, 0:2, :], sq4[:, 0:2, :])
            dve.drain()
            for k in range(4):
                stt(hT[:, 4 + k, :], hT[:, 4 + k, :], head_w[:, 1 + k:2 + k], sq4[:, k // 2, :], MUL, MUL)
            signal("mix_ready")
            residual("even_out", 1)

            def top16(L, n, src, vals, idx, count):
                for k in range(count):
                    dve.max(vals(k)[:, 0:8], src(k))
                dve.drain()
                for k in range(count):
                    dve.max_index(idx(k)[:, 0:8], vals(k)[:, 0:8], src(k))
                dve.drain()
                for k in range(count):
                    dve.match_replace(out=src(k), in_to_replace=vals(k)[:, 0:8], in_values=src(k), imm_value=-3e38)
                dve.drain()
                for k in range(count):
                    dve.max(vals(k)[:, 8:16], src(k))
                dve.drain()
                for k in range(count):
                    dve.max_index(idx(k)[:, 8:16], vals(k)[:, 8:16], src(k))
                dve.drain()

            def peer(L):
                norm(2 * L + 1)
                R = slice(0, TILE)
                dve.wait_ge(sem("iota_ready"), 1)
                dve.wait_ge(sem("keys_loaded"), 16 * (L + 1))
                signal("topk_free")
                with dve.Fori(0, NT) as n:
                    dve.wait_ge(sem("score_ready"), n + (L * NT + 1))
                    cp(iota16, iota[:, 0:TOPK])
                    top16(L, n, lambda k: score[R, k, :], lambda k: topv[R, k, :], lambda k: topi[R, k, :], 2 * PH)
                    dve.sem_inc(sem("topk_free"), 1)
                    cp(topf[R], topi[R])
                    for h in range(PH):
                        tt(cand[R, h, :].rearrange("p (a b) -> p a b", a=TOPK),
                           topv[R, 2 * h, :].rearrange("p (a b) -> p a b", b=1).to_broadcast([TILE, TOPK, TOPK]),
                           topv[R, 2 * h + 1, :].rearrange("p (a b) -> p a b", a=1).to_broadcast([TILE, TOPK, TOPK]), ADD)
                    dve.drain()
                    top16(L, n, lambda k: cand[R, k, :], lambda k: bests[R, k, :], lambda k: bestj[R, k, :], PH)
                    tt(diff[R], bests[R], bests[R, :, 0:1].to_broadcast([TILE, PH, TOPK]), SUB)\
                        .then_inc(sem("best_diff"), 1)
                    for side, (op, by) in enumerate(((ALU.logical_shift_right, 4), (ALU.bitwise_and, 15))):
                        tsc(posu[R], bestj[R], by, None, op)
                        dve.drain()
                        cp(posf[R], posu[R])
                        dve.drain()
                        tt(eq[R], posf[R].rearrange("p h (k a) -> p (h k) a", a=1).to_broadcast([TILE, PH * TOPK, TOPK]),
                           iota16[R].rearrange("p (k a) -> p k a", k=1).to_broadcast([TILE, PH * TOPK, TOPK]), ALU.is_equal)
                        dve.drain()
                        for h in range(PH):
                            e = eq[R, h * TOPK:(h + 1) * TOPK, :]
                            tt(e, e, topf[R, 2 * h + side:2 * h + side + 1, :].to_broadcast([TILE, TOPK, TOPK]), MUL)
                        dve.drain()
                        dve.reduce_sum(res[R, side, :], eq[R], axis=X)
                        dve.drain()
                    dve.wait_ge(sem("best_exp"), n + (L * NT + 1))
                    dve.reduce_sum(ssum[R], diff[R], axis=X)
                    dve.drain()
                    dve.reciprocal(ssum[R], ssum[R])
                    dve.drain()
                    tt(res[R, 2, :].rearrange("p (h k) -> p h k", h=PH), diff[R],
                       ssum[R].rearrange("p (h a) -> p h a", a=1).to_broadcast([TILE, PH, TOPK]), MUL)
                    dve.drain()
                    dve.sem_inc(sem("chosen"), 1)
                    dve.wait_ge(sem("chosen_mm"), n + (L * NT + 1))
                    cols = ds(n * TILE, TILE)
                    cp(idx1T[:, cols], ps[:, 4, 0:TILE])
                    cp(idx2T[:, cols], ps[:, 4, TILE:2 * TILE])
                    cp(gT[:, cols], ps[:, 4, 2 * TILE:3 * TILE])
                    dve.drain()

                def step(n, s):
                    dve.wait_ge(sem("gate_mm"), n + (L * NT * GS + 1))
                    at = ds(n * GT, GT)

                    def hot(idx):
                        return (iota[:, :].rearrange("p (a i) -> p a i", a=1).to_broadcast([P, GT, NKEY]),
                                idx[:, at].rearrange("p (t a) -> p t a", a=1).to_broadcast([P, GT, NKEY]), ALU.is_equal)
                    tt(hot_j[:, place(s)], *hot(idx2T)).then_inc(sem("hot_eq_ready"), 1)
                    tt(hot_i[:, place(s)], *hot(idx1T)).then_inc(sem("hot_i_ready"), 1)
                with dve.Fori(0, NT) as n:
                    with dve.Fori(0, GS // GTURN) as i:
                        for s in range(GTURN):
                            step(n * GS + i * GTURN + s, s)
                    step(n * GS + (GS - 1), GTURN)

                def gate(j, slot, gslot, m, made=False):
                    if j == 0:
                        dve.wait_ge(sem(f"g_loaded{gslot}"), 16 * m + 16 * (L * NG // 2 + 1))
                    if not made:
                        dve.wait_ge(sem("pre_free"), m * (2 * JG) + (gslot * JG + L * NN * JG + j + 3))
                    a = a_of(slot)[0][:, j, :].rearrange("p (n t) -> p n t", n=NT)
                    tt(a, a, gring[:, gslot, :, j, :], MUL).then_inc(sem("gated"), 1)

                def gate_ahead(j, k, m):
                    if j == 0:
                        dve.wait_ge(sem(f"a_loaded{ASLOT[k]}"), 16 * m + 16 * (L * AG // 4 + 1))
                    gate(j, ASLOT[k], k % 2, 2 * m + (k // 2 + NN // 2), True)

                def rest_a(slot, t, j):
                    dve.wait_ge(sem("ahi_ready"), t * JG + (L * NKEY + j + 1))
                    full, hi, lo = a_of(slot)
                    tt(lo[:, j, :], full[:, j, :], hi[:, j, :].bitcast(f32), SUB).then_inc(sem("act_ready"), 1)

                def turn(t, nxt=None, gating=None, *what):
                    for c in range(KD):
                        dve.wait_ge(sem("y_done"), t * KD + (L * KD * NG + c + 1))
                        tt(split(xT[:, c, :]), both(4 + 2 * (c % 2)), split(xT[:, c, :]), ADD).then_inc(sem("y_free"), 1)
                        if nxt is not None and c < JG:
                            gating(c, *what)
                        if nxt is not None and JG < c <= 2 * JG:
                            rest_a(nxt, t + 1, c - JG - 1)
                        if nxt is None and c:
                            add_squares(2 * L + 2, c - 1, (c - 1) % 2)
                    dve.drain()

                for c in range(KD):
                    dve.wait_ge(sem("hhi_ready"), L * KD + c + 1)
                    tt(hlo[:, c, :], hT[:, c, :], hhi[:, c, :].bitcast(f32), SUB).then_inc(sem("h_split"), 1)
                for slot in range(2):
                    dve.wait_ge(sem("uhi_ready"), L * NN + slot + 1)
                    tt(ulo[:, slot], uring[:, slot], uhi[:, slot].bitcast(f32), SUB).then_inc(sem("u_ready"), 1)
                for j in range(JG):
                    gate(j, 0, 0, 0)
                for j in range(JG):
                    rest_a(0, 0, j)
                with dve.Fori(0, NN // 2 - 1) as m:
                    turn(2 * m, 1, gate, 1, 1, m)
                    turn(2 * m + 1, 0, gate, 0, 0, m + 1)
                turn(NN - 2, 1, gate, 1, 1, NN // 2 - 1)
                turn(NN - 1, ASLOT[0], gate_ahead, 0, 0)
                with dve.Fori(0, AG // 4 - 1) as m:
                    for k in range(4):
                        turn(4 * m + (k + NN), ASLOT[(k + 1) % 4], gate_ahead, (k + 1) % 4, m + (k + 1) // 4)
                for k in range(3):
                    turn(NG - 4 + k, ASLOT[k + 1], gate_ahead, k + 1, AG // 4 - 1)
                dve.memset(nacc, 0.0)
                turn(NG - 1)
                add_squares(2 * L + 2, KD - 1, (KD - 1) % 2)

            dve.sem_inc(sem("y_free"), 2)
            peer(0)
            norm(2)

            dve.wait_ge(sem("odd_loads"), 16)
            dve.wait_ge(sem("gk_sample_mm"), 1)
            tt(gk, ps[:, 4:8, :], gbias.rearrange("p (a c) -> p a c", a=1).to_broadcast([P, GROUPS, 512]), ADD)
            tt(sm_a, ps[:, 2, 0:32].rearrange("p (h b) -> p h b", h=4),
               head_w[:, 11:15].rearrange("p (h b) -> p h b", b=1).to_broadcast([P, 4, NS_TOK]), ADD)
            dve.drain()
            stt(gk2, gk, -1.0, gk, MUL, ALU.max)
            stt(sm_a2, sm_a, -1.0, sm_a, MUL, ALU.max)
            tsc(gk, gk, 0.0, None, ALU.min)
            tsc(sm_a, sm_a, 0.0, None, ALU.min)
            signal("gk_abs")
            dve.wait_ge(sem("act_gk"), 4)
            tt(sm_a, sm_a, sm_a2, SUB).then_inc(sem("sm_gk"), 1)
            tt(gk, gk, gk2, SUB)
            dve.drain()
            tsc(gk, gk, 1.0 / 16, None, MUL)
            dve.memset(s_gla, 0.0)
            signal("odd_group")
            dve.sem_inc(sem("s_ready"), 1)
            scale = float(P) ** -0.5

            def chunks(v):
                return v.rearrange("p h (c i) -> p (h c) i", i=GC)
            with dve.Fori(0, GROUPS) as g:
                def at(name, per=1, k=1):
                    dve.wait_ge(sem(name), g * per + k)
                at("bt_mm")
                cp(bt, bank4(0))
                dve.drain()
                b16 = chunks(bt)
                tt(chunks(dm), b16, b16[:, :, GC // 2 - 1:GC // 2].to_broadcast([P, 16, GC]), SUB)
                tt(chunks(dl), b16[:, :, GC - 1:GC].to_broadcast([P, 16, GC]), b16, SUB).then_inc(sem("dm_ready"), 1)
                at("odd_cut")
                at("exps_ready")
                stt(qt, o_sl[:, 0:4, :], scale, e_q, MUL, MUL)
                tt(kt, o_sl[:, 4:8, :], e_k, MUL)
                tt(kc, o_sl[:, 4:8, :], dl, MUL).then_inc(sem("qk_ready"), 1)
                stt(qb, o_sl[:, 0:4, :], scale, e_b, MUL, MUL)
                at("gatt_mm")
                tsc(gatt, bank4(1), BIG, -BIG, ALU.min, ALU.max)
                cp(ko, bank4(4))
                dve.drain()
                tt(gatt, gatt, mask4(GLAMASK), MUL).then_inc(sem("gatt_ready"), 1)
                at("intra_mm")
                o = hT[:, :, ds(g * P, P)]
                cp(o, ps[:, 5:7, :].rearrange("p b (v i) -> p (b v) i", v=4)).then_inc(sem("intra_read"), 1)
                for c in range(P // GC):
                    at("inter_mm", P // GC, c + 1)
                    for h in range(4):
                        last = stt(s_gla[:, h, :], s_gla[:, h, :], e_b[:, h, (c + 1) * GC - 1:(c + 1) * GC],
                                   ps[:, 2 + 2 * (c % 2) + h // 2, (h % 2) * 256:(h % 2) * 256 + 256], MUL, ADD)
                    last.then_inc(sem("s_ready"), 1)
                tt(o, o, ps[:, 6:8, :].rearrange("p b (v i) -> p (b v) i", v=4), ADD)
                dve.drain()
                dve.sem_inc(sem("odd_group"), 1)

            tsc(sm_q, oproj[:, 0:4, NP_TOK:T], scale, None, MUL)
            signal("gla_rows_read")
            dve.wait_ge(sem("sm_alpha"), 1)
            dve.wait_ge(sem("odd_states"), 16)
            for h in range(4):
                v = sm_gla.rearrange("p (b h) d -> p h b d", h=4)[:, h]
                tt(v, v, sm_a[:, h, :].rearrange("p (b a) -> p b a", a=1).to_broadcast([P, NS_TOK, 256]), MUL)
            dve.drain()
            for r in range(2):
                dve.wait_ge(sem("gla_rows"), r + 1)
                for b in range(4):
                    for h in range(4):
                        s = sm_gla[:, (4 * r + b) * 4 + h, :]
                        stt(s, ps[:, 2 * b + h // 2, (h % 2) * 256:(h % 2) * 256 + 256],
                            oproj[:, 4 + h, NP_TOK + 4 * r + b:NP_TOK + 4 * r + b + 1], s, MUL, ADD)
                signal("gla_rows_read")
            dve.sem_inc(sem("gla_states_new"), 1)
            dve.wait_ge(sem("gla_o_mm"), 1)
            cp(hT[:, :, NP_TOK:T], ps[:, 0, 0:64].rearrange("p (k b) -> p k b", k=8))
            signal("odd_sample")
            dve.wait_ge(sem("roots4_ready"), 5)
            dve.reciprocal(o_r, o_r)
            dve.drain()
            for k in range(8):
                stt(hT[:, k, :], hT[:, k, :], head_w[:, 9 + k % 2:10 + k % 2], o_r[:, k // 2, :], MUL, MUL)
            dve.drain()
            tt(hT[:, :, :], hT[:, :, :], oproj[:, 16:24, :], MUL)
            signal("mix_ready")
            residual("odd_out", 3)
            peer(1)
            norm(4)


INPUTS = dict(
    masks=(P, NMASK, P), xT=(P, KD, T), ln=(P, 5, KD), conv_w=(P, 20, 4), conv_b=(P, 20), small_w=(P, KD, 16),
    glr_w=(P, KD, 16), head_w=(P, 16), gate2=(16, 512), small_b=(1, 16), a_log=(1, 12), gbias=(1, 512),
    conv_buf=(P, 3, 20, NS_TOK), s_dn=(P, 32 * P), s_ssm=(P, NS_TOK * 512), s_gla=(P, 32 * 256),
    keys0=(P, 16, NKEY), keys1=(P, 16, NKEY), weights=(NBLOCKS, P, D),
    u0=(NG, P, JG * D), u1=(NG, P, JG * D), v0=(NG, P, JG * D), v1=(NG, P, JG * D))
OUTPUTS = dict(
    o_y=(P, KD, T), o_conv_p=(P, 3, 20), o_conv_s=(P, 3, 20, NS_TOK), o_dn=(P, 9, 512), o_ssm=(P, 9, 512),
    o_gla=(P, 9, 1024))


def constant_masks():
    import numpy as np
    r, c = np.arange(P)[:, None], np.arange(P)[None, :]
    m = [r == c, r == r + 0 * c, c >= r, c > r]
    for l in range(LEVELS):
        s = 1 << l
        m.append((r // (2 * s) == c // (2 * s)) & (r // s < c // s))
    m.append((r // GC == c // GC) & (c >= r))
    return np.ascontiguousarray(np.stack(m, axis=1).astype(np.float32))


def kernel(**inp):
    import numpy as np
    import concourse.bacc as bacc
    from concourse.bass_utils import run_bass_kernel_spmd

    A = {k: np.asarray(v) for k, v in inp.items()}
    f = np.ascontiguousarray

    def rows(w):
        return w.reshape(KD, P, -1).transpose(1, 0, 2)

    def blocks(w):
        return w.reshape(KD, P, -1, P).transpose(2, 1, 0, 3).reshape(-1, P, D)

    def cols(v):
        return v.reshape(-1, P).T

    we, wo = A["w_in_even"][0], A["w_in_odd"][0]
    qkv, a_in, b_in, gate, z, xbc, dt_in = np.split(we, [1536, 1540, 1544, 2056, 2568, 3592], axis=1)
    qk, v_in, glr, og = np.split(wo, [1024, 2048, 2064], axis=1)
    x = np.concatenate([A["x_prompt"][0], A["x_sample"][:, 0]], axis=0)
    zero = np.zeros
    keys = [np.stack([A["peer_keys1"][l], A["peer_keys2"][l]], axis=1).reshape(16, NKEY, P).transpose(2, 0, 1)
            for l in range(2)]
    conv_buf = np.concatenate([A["state_dn_conv"][0], A["state_ssm_conv"][0]], axis=2)
    ins = dict(
        masks=constant_masks(),
        xT=x.T.reshape(KD, P, T).transpose(1, 0, 2),
        ln=np.stack([A["ln_mix"][0], A["ln_ffn"][0], A["ln_mix"][1], A["ln_ffn"][1], A["ln_final"]])
        .reshape(5, KD, P).transpose(2, 0, 1),
        conv_w=np.concatenate([A["dn_conv_w"][0], A["ssm_conv_w"][0]], axis=1).reshape(4, 20, P).transpose(2, 1, 0),
        conv_b=np.concatenate([zero((12, P), np.float32), A["ssm_conv_b"][0].reshape(8, P)], axis=0).T,
        small_w=rows(np.concatenate([a_in, dt_in, b_in], axis=1)),
        glr_w=rows(glr),
        head_w=np.concatenate([cols(A["dn_norm_w"][0]), cols(A["ssm_norm_w"][0]),
                               cols(np.repeat(A["ssm_d"][0], 64)), cols(A["gla_norm_w"][0]),
                               cols(A["gla_b_gate"][0]), zero((P, 1), np.float32)], axis=1),
        gate2=A["gla_w_gate2"][0],
        small_b=np.concatenate([A["dn_dt_bias"][0], A["ssm_dt_bias"][0], zero(4, np.float32)])[None],
        a_log=np.concatenate([A["dn_a_log"][0], A["ssm_a_log"][0]])[None],
        gbias=A["gla_b_gate"][0][None],
        conv_buf=conv_buf.reshape(NS_TOK, 3, 20, P).transpose(3, 1, 2, 0),
        s_dn=A["state_dn"][0].transpose(2, 0, 1, 3).reshape(P, -1),
        s_ssm=A["state_ssm"][0].transpose(3, 0, 1, 2).reshape(P, -1),
        s_gla=A["state_gla"][0].transpose(2, 0, 1, 3).reshape(P, -1),
        keys0=keys[0], keys1=keys[1],
        weights=np.concatenate([blocks(np.concatenate([qkv, xbc, gate, z], axis=1)), blocks(A["w_out_even"][0]),
                                blocks(A["peer_w_q"][0]), blocks(np.concatenate([qk, v_in, og], axis=1)),
                                blocks(A["w_out_odd"][0]), blocks(A["peer_w_q"][1])], axis=0),
    )
    for l in range(2):
        u = A["peer_u"][l].reshape(NKEY, NG, JG, KD, P)
        ins[f"u{l}"] = u.transpose(1, 4, 2, 3, 0).reshape(NG, P, JG * D)
        v = A["peer_v"][l].reshape(NKEY, NG, JG, D)
        ins[f"v{l}"] = v.transpose(1, 0, 2, 3).reshape(NG, P, JG * D)
    ins = {k: f(v) for k, v in ins.items()}

    nc = bacc.Bacc("TRN2", target_bir_lowering=False, num_devices=1)
    f32 = mybir.dt.float32
    io = {k: nc.dram_tensor("in_" + k, s, f32, kind="ExternalInput").ap() for k, s in INPUTS.items()}
    for k, s in INPUTS.items():
        assert ins[k].shape == s and ins[k].dtype == np.float32, (k, ins[k].shape, s)
    io.update({k: nc.dram_tensor("out_" + k, s, f32, kind="ExternalOutput").ap() for k, s in OUTPUTS.items()})
    for k in ("keys", "u", "v"):
        io[k] = [io[f"{k}0"], io[f"{k}1"]]
    io["gates"] = nc.dram_tensor("gates", (P, NT, NKEY, TILE), f32, kind="Internal").ap()
    io["ahead"] = nc.dram_tensor("ahead", (AG, P, JG * T), f32, kind="Internal").ap()
    build_program(nc, io)
    r = run_bass_kernel_spmd(nc, [{"in_" + k: v for k, v in ins.items()}], core_ids=[0]).results[0]

    y = r["out_o_y"].transpose(2, 1, 0).reshape(T, D)
    tail = r["out_o_conv_p"].transpose(1, 2, 0).reshape(1, 1, 3, 2560)
    new = r["out_o_conv_s"].transpose(3, 1, 2, 0).reshape(1, NS_TOK, 3, 2560)
    dn = r["out_o_dn"].reshape(P, 9, 4, P).transpose(1, 2, 0, 3)[None]
    ssm = r["out_o_ssm"].reshape(P, 9, 8, 64).transpose(1, 2, 3, 0)[None]
    gla = r["out_o_gla"].reshape(P, 9, 4, 256).transpose(1, 2, 0, 3)[None]
    return (f(y[None, :NP_TOK]), f(y[NP_TOK:, None]), f(tail[..., :1536]), f(dn[:, :1]), f(tail[..., 1536:]),
            f(ssm[:, :1]), f(gla[:, :1]), f(new[..., :1536]), f(dn[:, 1:]), f(new[..., 1536:]), f(ssm[:, 1:]),
            f(gla[:, 1:]))
```
